# Optimizing a Trainium2 kernel written in Bass

```python
import jax, jax.numpy as jnp
from jax import lax
import numpy as np

D_MODEL = 1024
BATCH = 1
SEQ = 512
DEPTH = 2

N_META = 16
N_A_LAYERS = DEPTH // 2
N_B_LAYERS = DEPTH - N_A_LAYERS
CONV_WIDTH = 31
HEAD_DIM = 64
N_HEADS = D_MODEL // HEAD_DIM
N_KV_HEADS = 4
Q_PER_KV = N_HEADS // N_KV_HEADS
WINDOW = 128
BLOCK = 128
D_FF = -(-8 * D_MODEL // (3 * 256)) * 256
NORM_EPS = 1e-6
NEG_INF = -1e30

kernel_name = "yoco_conformer_swa_sink_hybrid"

def rms_norm(x, g):
    xf = x.astype(jnp.float32)
    y = xf * lax.rsqrt(jnp.mean(xf * xf, axis=-1, keepdims=True) + NORM_EPS)
    return (y * g.astype(jnp.float32)).astype(x.dtype)

def layer_norm(x, g, b):
    xf = x.astype(jnp.float32)
    mu = jnp.mean(xf, axis=-1, keepdims=True)
    var = jnp.mean(jnp.square(xf - mu), axis=-1, keepdims=True)
    y = (xf - mu) * lax.rsqrt(var + NORM_EPS)
    return (y * g.astype(jnp.float32) + b.astype(jnp.float32)).astype(x.dtype)

def conformer_conv(u, w_in, b_in, dw, ln_g, ln_b, w_out, b_out):
    d = u.shape[-1]
    a = u @ w_in + b_in
    a = a[..., :d] * jax.nn.sigmoid(a[..., d:])
    a = jnp.pad(a, ((0, 0), (CONV_WIDTH - 1, 0), (0, 0)))
    c = lax.conv_general_dilated(a, dw[:, None, :], window_strides=(1,), padding='VALID',
                                 dimension_numbers=('NWC', 'WIO', 'NWC'),
                                 feature_group_count=d)
    c = jax.nn.silu(layer_norm(c, ln_g, ln_b))
    return c @ w_out + b_out

def swiglu(u, w_gate, w_up, w_down):
    return (jax.nn.silu(u @ w_gate) * (u @ w_up)) @ w_down

def shared_kv(h, g, w_kv, k_norm):
    b, l, _ = h.shape
    kv = rms_norm(h, g) @ w_kv
    k, v = jnp.split(kv, 2, axis=-1)
    k = rms_norm(k.reshape(b, l, N_KV_HEADS, HEAD_DIM), k_norm)
    v = v.reshape(b, l, N_KV_HEADS, HEAD_DIM)
    return k, v

def band_keys(t, nb):
    b = t.shape[0]
    tp = jnp.pad(t, ((0, 0), (BLOCK, 0), (0, 0), (0, 0)))
    tb = tp.reshape(b, nb + 1, BLOCK, N_KV_HEADS, HEAD_DIM)
    band = jnp.concatenate([tb[:, :-1], tb[:, 1:]], axis=2)
    meta = jnp.broadcast_to(t[:, None, :N_META], (b, nb, N_META, N_KV_HEADS, HEAD_DIM))
    return jnp.concatenate([meta, band], axis=2)

def window_mask(nb):
    qpos = jnp.arange(nb)[:, None] * BLOCK + jnp.arange(BLOCK)[None, :]
    band_pos = jnp.arange(nb)[:, None] * BLOCK - BLOCK + jnp.arange(2 * BLOCK)[None, :]
    diff = qpos[:, :, None] - band_pos[:, None, :]
    band_ok = (diff >= 0) & (diff < WINDOW) & (band_pos[:, None, :] >= N_META)
    meta_ok = jnp.arange(N_META)[None, None, :] <= qpos[:, :, None]
    return jnp.concatenate([meta_ok, band_ok], axis=-1)

def sliding_window_attention(u, w_q, q_g, sinks, w_o, k, v):
    b, l, _ = u.shape
    nb = l // BLOCK
    q = (u @ w_q).reshape(b, l, N_KV_HEADS, Q_PER_KV, HEAD_DIM)
    q = rms_norm(q, q_g).reshape(b, nb, BLOCK, N_KV_HEADS, Q_PER_KV, HEAD_DIM)
    kw = band_keys(k, nb)
    vw = band_keys(v, nb)
    s = jnp.einsum('bnqgrd,bnkgd->bgrnqk', q, kw).astype(jnp.float32) * (HEAD_DIM ** -0.5)
    s = jnp.where(window_mask(nb), s, NEG_INF)
    sink = sinks.astype(jnp.float32).reshape(1, N_KV_HEADS, Q_PER_KV, 1, 1, 1)
    m = jnp.maximum(jnp.max(s, axis=-1, keepdims=True), sink)
    p = jnp.exp(s - m)
    denom = jnp.sum(p, axis=-1, keepdims=True) + jnp.exp(sink - m)
    p = (p / denom).astype(vw.dtype)
    o = jnp.einsum('bgrnqk,bnkgd->bnqgrd', p, vw).reshape(b, l, N_HEADS * HEAD_DIM)
    return o @ w_o

def setup_inputs(seed: int = 0) -> dict:
    key = jax.random.key(seed)
    ks = jax.random.split(key, 21)
    out_scale = (2 * DEPTH) ** -0.5
    kvd = 2 * N_KV_HEADS * HEAD_DIM
    qd = N_HEADS * HEAD_DIM

    def nrm(k, shape, scale):
        return jax.random.normal(k, shape, jnp.float32) * scale

    def gain(k, shape):
        return 1.0 + nrm(k, shape, 0.02)

    return {
        "x": nrm(ks[0], (BATCH, SEQ, D_MODEL), 1.0),
        "meta_tokens": nrm(ks[1], (N_META, D_MODEL), 1.0),
        "norm_mix": gain(ks[2], (DEPTH, D_MODEL)),
        "norm_ffn": gain(ks[3], (DEPTH, D_MODEL)),
        "conv_w_in": nrm(ks[4], (N_A_LAYERS, D_MODEL, 2 * D_MODEL), D_MODEL ** -0.5),
        "conv_b_in": nrm(ks[5], (N_A_LAYERS, 2 * D_MODEL), 0.02),
        "conv_dw": nrm(ks[6], (N_A_LAYERS, CONV_WIDTH, D_MODEL), CONV_WIDTH ** -0.5),
        "conv_ln_g": gain(ks[7], (N_A_LAYERS, D_MODEL)),
        "conv_ln_b": nrm(ks[8], (N_A_LAYERS, D_MODEL), 0.02),
        "conv_w_out": nrm(ks[9], (N_A_LAYERS, D_MODEL, D_MODEL), D_MODEL ** -0.5 * out_scale),
        "conv_b_out": nrm(ks[10], (N_A_LAYERS, D_MODEL), 0.02),
        "kv_norm": gain(ks[11], (D_MODEL,)),
        "w_kv": nrm(ks[12], (D_MODEL, kvd), D_MODEL ** -0.5),
        "k_norm": gain(ks[13], (HEAD_DIM,)),
        "w_q": nrm(ks[14], (N_B_LAYERS, D_MODEL, qd), D_MODEL ** -0.5),
        "q_norm": gain(ks[15], (N_B_LAYERS, HEAD_DIM)),
        "attn_sinks": nrm(ks[16], (N_B_LAYERS, N_HEADS), 0.5),
        "w_o": nrm(ks[17], (N_B_LAYERS, qd, D_MODEL), qd ** -0.5 * out_scale),
        "ffn_w_gate": nrm(ks[18], (DEPTH, D_MODEL, D_FF), D_MODEL ** -0.5),
        "ffn_w_up": nrm(ks[19], (DEPTH, D_MODEL, D_FF), D_MODEL ** -0.5),
        "ffn_w_down": nrm(ks[20], (DEPTH, D_FF, D_MODEL), D_FF ** -0.5 * out_scale),
    }

def reference(x, meta_tokens, norm_mix, norm_ffn, conv_w_in, conv_b_in, conv_dw, conv_ln_g, conv_ln_b,
              conv_w_out, conv_b_out, kv_norm, w_kv, k_norm, w_q, q_norm, attn_sinks, w_o,
              ffn_w_gate, ffn_w_up, ffn_w_down):
    b, seq, d = x.shape
    l = N_META + seq
    lp = -(-l // BLOCK) * BLOCK
    meta = jnp.broadcast_to(meta_tokens.astype(x.dtype)[None], (b, N_META, d))
    h = jnp.concatenate([meta, x, jnp.zeros((b, lp - l, d), x.dtype)], axis=1)
    k_sh = None
    v_sh = None
    for layer in range(DEPTH):
        u = rms_norm(h, norm_mix[layer])
        if layer < N_A_LAYERS:
            i = layer
            h = h + conformer_conv(u, conv_w_in[i], conv_b_in[i], conv_dw[i], conv_ln_g[i],
                                   conv_ln_b[i], conv_w_out[i], conv_b_out[i])
        else:
            if layer == N_A_LAYERS:
                k_sh, v_sh = shared_kv(h, kv_norm, w_kv, k_norm)
            j = layer - N_A_LAYERS
            h = h + sliding_window_attention(u, w_q[j], q_norm[j], attn_sinks[j], w_o[j], k_sh, v_sh)
        h = h + swiglu(rms_norm(h, norm_ffn[layer]), ffn_w_gate[layer], ffn_w_up[layer], ffn_w_down[layer])
    return h[:, N_META:l]


_drawn_inputs = setup_inputs


def setup_inputs(seed=0):
    import zlib

    import numpy as np

    out = dict(_drawn_inputs(seed))
    spreads = {}
    factors = {'norm_mix': 7.891,
     'norm_ffn': 5.262,
     'conv_b_in': 7.614,
     'conv_ln_g': 7.497,
     'conv_ln_b': 8.0,
     'kv_norm': 8.0,
     'k_norm': 8.0,
     'q_norm': 8.0,
     'attn_sinks': 8.0}
    for name, (base, spread) in spreads.items():
        noise = np.random.default_rng([zlib.crc32(name.encode()), seed]).standard_normal(out[name].shape)
        drawn = base * np.exp(spread * noise) if base else spread * noise
        out[name] = __import__('jax').numpy.asarray(drawn.astype(out[name].dtype))
    for name, factor in factors.items():
        out[name] = (out[name] * factor).astype(out[name].dtype)
    return out
```

```python
from contextlib import ExitStack

import concourse.bass as bass
from concourse import mybir

F32 = mybir.dt.float32
F32R = mybir.dt.float32r
ACT = mybir.ActivationFunctionType
ALU = mybir.AluOpType
AX_X = mybir.AxisListType.X

P = 128
EPS = 1e-6
NEG = -1e30
SLOTS = 4
WIDE = 1024
PE_TAPS = 8
LAG_HI = 3
LAG_LO = 2


def trunk_kernel(nc, x, meta_tokens, norm_mix, norm_ffn, conv_w_in, conv_b_in, conv_dw, conv_ln_g, conv_ln_b,
                 conv_w_out, conv_b_out, kv_norm, w_kv, k_norm, w_q, q_norm, attn_sinks, w_o,
                 ffn_w_gate, ffn_w_up, ffn_w_down, out):
    _, SEQ, D = x.shape
    META = meta_tokens.shape[0]
    T = META + SEQ
    KT = D // P
    HALF = T // 2
    TILES = SEQ // P
    TAPS = conv_dw.shape[1]
    PAD = TAPS - 1
    DVE_TAPS = TAPS - PE_TAPS
    DH = k_norm.shape[0]
    HEADS = attn_sinks.shape[1]
    GROUPS = w_kv.shape[1] // (2 * DH)
    PER = HEADS // GROUPS
    PAIRS = GROUPS // 2
    KV = GROUPS * DH
    FT = ffn_w_gate.shape[2] // P
    FH = [12, FT - 12]
    PARTS = [6, 5]
    assert (D, T, DH, TILES, GROUPS, PER, FT) == (1024, 528, 64, 4, 4, 4, 22)

    q = 0
    Q_IN = q; q += 2 * KT // SLOTS
    Q_CO = q; q += KT // SLOTS
    Q_GU, Q_DN = [[0, 0], [0, 0]], [[0, 0], [0, 0]]
    for s in range(2):
        Q_GU[0][s] = q; q += 2 * FH[s] // SLOTS
        Q_DN[0][s] = q; q += 2 * KT // SLOTS
    Q_KV = q; q += 1
    Q_Q = q; q += KT // SLOTS
    Q_O = q; q += KT // SLOTS
    for s in range(2):
        Q_GU[1][s] = q; q += 2 * FH[s] // SLOTS
        Q_DN[1][s] = q; q += 2 * KT // SLOTS
    QUADS = q

    o = 0
    O_IN = o; o += 2 * KT
    O_CO = o; o += KT
    O_GU, O_DN = [[0, 0], [0, 0]], [[0, 0], [0, 0]]
    for L in range(2):
        if L == 1:
            O_O = o; o += KT
        for s in range(2):
            O_GU[L][s] = o; o += 2 * FH[s]
            O_DN[L][s] = o; o += KT

    G0 = [[0, FH[0]], [FT, FT + FH[0]]]

    R_MIX0, R_MEAN, R_VAR, R_FFN0, R_MIX1, R_FFN1 = range(6)
    STEPS = [6, 1, 6, 6, 6, 6]
    PREP = {R_MIX0: 0, R_FFN0: 1, R_MIX1: 2, R_FFN1: 3}
    SQ0 = {R_MIX0: 0, R_VAR: 1, R_FFN0: 2, R_MIX1: 3, R_FFN1: 4}

    rows = {}
    at = 0
    for name, n in (("mix0", KT), ("mix1", KT), ("ffn0", KT), ("ffn1", KT), ("b_in", 2 * KT), ("ln_g", KT),
                    ("ln_b", KT), ("b_out", KT), ("kv", KT)):
        rows[name] = at
        at += n
    NROWS = at
    units = [(a, b, i) for a in range(PAIRS) for b in range(2) for i in range(TILES)]
    NU = len(units)
    QJ = PAIRS * PER

    ctx = ExitStack()
    with ctx:
        def sb(name, shape, dt, where=ctx):
            return where.enter_context(nc.sbuf_tensor(name, shape, dt))

        def sem(name):
            return ctx.enter_context(nc.semaphore(name))

        h = sb("h", [P, KT, T], F32)
        act_hi = sb("act_hi", [P, KT, T], F32R)
        act_lo = sb("act_lo", [P, KT, T], F32R)
        raw = sb("raw", [P, SLOTS, WIDE], F32)
        w_hi = sb("w_hi", [P, SLOTS, WIDE], F32R)
        w_lo = sb("w_lo", [P, SLOTS, WIDE], F32R)
        tmp = sb("tmp", [P, 4, T], F32)
        sq = sb("sq", [P, 2, T], F32)
        acc = sb("acc", [P, T], F32)
        rb = sb("rb", [P, T], F32)
        ident = sb("ident", [P, P], F32)
        ones = sb("ones", [P, P], F32)
        blk2 = sb("blk2", [P, 2], F32)
        mask = sb("mask", [P, META + 2 * P], F32)
        mask0 = sb("mask0", [P, META + P], F32)
        par = sb("par", [P, NROWS], F32)
        sinks = sb("sinks", [P, HEADS], F32)
        gk = sb("gk", [P, DH], F32)
        gq = sb("gq", [P, DH], F32)
        gqk = sb("gqk", [P, DH], F32)
        st = sb("st", [P, 5, 5], F32)
        diag = tmp[:, 2:4, :].rearrange("p a t -> p (a t)")[:, 0:5 * P].rearrange("p (t n) -> p t n", t=5)

        rk = sb("rk", [P, 5, (1 + TILES) * GROUPS], F32)
        rq = sb("rq", [P, 5, 2 * PER * TILES], F32)
        rqs = sb("rqs", [P, PAIRS, PER, TILES, 2], F32)
        smx = sb("smx", [P, 2, 8, PER], F32)
        sden = sb("sden", [P, 2, PER], F32)

        with ExitStack() as region:
            dw = sb("dw", [P, KT, 32], F32, region)
            dw_hi = sb("dw_hi", [P, KT, 32], F32R, region)
            dw_lo = sb("dw_lo", [P, KT, 32], F32R, region)
            apad = sb("apad", [P, PAD + T], F32, region)
            a_hi = sb("a_hi", [P, 2, PAD + T], F32R, region)
            a_lo = sb("a_lo", [P, 2, PAD + T], F32R, region)
            ca = sb("ca", [P, T], F32, region)
            cb = sb("cb", [P, T], F32, region)
            dg_hi = sb("dg_hi", [P, 2, PE_TAPS, P], F32R, region)
            dg_lo = sb("dg_lo", [P, 2, PE_TAPS, P], F32R, region)
            with ExitStack() as early:
                x_tok = sb("x_tok", [P, TILES, D], F32, early)
                meta_tok = sb("meta_tok", [META, D], F32, early)
                par_rows = sb("par_rows", [NROWS, P], F32, early)
                dw_rows = sb("dw_rows", [TAPS, D], F32, early)
            conv = sb("conv", [P, KT, T], F32, region)
            ln_hi = sb("ln_hi", [P, KT, T], F32R, region)
            ln_lo = sb("ln_lo", [P, KT, T], F32R, region)
        with ExitStack() as region:
            hid_hi = sb("hid_hi", [P, FH[0], T], F32R, region)
            hid_lo = sb("hid_lo", [P, FH[0], T], F32R, region)
        with ExitStack() as region:
            q_hi = sb("q_hi", [P, QJ, SEQ], F32R, region)
            q_lo = sb("q_lo", [P, QJ, SEQ], F32R, region)
            kt_hi = sb("kt_hi", [P, PAIRS, T], F32R, region)
            kt_lo = sb("kt_lo", [P, PAIRS, T], F32R, region)
            v_hi = sb("v_hi", [P, 1 + TILES, KV], F32R, region)
            v_lo = sb("v_lo", [P, 1 + TILES, KV], F32R, region)
            with ExitStack() as early:
                kx = sb("kx", [P, 1 + TILES, KV], F32, early)
                kva_hi = sb("kva_hi", [P, 2, KT, P], F32R, early)
                kva_lo = sb("kva_lo", [P, 2, KT, P], F32R, early)
                kva = sb("kva", [P, 2, KT, P], F32, early)
            s_sb = sb("s_sb", [P, 2, PER, META + 2 * P], F32, region)
            pt_hi = sb("pt_hi", [P, 3, PER * P], F32R, region)
            pt_lo = sb("pt_lo", [P, 3, PER * P], F32R, region)
            o_hi = sb("o_hi", [P, PER, SEQ], F32R, region)
            o_lo = sb("o_lo", [P, PER, SEQ], F32R, region)
        ps = ctx.enter_context(nc.psum_tensor("ps", [P, 8, 512], F32))

        par_in, sink_in, dwr_in = sem("par_in"), sem("sink_in"), sem("dwr_in")
        x_in = [sem(f"x_in{i}") for i in range(1 + TILES)]
        landed = [sem(f"landed{c}") for c in range(SLOTS)]
        landed2 = [sem(f"landed_second_half{c}") for c in range(SLOTS)]
        hi_done, lo_done, used = sem("w_hi_done"), sem("w_lo_done"), sem("w_used")
        consts, zeroed = sem("consts"), sem("acc_zeroed")
        turned, turned_out = sem("turned"), sem("turned_out")
        dw_split = sem("dw_split")
        sq_done, acc_added = sem("sq_done"), sem("acc_added")
        ahi_done, alo_done = sem("act_hi_done"), sem("act_lo_done")
        st_ready, st_step, st_sqrt = sem("st_ready"), sem("st_step"), sem("st_sqrt")
        diag_done, bc_ready, rb_done = sem("diag_done"), sem("bc_ready"), sem("rb_done")
        slot_free = sem("slot_free")
        sig_done, a_done, cahi_done, calo_done = sem("sig_done"), sem("a_done"), sem("conv_a_hi"), sem("conv_a_lo")
        tap_done, taps_pe, conv_mix, c_done = sem("tap_done"), sem("taps_pe"), sem("conv_mix"), sem("c_done")
        dg_done = sem("dg_done")
        cc_done, ln_mul, ln_silu, lnhi_done, lnlo_done = (sem("cc_done"), sem("ln_mul"), sem("ln_silu"),
                                                         sem("ln_hi_done"), sem("ln_lo_done"))
        silu_done, p_done, hidhi_done, hidlo_done = (sem("silu_done"), sem("hid_product"), sem("hid_hi_done"),
                                                     sem("hid_lo_done"))
        kva_done, kvahi_done, kvalo_done, kv_ready = sem("kva_done"), sem("kva_hi"), sem("kva_lo"), sem("kv_ready")
        vhi_done, kx_done, ksq_done, k_step, k_sqrt = (sem("v_hi_done"), sem("kx_done"), sem("ksq_done"),
                                                      sem("k_step"), sem("k_sqrt"))
        kt_ready, kthi_done, ktlo_done = sem("kt_ready"), sem("kt_hi_done"), sem("kt_lo_done")
        q_out, qsq_done, qhi_done, qlo_done, qss_ready = (sem("q_out"), sem("qsq_done"), sem("q_hi_done"),
                                                         sem("q_lo_done"), sem("q_sums"))
        rq_step, rq_sqrt = sem("rq_step"), sem("rq_sqrt")
        s_ready, s_read, m_step, p_exp, p_step, p_norm = (sem("s_ready"), sem("s_read"), sem("m_step"), sem("p_exp"),
                                                         sem("p_step"), sem("p_norm"))
        pt_ready, pthi_done, ptlo_done, pv_ready = sem("pt_ready"), sem("pt_hi_done"), sem("pt_lo_done"), sem("pv_ready")
        ohi_done, olo_done = sem("o_hi_done"), sem("o_lo_done")
        outT_ready, out_sb, out_sent = sem("out_turned"), sem("out_copied"), [sem("out_sent0"), sem("out_sent1")]

        v_low, gqk_done = sem("v_low_done"), sem("gqk_done")
        tmp2k = tmp[:, :, :].rearrange("p a t -> p (a t)")[:, 0:(1 + TILES) * KV]

        block = ctx.enter_context(nc.Block())

        def n_of(qd, c):
            return qd * SLOTS + c

        def slot_bank(o):
            return 2 * (o % 2)

        def pair_view(bank, cols=None):
            return ps[:, bank:bank + 2, 0:HALF]

        def two(ap):
            return ap.rearrange("p (b n) -> p b n", b=2)

        def quad_loop(eng, start, count, body):
            body(start, True)
            if count > 1:
                with eng.Fori(start + 1, start + count) as qd:
                    body(qd, False)

        def steps_before(r):
            return sum(STEPS[:r])

        def sqrts_before(r):
            return sum(1 for s in STEPS[:r] if s > 1)

        @block.sync
        def _(sp):
            sp.dma_start(meta_tok[:, :], meta_tokens).then_inc(x_in[0], 16)
            for i in range(TILES):
                sp.dma_start(x_tok[:, i, :], x[0, i * P:(i + 1) * P, :]).then_inc(x_in[1 + i], 16)

            def col_of(i):
                return i * P if isinstance(i, int) else sp.snap(i * P)

            def load(qd, c, src, k):
                if not (isinstance(qd, int) and qd == 0):
                    sp.wait_ge(lo_done, n_of(qd, c) - SLOTS + 1)
                sp.dma_start(raw[:, c, 0:k * P].rearrange("p (k n) -> p k n", k=k), src).then_inc(landed[c], 16)

            w_in = conv_w_in[0].rearrange("(k p) n -> p k n", p=P)

            def conv_in(qd, first):
                for c in range(SLOTS):
                    ct = (qd - Q_IN) * 2 + c // 2
                    col = col_of(ct + (KT if c % 2 == 0 else 0))
                    load(qd, c, w_in[:, :, bass.ds(col, P)], KT)
            quad_loop(sp, Q_IN, 4, conv_in)

            w_out = conv_w_out[0].rearrange("(k p) n -> p k n", p=P)
            for m in range(KT):
                load(Q_CO + m // 4, m % 4, w_out[:, :, m * P:(m + 1) * P], KT)

            def ffn(L, s):
                gate = ffn_w_gate[L].rearrange("(k p) n -> p k n", p=P)
                up = ffn_w_up[L].rearrange("(k p) n -> p k n", p=P)
                down = ffn_w_down[L].rearrange("(k p) n -> p k n", p=P)
                f0 = s * FH[0]

                def gu(qd, first):
                    for c in range(SLOTS):
                        col = col_of((qd - Q_GU[L][s]) * 2 + c // 2 + f0)
                        load(qd, c, (gate if c % 2 == 0 else up)[:, :, bass.ds(col, P)], KT)

                def dn(qd, first):
                    for c in range(SLOTS):
                        col = col_of((qd - Q_DN[L][s]) * 2 + c // 2)
                        k0 = f0 + (c % 2) * PARTS[s]
                        load(qd, c, down[:, k0:k0 + PARTS[s], bass.ds(col, P)], PARTS[s])
                quad_loop(sp, Q_GU[L][s], FH[s] // 2, gu)
                quad_loop(sp, Q_DN[L][s], KT // 2, dn)

            ffn(0, 0)
            ffn(0, 1)

            w_kv_v = w_kv.rearrange("(k p) n -> p k n", p=P)
            for c in range(SLOTS):
                sp.wait_ge(lo_done, n_of(Q_KV, c) - SLOTS + 1)
                sp.dma_start(raw[:, c, :].rearrange("p (k n) -> p k n", k=2), w_kv_v[:, 2 * c:2 * c + 2, :])\
                  .then_inc(landed[c], 16)

            w_q_v = w_q[0].rearrange("(k p) (g r d) -> g r p k d", p=P, g=GROUPS, r=PER)
            for j in range(QJ):
                c = j % 4
                sp.wait_ge(lo_done, n_of(Q_Q + j // 4, c) - SLOTS + 1)
                dst = raw[:, c, :].rearrange("p (k n) -> p k n", k=KT)
                for b in range(2):
                    sp.dma_start(dst[:, :, b * DH:(b + 1) * DH], w_q_v[2 * (j // PER) + b, j % PER])\
                      .then_inc((landed, landed2)[b][c], 16)

            w_o_v = w_o[0].rearrange("(a b r d) n -> b a d r n", a=PAIRS, b=2, r=PER)
            for m in range(KT):
                c = m % 4
                sp.wait_ge(lo_done, n_of(Q_O + m // 4, c) - SLOTS + 1)
                for b in range(2):
                    for a in range(PAIRS):
                        dst = raw[b * DH:(b + 1) * DH, c, a * PER * P:(a + 1) * PER * P]
                        sp.dma_start(dst.rearrange("p (r n) -> p r n", r=PER), w_o_v[b, a, :, :, m * P:(m + 1) * P])\
                          .then_inc((landed if a == b == 0 else landed2)[c], 16)

            ffn(1, 0)
            ffn(1, 1)

        @block.scalar
        def _(act):
            for name, src in (("mix0", norm_mix[0]), ("mix1", norm_mix[1]), ("ffn0", norm_ffn[0]),
                              ("ffn1", norm_ffn[1]), ("b_in", conv_b_in[0]), ("ln_g", conv_ln_g[0]),
                              ("ln_b", conv_ln_b[0]), ("b_out", conv_b_out[0]), ("kv", kv_norm)):
                v = src.rearrange("(k p) -> k p", p=P)
                act.dma_start(par_rows[rows[name]:rows[name] + v.shape[0], :], v).then_inc(par_in, 16)
            act.dma_start(dw_rows[:, :], conv_dw[0]).then_inc(dwr_in, 16)
            for dst, src in ((gk, k_norm), (gq, q_norm[0]), (sinks, attn_sinks[0])):
                n = src.shape[0]
                act.dma_start(dst[:, :], src.rearrange("(a n) -> a n", a=1).broadcast_to([P, n]))\
                   .then_inc(sink_in, 16)

            def hi(qd, c):
                qd, c = (qd + c // SLOTS, c % SLOTS)
                static = isinstance(qd, int)
                if static and qd >= QUADS:
                    return
                act.wait_ge(landed[c], 16 * (qd + 1))
                if static and Q_Q <= qd < Q_Q + 2:
                    act.wait_ge(landed2[c], 16 * (qd - Q_Q + 1))
                if static and Q_O <= qd < Q_O + 2:
                    act.wait_ge(landed2[c], 16 * (2 + 3 * (qd - Q_O + 1)))
                if not (static and qd == 0):
                    act.wait_ge(used, n_of(qd, c) - SLOTS + 1)
                act.activation(w_hi[:, c, :], raw[:, c, :], ACT.Copy).then_inc(hi_done, 1)

            def square(r, k, src, ready, count):
                act.wait_ge(ready, count)
                if not (isinstance(k, int) and k < 2):
                    act.wait_ge(acc_added, 8 * r + k - 1)
                return act.activation(sq[:, k_par[0], :], src, ACT.Square).then_inc(sq_done, 1)

            k_par = [0]

            def prep(r, k, gain, ready, count):
                k_par[0] = k % 2
                square(r, k, h[:, k, :], ready, count)
                act.activation(act_hi[:, k, :], h[:, k, :], ACT.Copy,
                               scale=par[:, rows[gain] + k:rows[gain] + k + 1]).then_inc(ahi_done, 1)

            def stat_sqrt(r):
                act.wait_ge(st_step, steps_before(r) + 1)
                act.activation(st[:, 1, :], st[:, 0, :], ACT.Sqrt).then_inc(st_sqrt, 1)

            for c in range(LAG_HI):
                hi(0, c)
            act.wait_ge(turned_out, 2)
            act.activation(dw_hi[:, :, 0:TAPS], dw[:, :, 0:TAPS], ACT.Copy).then_inc(dw_split, 1)
            for k in range(KT):
                prep(R_MIX0, k, "mix0", turned_out, 2 + 1 + 2 * TILES)
            stat_sqrt(R_MIX0)

            def conv_in(qd, first):
                for e in range(2):
                    ct = (qd - Q_IN) * 2 + e
                    hi(qd, 2 * e + LAG_HI)
                    act.wait_ge(slot_free, O_IN + 2 * ct + 1)
                    if not (first and e == 0):
                        act.wait_ge(a_done, ct)
                    act.activation(tmp[:, 1, :], tmp[:, 0, :], ACT.Sigmoid,
                                   bias=par[:, bass.ds(rows["b_in"] + KT + ct, 1)]).then_inc(sig_done, 1)
                    hi(qd, 2 * e + 1 + LAG_HI)
                    act.wait_ge(a_done, ct + 1)
                    if not first:
                        act.wait_ge(taps_pe, ct - 1)
                    act.activation(a_hi[:, e, :], apad[:, :], ACT.Copy).then_inc(cahi_done, 1)
            quad_loop(act, Q_IN, 4, conv_in)

            for k in range(KT):
                k_par[0] = k % 2
                square(R_VAR, k, conv[:, k, :], cc_done, k + 1)
            stat_sqrt(R_VAR)
            for k in range(KT):
                act.wait_ge(ln_mul, k + 1)
                if k >= 2:
                    act.wait_ge(lnlo_done, k - 1)
                act.activation(tmp[:, k % 2, :], conv[:, k, :], ACT.Silu,
                               scale=par[:, rows["ln_g"] + k:rows["ln_g"] + k + 1],
                               bias=par[:, rows["ln_b"] + k:rows["ln_b"] + k + 1]).then_inc(ln_silu, 1)
                act.wait_ge(ln_silu, k + 1)
                act.activation(ln_hi[:, k, :], tmp[:, k % 2, :], ACT.Copy).then_inc(lnhi_done, 1)

            for m in range(KT):
                hi(Q_CO, m + LAG_HI)
                prep(R_FFN0, m, "ffn0", slot_free, O_CO + m + 1)
            stat_sqrt(R_FFN0)

            def ffn(L, s, gain, round_):
                N = T if L == 0 else SEQ

                def hid_hi_of(qd, e):
                    fi = (qd - Q_GU[L][s]) * 2 + e
                    g = G0[L][s] + fi
                    act.wait_ge(p_done, g + 1)
                    act.activation(hid_hi[:, bass.ds(fi, 1), 0:N], tmp[:, 3:4, 0:N], ACT.Copy)\
                       .then_inc(hidhi_done, 1)

                def gu(qd, first):
                    for e in range(2):
                        fi = (qd - Q_GU[L][s]) * 2 + e
                        g = G0[L][s] + fi
                        hi(qd, 2 * e + LAG_HI)
                        act.wait_ge(slot_free, O_GU[L][s] + 2 * fi + 1)
                        if not (isinstance(g, int) and g == 0):
                            act.wait_ge(p_done, g)
                        act.activation(tmp[:, 1, 0:N], tmp[:, 0, 0:N], ACT.Silu).then_inc(silu_done, 1)
                        hi(qd, 2 * e + 1 + LAG_HI)
                        if not (first and e == 0):
                            hid_hi_of(qd, e - 1)
                quad_loop(act, Q_GU[L][s], FH[s] // 2, gu)
                hid_hi_of(Q_GU[L][s] + FH[s] // 2 - 1, 1)

                def dn(qd, first):
                    for e in range(2):
                        m = (qd - Q_DN[L][s]) * 2 + e
                        hi(qd, 2 * e + LAG_HI)
                        hi(qd, 2 * e + 1 + LAG_HI)
                        if s == 1 and L == 0:
                            act.wait_ge(slot_free, O_DN[L][s] + m + 1)
                            if not (first):
                                act.wait_ge(acc_added, 8 * round_ + m - 1)
                            act.activation(sq[:, e, :], h[:, bass.ds(m, 1), :].rearrange("p a t -> p (a t)"),
                                           ACT.Square).then_inc(sq_done, 1)
                            act.activation(act_hi[:, bass.ds(m, 1), :], h[:, bass.ds(m, 1), :], ACT.Copy,
                                           scale=par[:, bass.ds(rows[gain] + m, 1)]).then_inc(ahi_done, 1)
                        if s == 1 and L == 1:
                            act.wait_ge(outT_ready, m + 1)
                            if not first:
                                act.wait_ge(out_sent[e], 16 * ((qd - Q_DN[L][s])))
                            act.activation(tmp[:, 2 + e, 0:SEQ], ps[:, 4 + e, :], ACT.Copy).then_inc(out_sb, 1)
                            act.wait_ge(out_sb, m + 1)
                            act.dma_start(out[0].rearrange("(i p) d -> p i d", p=P)[:, :, bass.ds(m * P, P)],
                                          tmp[:, 2 + e, 0:SEQ].rearrange("p (i n) -> p i n", i=TILES))\
                               .then_inc(out_sent[e], 16)
                if L == 1 and s == 1:
                    body_count = KT // 2
                    dn(Q_DN[L][s], True)
                    with act.Fori(Q_DN[L][s] + 1, Q_DN[L][s] + body_count - 1) as qd:
                        dn(qd, False)
                    dn(Q_DN[L][s] + body_count - 1, False)
                else:
                    quad_loop(act, Q_DN[L][s], KT // 2, dn)

            ffn(0, 0, None, None)
            ffn(0, 1, "mix1", R_MIX1)

            hi(Q_KV, LAG_HI)
            for t in range(1 + TILES):
                act.wait_ge(kva_done, t + 1)
                if t >= 2:
                    act.wait_ge(kv_ready, t - 1)
                act.activation(kva_hi[:, t % 2], kva[:, t % 2], ACT.Copy).then_inc(kvahi_done, 1)
                if t == 0:
                    stat_sqrt(R_MIX1)
                else:
                    act.wait_ge(kv_ready, t)
                    if t == 1:
                        act.wait_ge(st_step, steps_before(R_MIX1) + STEPS[R_MIX1])
                    act.activation(v_hi[:, t - 1, :], ps[:, 4 + (t - 1) % 2, KV:2 * KV], ACT.Copy,
                                   scale=st[:, 4, t - 1:t]).then_inc(vhi_done, 1)
            act.wait_ge(used, n_of(Q_KV, SLOTS))
            act.activation(v_hi[:, TILES, :], ps[:, 4 + TILES % 2, KV:2 * KV], ACT.Copy,
                           scale=st[:, 4, TILES:TILES + 1]).then_inc(vhi_done, 1)
            for c in range(LAG_HI):
                hi(Q_Q, c)
            act.wait_ge(kx_done, 1 + TILES)
            act.activation(tmp2k, kx[:, :, :].rearrange("p t n -> p (t n)"), ACT.Square).then_inc(ksq_done, 1)
            act.wait_ge(k_step, 2)
            act.activation(rk[:, 1, :], rk[:, 0, :], ACT.Sqrt).then_inc(k_sqrt, 1)

            def q_tile(j):
                if j + LAG_HI < 2 * KT:
                    hi(Q_Q, j + LAG_HI)
                act.wait_ge(q_out, j + 1)
                if j == 0:
                    act.wait_ge(k_step, 1)
                if j >= 2:
                    act.wait_ge(qss_ready, j - 1)
                act.activation(tmp[:, 2 + j % 2, 0:SEQ], tmp[:, j % 2, 0:SEQ], ACT.Square).then_inc(qsq_done, 1)
                act.activation(q_hi[:, j, :], tmp[:, j % 2, 0:SEQ], ACT.Copy).then_inc(qhi_done, 1)

            def q_sqrt(a):
                act.wait_ge(rq_step, 7 * a + 1)
                act.activation(rq[:, 1, :], rq[:, 0, :], ACT.Sqrt).then_inc(rq_sqrt, 1)

            def exps(u):
                a, b, i = units[u]
                n = META + P * (1 if i == 0 else 2)
                w = u % 2
                act.wait_ge(m_step, 4 * (u + 1))
                act.wait_ge(s_read, 4 * (u + 1))
                for r in range(PER):
                    act.activation(s_sb[:, w, r, 0:n], s_sb[:, w, r, 0:n], ACT.Exp, bias=smx[:, w, 3, r:r + 1],
                                   scale=rqs[:, a, r, i, b:b + 1], accum_out=smx[:, w, 6, r:r + 1]).then_inc(p_exp, 1)
                act.activation(smx[:, w, 5, :], smx[:, w, 4, :], ACT.Exp).then_inc(p_exp, 1)

            def pt_high(u):
                a, b, i = units[u]
                act.wait_ge(pt_ready, u + 1)
                if u >= 1:
                    act.wait_ge(pv_ready, u)
                act.activation(pt_hi[0:META, 0, :], ps[0:META, 6, :], ACT.Copy).then_inc(pthi_done, 1)
                if i > 0:
                    act.activation(pt_hi[:, 1, :], ps[:, 4, :], ACT.Copy).then_inc(pthi_done, 1)
                act.activation(pt_hi[:, 2, :], ps[:, 5, :], ACT.Copy).then_inc(pthi_done, 1)

            def o_high(u):
                a, b, i = units[u]
                rowsel = slice(b * DH, (b + 1) * DH)
                act.wait_ge(pv_ready, u + 1)
                dst = (o_hi, q_hi)[a]
                act.activation(dst[rowsel, 0:PER, i * P:(i + 1) * P],
                               ps[rowsel, 7, :].rearrange("p (r n) -> p r n", r=PER), ACT.Copy).then_inc(ohi_done, 1)

            for j in range(PER):
                q_tile(j)
            act.wait_ge(kt_ready, 1)
            for a in range(PAIRS):
                act.activation(kt_hi[:, a, META:T], ps[:, 4 + a, :], ACT.Copy).then_inc(kthi_done, 1)
                act.activation(kt_hi[:, a, 0:META], ps[:, 6, a * P:a * P + META], ACT.Copy).then_inc(kthi_done, 1)
            q_sqrt(0)
            exps(0)
            for u in range(NU):
                if u + 1 == NU // 2:
                    q_sqrt(1)
                pt_high(u)
                if u + 1 < NU:
                    exps(u + 1)
                if u < NU // 2 and u % 2 == 0:
                    q_tile(PER + u // 2)
                if u >= 1:
                    o_high(u - 1)
            o_high(NU - 1)

            for m in range(KT):
                hi(Q_O, m + LAG_HI)
                prep(R_FFN1, m, "ffn1", slot_free, O_O + m + 1)
            stat_sqrt(R_FFN1)
            ffn(1, 0, None, None)
            ffn(1, 1, None, None)
            for e in range(2):
                act.wait_ge(out_sent[e], 16 * (KT // 2))

        @block.gpsimd
        def _(pool):
            NC = 9
            pool.memset(ident[:, :], 0.0).then_inc(consts, 1)
            pool.memset(ones[:, :], 1.0).then_inc(consts, 1)
            pool.memset(blk2[:, :], 1.0).then_inc(consts, 1)
            pool.memset(mask[:, :], 0.0).then_inc(consts, 1)
            pool.memset(mask0[:, :], 0.0).then_inc(consts, 1)
            pool.memset(apad[:, 0:PAD], 0.0).then_inc(consts, 1)
            pool.wait_ge(consts, 6)
            pool.affine_select(out=ident[:, :], in_=ident[:, :], compare_op=ALU.not_equal, fill=1.0, base=0,
                               pattern=[[-1, P]], channel_multiplier=1).then_inc(consts, 1)
            pool.affine_select(out=blk2[:, :], in_=blk2[:, :], compare_op=ALU.is_ge, fill=0.0, base=0,
                               pattern=[[-DH, 2]], channel_multiplier=1).then_inc(consts, 1)
            pool.wait_ge(consts, 8)
            pool.affine_select(out=blk2[:, :], in_=blk2[:, :], compare_op=ALU.is_ge, fill=0.0, base=DH - 1,
                               pattern=[[DH, 2]], channel_multiplier=-1).then_inc(consts, 1)
            pool.affine_select(out=mask[:, META:META + P], in_=mask[:, META:META + P], compare_op=ALU.is_ge, fill=NEG,
                               base=-1, pattern=[[1, P]], channel_multiplier=-1).then_inc(consts, 1)
            for m_, at_ in ((mask, META + P), (mask0, META)):
                pool.affine_select(out=m_[:, at_:at_ + P], in_=m_[:, at_:at_ + P], compare_op=ALU.is_ge, fill=NEG,
                                   base=0, pattern=[[-1, P]], channel_multiplier=1).then_inc(consts, 1)

            def lo(qd, c):
                qd, c = (qd + c // SLOTS, c % SLOTS)
                if isinstance(qd, int) and qd >= QUADS:
                    return
                pool.wait_ge(hi_done, n_of(qd, c) + 1)
                pool.tensor_tensor(w_lo[:, c, :], raw[:, c, :], w_hi[:, c, :].bitcast(F32), ALU.subtract)\
                    .then_inc(lo_done, 1)

            def zero(r):
                if r > 0:
                    pool.wait_ge(st_ready, r)
                pool.memset(acc[:, :], 0.0).then_inc(zeroed, 1)

            def add(r, k, src, ready, count):
                pool.wait_ge(ready, count)
                if isinstance(k, int) and k == 0:
                    pool.wait_ge(zeroed, r + 1)
                else:
                    pool.wait_ge(acc_added, 8 * r + k)
                pool.tensor_tensor(acc[:, :], acc[:, :], src, ALU.add).then_inc(acc_added, 1)

            def add_square(r, k):
                add(r, k, sq[:, k % 2, :], sq_done, 8 * SQ0[r] + k + 1)

            zero(R_MIX0)
            for c in range(LAG_LO):
                lo(0, c)
            for k in range(KT):
                add_square(R_MIX0, k)
            zero(R_MEAN)

            def conv_in(qd, first):
                for e in range(2):
                    ct = (qd - Q_IN) * 2 + e
                    if first and e == 0:
                        pool.wait_ge(dw_split, 2)
                    if not first:
                        pool.wait_ge(taps_pe, ct - 1)
                    for dst, src in ((dg_hi, dw_hi), (dg_lo, dw_lo)):
                        w = src[:, bass.ds(ct, 1), DVE_TAPS:TAPS].bitcast(F32).rearrange("p a w -> p (a w)")
                        pool.tensor_tensor(dst[:, e], ident[:, :].unsqueeze(1).broadcast_to([P, PE_TAPS, P]),
                                           w.unsqueeze(2).broadcast_to([P, PE_TAPS, P]), ALU.mult)\
                            .then_inc(dg_done, 1)
                        lo(qd, 2 * e + (dst is dg_lo) + LAG_LO)
                    if not (first and e == 0):
                        add(R_MEAN, ct - 1, conv[:, bass.ds(ct - 1, 1), :].rearrange("p a t -> p (a t)"), c_done, ct)
            quad_loop(pool, Q_IN, 4, conv_in)
            add(R_MEAN, KT - 1, conv[:, KT - 1, :], c_done, KT)
            zero(R_VAR)
            for k in range(KT):
                add_square(R_VAR, k)
            zero(R_FFN0)
            for m in range(KT):
                lo(Q_CO, m + LAG_LO)
                add_square(R_FFN0, m)
            zero(R_MIX1)

            def ffn(L, s, round_):
                N = T if L == 0 else SEQ

                def gu(qd, first):
                    for e in range(2):
                        fi = (qd - Q_GU[L][s]) * 2 + e
                        g = G0[L][s] + fi
                        lo(qd, 2 * e + LAG_LO)
                        lo(qd, 2 * e + 1 + LAG_LO)
                        pool.wait_ge(silu_done, g + 1)
                        pool.wait_ge(slot_free, O_GU[L][s] + 2 * fi + 2)
                        if not (isinstance(g, int) and g == 0):
                            pool.wait_ge(hidlo_done, g)
                        pool.tensor_tensor(tmp[:, 3, 0:N], tmp[:, 1, 0:N], tmp[:, 2, 0:N], ALU.mult)\
                            .then_inc(p_done, 1)
                quad_loop(pool, Q_GU[L][s], FH[s] // 2, gu)

                def dn(qd, first):
                    for e in range(2):
                        m = (qd - Q_DN[L][s]) * 2 + e
                        lo(qd, 2 * e + LAG_LO)
                        lo(qd, 2 * e + 1 + LAG_LO)
                        if L == 0 and s == 1:
                            add(round_, m, sq[:, e, :], sq_done, 8 * SQ0[round_] + m + 1)
                if L == 1 and s == 1:
                    dn(Q_DN[L][s], True)
                    with pool.Fori(Q_DN[L][s] + 1, Q_DN[L][s] + KT // 2 - 1) as qd:
                        dn(qd, False)
                    dn(Q_DN[L][s] + KT // 2 - 1, False)
                else:
                    quad_loop(pool, Q_DN[L][s], KT // 2, dn)

            ffn(0, 0, None)
            ffn(0, 1, R_MIX1)
            zero(R_FFN1)
            for c in range(LAG_LO, SLOTS):
                lo(Q_KV, c)
            for j in range(KT + LAG_LO):
                lo(Q_Q, j)
            for m in range(KT):
                lo(Q_O, m + LAG_LO)
                add_square(R_FFN1, m)
            ffn(1, 0, None)
            ffn(1, 1, None)

        @block.vector
        def _(dve):
            dve.wait_ge(turned, 1)
            dve.tensor_copy(par[:, :], ps[:, 4, 0:NROWS]).then_inc(turned_out, 1)
            dve.wait_ge(turned, 2)
            dve.tensor_copy(dw[:, :, 0:TAPS], ps[:, 5, 0:KT * 32].rearrange("p (k w) -> p k w", w=32)[:, :, 0:TAPS])\
               .then_inc(turned_out, 1)
            dve.wait_ge(turned, 3)
            dve.tensor_copy(h[:, :, 0:META], ps[:, 0, 0:KT * META].rearrange("p (k n) -> p k n", k=KT))\
               .then_inc(turned_out, 1)
            for g in range(2 * TILES):
                i, kh = g // 2, g % 2
                dve.wait_ge(turned, 4 + g)
                dve.tensor_copy(h[:, 4 * kh:4 * kh + 4, META + i * P:META + (i + 1) * P],
                                ps[:, (g + 1) % 4, :].rearrange("p (k n) -> p k n", k=4)).then_inc(turned_out, 1)
            dve.wait_ge(dw_split, 1)
            dve.tensor_tensor(dw_lo[:, :, 0:TAPS], dw[:, :, 0:TAPS], dw_hi[:, :, 0:TAPS].bitcast(F32), ALU.subtract)\
               .then_inc(dw_split, 1)

            def prep(r, k, gain):
                dve.wait_ge(ahi_done, 8 * PREP[r] + k + 1)
                dve.scalar_tensor_tensor(out=act_lo[:, k, :], in0=h[:, k, :],
                                         scalar=par[:, rows[gain] + k:rows[gain] + k + 1],
                                         in1=act_hi[:, k, :].bitcast(F32), op0=ALU.mult, op1=ALU.subtract)\
                   .then_inc(alo_done, 1)

            def newton(s, step, base, sqrt_sem, sqrt_count, ms, sd, r, t, res, last=None):
                dve.wait_ge(sqrt_sem, sqrt_count)
                dve.reciprocal(r, sd).then_inc(step, 1)
                dve.wait_ge(step, base + 1)
                dve.tensor_tensor(t, r, r, ALU.mult).then_inc(step, 1)
                dve.wait_ge(step, base + 2)
                dve.tensor_tensor(t, t, ms, ALU.mult).then_inc(step, 1)
                dve.wait_ge(step, base + 3)
                dve.tensor_scalar(t, t, -0.5, 1.5, ALU.mult, ALU.add).then_inc(step, 1)
                dve.wait_ge(step, base + 4)
                dve.tensor_tensor(res, r, t, ALU.mult).then_inc(step, 1)

            def stats(r):
                b0 = steps_before(r)
                dve.wait_ge(st_ready, r + 1)
                if r > 0:
                    dve.wait_ge(diag_done, r)
                if STEPS[r] == 1:
                    dve.tensor_scalar(st[:, 4, :], ps[:, 6, 0:5], -1.0 / D, None, ALU.mult).then_inc(st_step, 1)
                else:
                    dve.tensor_scalar(st[:, 0, :], ps[:, 6, 0:5], 1.0 / D, EPS, ALU.mult, ALU.add)\
                       .then_inc(st_step, 1)
                    newton(None, st_step, b0 + 1, st_sqrt, sqrts_before(r) + 1, st[:, 0, :], st[:, 1, :],
                           st[:, 2, :], st[:, 3, :], st[:, 4, :])
                dve.wait_ge(st_step, b0 + STEPS[r])
                if r > 0:
                    dve.wait_ge(bc_ready, r)
                dve.tensor_tensor(diag[:, :, :], ident[:, :].unsqueeze(1).broadcast_to([P, 5, P]),
                                  st[:, 4, :].unsqueeze(2).broadcast_to([P, 5, P]), ALU.mult).then_inc(diag_done, 1)
                dve.wait_ge(bc_ready, r + 1)
                dve.tensor_copy(rb[:, 0:META], ps[:, 6, P:P + META]).then_inc(rb_done, 1)
                dve.tensor_copy(rb[:, META:T], ps[:, 7, :]).then_inc(rb_done, 1)
                dve.wait_ge(rb_done, 2 * (r + 1))

            for k in range(KT):
                prep(R_MIX0, k, "mix0")
            dve.wait_ge(consts, 12)
            stats(R_MIX0)

            rb2 = two(rb[:, :])

            def conv_in(qd, first):
                for e in range(2):
                    ct = (qd - Q_IN) * 2 + e
                    prime = first and e == 0
                    dve.wait_ge(used, 2 * ct + 1)
                    if not prime:
                        dve.wait_ge(sig_done, ct)
                    dve.tensor_tensor(two(tmp[:, 0, :]), pair_view(0), rb2, ALU.mult).then_inc(slot_free, 1)
                    dve.wait_ge(used, 2 * ct + 2)
                    if not prime:
                        dve.wait_ge(a_done, ct)
                    dve.tensor_tensor(two(tmp[:, 2, :]), pair_view(2), rb2, ALU.mult).then_inc(slot_free, 1)
                    dve.wait_ge(sig_done, ct + 1)
                    dve.wait_ge(slot_free, O_IN + 2 * ct + 2)
                    if not prime:
                        dve.wait_ge(c_done, ct)
                    dve.scalar_tensor_tensor(out=apad[:, PAD:PAD + T], in0=tmp[:, 2, :],
                                             scalar=par[:, bass.ds(rows["b_in"] + ct, 1)], in1=tmp[:, 1, :],
                                             op0=ALU.add, op1=ALU.mult).then_inc(a_done, 1)
                    dve.wait_ge(a_done, ct + 1)

                    def tap(w):
                        dst = (ca, cb)[w % 2]
                        tapw = dw[:, bass.ds(ct, 1), w:w + 1].rearrange("p a w -> p (a w)")
                        if w < 2:
                            dve.tensor_scalar(dst[:, :], apad[:, w:w + T], tapw, None, ALU.mult).then_inc(tap_done, 1)
                        else:
                            dve.wait_ge(tap_done, DVE_TAPS * ct + w - 1)
                            dve.scalar_tensor_tensor(out=dst[:, :], in0=apad[:, w:w + T], scalar=tapw,
                                                     in1=dst[:, :], op0=ALU.mult, op1=ALU.add).then_inc(tap_done, 1)
                    for w in range(4):
                        tap(w)
                    dve.wait_ge(cahi_done, ct + 1)
                    dve.tensor_tensor(a_lo[:, e, :], apad[:, :], a_hi[:, e, :].bitcast(F32), ALU.subtract)\
                       .then_inc(calo_done, 1)
                    for w in range(4, DVE_TAPS):
                        tap(w)
                    dve.wait_ge(taps_pe, ct + 1)
                    dve.wait_ge(tap_done, DVE_TAPS * (ct + 1))
                    dve.tensor_tensor(two(cb[:, :]), pair_view(4), two(cb[:, :]), ALU.add).then_inc(conv_mix, 1)
                    dve.wait_ge(conv_mix, ct + 1)
                    dve.tensor_tensor(conv[:, bass.ds(ct, 1), :].rearrange("p a t -> p (a t)"), ca[:, :], cb[:, :],
                                      ALU.add).then_inc(c_done, 1)
            quad_loop(dve, Q_IN, 4, conv_in)

            stats(R_MEAN)
            for k in range(KT):
                if k == 0:
                    dve.wait_ge(acc_added, 8 * (R_MEAN + 1))
                    dve.wait_ge(c_done, KT)
                dve.tensor_tensor(conv[:, k, :], conv[:, k, :], rb[:, :], ALU.add).then_inc(cc_done, 1)
            dve.wait_ge(cc_done, KT)
            stats(R_VAR)

            def ln_low(k):
                dve.wait_ge(lnhi_done, k + 1)
                dve.tensor_tensor(ln_lo[:, k, :], tmp[:, k % 2, :], ln_hi[:, k, :].bitcast(F32), ALU.subtract)\
                   .then_inc(lnlo_done, 1)
            for k in range(KT):
                dve.tensor_tensor(conv[:, k, :], conv[:, k, :], rb[:, :], ALU.mult).then_inc(ln_mul, 1)
                if k >= 2:
                    ln_low(k - 2)
            dve.wait_ge(ln_mul, KT)
            ln_low(KT - 2)
            ln_low(KT - 1)

            for m in range(KT):
                dve.wait_ge(used, n_of(Q_CO, m) + 1)
                dve.scalar_tensor_tensor(out=two(h[:, m, :]), in0=pair_view(slot_bank(O_CO + m)),
                                         scalar=par[:, rows["b_out"] + m:rows["b_out"] + m + 1], in1=two(h[:, m, :]),
                                         op0=ALU.add, op1=ALU.add).then_inc(slot_free, 1)
                if m >= 1:
                    prep(R_FFN0, m - 1, "ffn0")
            prep(R_FFN0, KT - 1, "ffn0")
            stats(R_FFN0)

            def ffn(L, s, gain, round_):
                N = T if L == 0 else SEQ
                if L == 0:
                    view = lambda ap: two(ap)
                    bank = lambda b: pair_view(b)
                    rbv = rb2
                else:
                    view = lambda ap: ap
                    bank = lambda b: ps[:, b, :]
                    rbv = rb[:, META:T]

                def low(qd, e):
                    fi = (qd - Q_GU[L][s]) * 2 + e
                    g = G0[L][s] + fi
                    dve.wait_ge(hidhi_done, g + 1)
                    dve.tensor_tensor(hid_lo[:, bass.ds(fi, 1), 0:N], tmp[:, 3:4, 0:N],
                                      hid_hi[:, bass.ds(fi, 1), 0:N].bitcast(F32), ALU.subtract)\
                       .then_inc(hidlo_done, 1)

                def gu(qd, first):
                    for e in range(2):
                        fi = (qd - Q_GU[L][s]) * 2 + e
                        g = G0[L][s] + fi
                        dve.wait_ge(used, n_of(qd, 2 * e) + 1)
                        if not (isinstance(g, int) and g == 0):
                            dve.wait_ge(silu_done, g)
                        dve.tensor_tensor(view(tmp[:, 0, 0:N]), bank(0), rbv, ALU.mult).then_inc(slot_free, 1)
                        if not (first and e == 0):
                            low(qd, e - 1)
                        dve.wait_ge(used, n_of(qd, 2 * e + 1) + 1)
                        if not (isinstance(g, int) and g == 0):
                            dve.wait_ge(p_done, g)
                        dve.tensor_tensor(view(tmp[:, 2, 0:N]), bank(2), rbv, ALU.mult).then_inc(slot_free, 1)
                quad_loop(dve, Q_GU[L][s], FH[s] // 2, gu)
                low(Q_GU[L][s] + FH[s] // 2 - 1, 1)

                def prep_m(qd, e):
                    m = (qd - Q_DN[L][s]) * 2 + e
                    dve.wait_ge(ahi_done, 8 * PREP[round_] + m + 1)
                    dve.scalar_tensor_tensor(out=act_lo[:, bass.ds(m, 1), :], in0=h[:, bass.ds(m, 1), :],
                                             scalar=par[:, bass.ds(rows[gain] + m, 1)],
                                             in1=act_hi[:, bass.ds(m, 1), :].bitcast(F32), op0=ALU.mult,
                                             op1=ALU.subtract).then_inc(alo_done, 1)

                def dn(qd, first):
                    for e in range(2):
                        m = (qd - Q_DN[L][s]) * 2 + e
                        dve.wait_ge(used, n_of(qd, 2 * e + 1) + 1)
                        src = h[:, bass.ds(m, 1), T - N:T].rearrange("p a t -> p (a t)")
                        if L == 1 and s == 1:
                            if not first:
                                dve.wait_ge(outT_ready, m - 1)
                            dst = tmp[:, e, 0:N]
                        else:
                            dst = src
                        dve.tensor_tensor(view(dst), bank(2 * e), view(src), ALU.add).then_inc(slot_free, 1)
                        if round_ is not None and not (first and e == 0):
                            prep_m(qd, e - 1)
                quad_loop(dve, Q_DN[L][s], KT // 2, dn)
                if round_ is not None:
                    prep_m(Q_DN[L][s] + KT // 2 - 1, 1)

            ffn(0, 0, None, None)
            ffn(0, 1, "mix1", R_MIX1)

            def tok(t):
                return slice(0, P) if t == 0 else slice(META + (t - 1) * P, META + t * P)

            def kv_in(t):
                if t >= 2:
                    dve.wait_ge(kvahi_done, t - 1)
                    dve.wait_ge(kvalo_done, t - 1)
                g = par[:, rows["kv"]:rows["kv"] + KT].unsqueeze(2).broadcast_to([P, KT, P])
                dve.tensor_tensor(kva[:, t % 2], h[:, :, tok(t)], g, ALU.mult).then_inc(kva_done, 1)

            def kv_low(t):
                dve.wait_ge(kvahi_done, t + 1)
                dve.tensor_tensor(kva_lo[:, t % 2], kva[:, t % 2], kva_hi[:, t % 2].bitcast(F32), ALU.subtract)\
                   .then_inc(kvalo_done, 1)

            def kv_out(t):
                src = ps[:, 4 + t % 2, :]
                dve.wait_ge(vhi_done, t + 1)
                dve.scalar_tensor_tensor(out=v_lo[:, t, :], in0=src[:, KV:2 * KV], scalar=st[:, 4, t:t + 1],
                                         in1=v_hi[:, t, :].bitcast(F32), op0=ALU.mult, op1=ALU.subtract)\
                   .then_inc(v_low, 1)
                dve.tensor_scalar(kx[:, t, :], src[:, 0:KV], st[:, 4, t:t + 1], None, ALU.mult).then_inc(kx_done, 1)

            kv_in(0)
            kv_in(1)
            kv_low(0)
            stats(R_MIX1)
            for t in range(1 + TILES):
                if t + 1 <= TILES:
                    kv_low(t + 1)
                if t + 2 <= TILES:
                    kv_in(t + 2)
                kv_out(t)
            dve.wait_ge(sink_in, 48)
            dve.tensor_tensor(gqk[:, :], gk[:, :], gq[:, :], ALU.mult).then_inc(gqk_done, 1)

            def q_scale(j):
                dve.wait_ge(used, n_of(Q_Q, j) + 1)
                if j >= 2:
                    dve.wait_ge(qlo_done, j - 1)
                    dve.wait_ge(qsq_done, j - 1)
                dve.tensor_tensor(tmp[:, j % 2, 0:SEQ], ps[:, 2, :], rb[:, META:T], ALU.mult).then_inc(q_out, 1)

            def q_low(j):
                dve.wait_ge(qhi_done, j + 1)
                dve.tensor_tensor(q_lo[:, j, :], tmp[:, j % 2, 0:SEQ], q_hi[:, j, :].bitcast(F32), ALU.subtract)\
                   .then_inc(qlo_done, 1)

            dve.wait_ge(ksq_done, 1)
            dve.tensor_reduce(rk[:, 3, :], tmp2k.rearrange("p (t d) -> p t d", d=DH), AX_X, ALU.add)\
               .then_inc(k_step, 1)
            dve.wait_ge(k_step, 1)
            dve.tensor_scalar(rk[:, 0, :], rk[:, 3, :], 1.0 / DH, EPS, ALU.mult, ALU.add).then_inc(k_step, 1)
            q_scale(0)
            newton(None, k_step, 2, k_sqrt, 1, rk[:, 0, :], rk[:, 1, :], rk[:, 2, :], rk[:, 3, :], rk[:, 4, :])
            dve.wait_ge(k_step, 7)
            k3 = kx[:, :, :].rearrange("p t (g d) -> p (t g) d", d=DH)
            NG = (1 + TILES) * GROUPS
            dve.tensor_tensor(k3, k3, rk[:, 4, :].unsqueeze(2).broadcast_to([P, NG, DH]), ALU.mult)\
               .then_inc(k_step, 1)
            dve.wait_ge(k_step, 8)
            dve.wait_ge(gqk_done, 1)
            dve.tensor_tensor(k3, k3, gqk[:, :].unsqueeze(1).broadcast_to([P, NG, DH]), ALU.mult)\
               .then_inc(k_step, 1)
            q_low(0)
            for j in range(1, PER):
                q_scale(j)
                q_low(j)
            for a in range(PAIRS):
                for w, (dst, src) in enumerate(((slice(META, T), ps[:, 4 + a, :]),
                                                (slice(0, META), ps[:, 6, a * P:a * P + META]))):
                    dve.wait_ge(kthi_done, 2 * a + 1 if w == 0 else 2 * PAIRS)
                    dve.tensor_tensor(kt_lo[:, a, dst], src, kt_hi[:, a, dst].bitcast(F32), ALU.subtract)\
                       .then_inc(ktlo_done, 1)

            def q_norms(a):
                dve.wait_ge(qss_ready, PER * (a + 1))
                dve.tensor_scalar(rq[:, 0, :], ps[:, 3, 0:2 * PER * TILES], 1.0 / DH, EPS, ALU.mult, ALU.add)\
                   .then_inc(rq_step, 1)
                newton(None, rq_step, 7 * a + 1, rq_sqrt, a + 1, rq[:, 0, :], rq[:, 1, :], rq[:, 2, :], rq[:, 3, :],
                       rq[:, 4, :])
                dve.wait_ge(rq_step, 7 * a + 6)
                dve.tensor_scalar(rqs[:, a].rearrange("p r i b -> p (r i b)"), rq[:, 4, :], DH ** -0.5, None,
                                  ALU.mult).then_inc(rq_step, 1)
                dve.wait_ge(rq_step, 7 * (a + 1))

            def scores(u):
                a, b, i = units[u]
                w = u % 2
                n = META + P * (1 if i == 0 else 2)
                if u >= 2:
                    dve.wait_ge(pt_ready, u - 1)
                    dve.wait_ge(p_step, 2 * (u - 1))
                for r in range(PER):
                    dve.wait_ge(s_ready, 4 * u + r + 1)
                    dve.tensor_tensor_reduce(out=s_sb[:, w, r, 0:n], in0=ps[:, r % 2, 0:n],
                                             in1=(mask0 if i == 0 else mask)[:, 0:n], scale=1.0, scalar=-3.0e38,
                                             op0=ALU.add, op1=ALU.max, accum_out=smx[:, w, 0, r:r + 1])\
                       .then_inc(s_read, 1)

            def maxima(u):
                a, b, i = units[u]
                w = u % 2
                sink = sinks[:, (2 * a + b) * PER:(2 * a + b + 1) * PER]
                dve.wait_ge(s_read, 4 * (u + 1))
                dve.tensor_tensor(smx[:, w, 1, :], smx[:, w, 0, :], rqs[:, a, :, i, b], ALU.mult).then_inc(m_step, 1)
                dve.wait_ge(m_step, 4 * u + 1)
                dve.tensor_tensor(smx[:, w, 2, :], smx[:, w, 1, :], sink, ALU.max).then_inc(m_step, 1)
                dve.wait_ge(m_step, 4 * u + 2)
                dve.tensor_scalar(smx[:, w, 3, :], smx[:, w, 2, :], -1.0, None, ALU.mult).then_inc(m_step, 1)
                dve.wait_ge(m_step, 4 * u + 3)
                dve.tensor_tensor(smx[:, w, 4, :], smx[:, w, 3, :], sink, ALU.add).then_inc(m_step, 1)

            def normalise(u):
                a, b, i = units[u]
                w = u % 2
                n = META + P * (1 if i == 0 else 2)
                dve.wait_ge(p_exp, 5 * (u + 1))
                dve.tensor_tensor(sden[:, w, :], smx[:, w, 6, :], smx[:, w, 5, :], ALU.add).then_inc(p_step, 1)
                dve.wait_ge(p_step, 2 * u + 1)
                dve.reciprocal(smx[:, w, 7, :], sden[:, w, :]).then_inc(p_step, 1)
                dve.wait_ge(p_step, 2 * u + 2)
                dve.tensor_tensor(s_sb[:, w, :, 0:n], s_sb[:, w, :, 0:n],
                                  smx[:, w, 7, :].unsqueeze(2).broadcast_to([P, PER, n]), ALU.mult)\
                   .then_inc(p_norm, 1)

            before = [0]
            for a, b, i in units:
                before.append(before[-1] + (2 if i == 0 else 3))

            def pt_low(u):
                a, b, i = units[u]
                n = before[u]
                dve.wait_ge(pthi_done, n + 1)
                dve.tensor_tensor(pt_lo[0:META, 0, :], ps[0:META, 6, :], pt_hi[0:META, 0, :].bitcast(F32),
                                  ALU.subtract).then_inc(ptlo_done, 1)
                if i > 0:
                    n += 1
                    dve.wait_ge(pthi_done, n + 1)
                    dve.tensor_tensor(pt_lo[:, 1, :], ps[:, 4, :], pt_hi[:, 1, :].bitcast(F32), ALU.subtract)\
                       .then_inc(ptlo_done, 1)
                dve.wait_ge(pthi_done, n + 2)
                dve.tensor_tensor(pt_lo[:, 2, :], ps[:, 5, :], pt_hi[:, 2, :].bitcast(F32), ALU.subtract)\
                   .then_inc(ptlo_done, 1)

            def o_low(u):
                a, b, i = units[u]
                rowsel = slice(b * DH, (b + 1) * DH)
                hi_, lo_ = ((o_hi, o_lo), (q_hi, q_lo))[a]
                dve.wait_ge(ohi_done, u + 1)
                dve.tensor_tensor(lo_[rowsel, 0:PER, i * P:(i + 1) * P],
                                  ps[rowsel, 7, :].rearrange("p (r n) -> p r n", r=PER),
                                  hi_[rowsel, 0:PER, i * P:(i + 1) * P].bitcast(F32), ALU.subtract)\
                   .then_inc(olo_done, 1)

            q_norms(0)
            scores(0)
            maxima(0)
            for u in range(NU):
                normalise(u)
                if u + 1 < NU:
                    if u + 1 == NU // 2:
                        q_norms(1)
                    scores(u + 1)
                    maxima(u + 1)
                pt_low(u)
                if u < NU // 2 and u % 2 == 0:
                    q_scale(PER + u // 2)
                    q_low(PER + u // 2)
                if u >= 1:
                    o_low(u - 1)
            o_low(NU - 1)

            for m in range(KT):
                dve.wait_ge(used, n_of(Q_O, m) + 1)
                dve.tensor_tensor(h[:, m, META:T], ps[:, slot_bank(O_O + m), :], h[:, m, META:T], ALU.add)\
                   .then_inc(slot_free, 1)
                if m >= 1:
                    prep(R_FFN1, m - 1, "ffn1")
            prep(R_FFN1, KT - 1, "ffn1")
            stats(R_FFN1)
            ffn(1, 0, None, None)
            ffn(1, 1, None, None)

        @block.tensor
        def _(pe):
            pe.wait_ge(consts, 12)
            pe.wait_ge(par_in, 16 * 9)
            pe.transpose(ps[:, 4, 0:NROWS], par_rows[:, :], ident[0:NROWS, 0:NROWS]).then_inc(turned, 1)
            pe.wait_ge(dwr_in, 16)
            for k in range(KT):
                t = pe.transpose(ps[:, 5, 32 * k:32 * k + TAPS], dw_rows[:, k * P:(k + 1) * P],
                                 ident[0:TAPS, 0:TAPS])
            t.then_inc(turned, 1)
            pe.wait_ge(x_in[0], 16)
            for k in range(KT):
                t = pe.transpose(ps[:, 0, META * k:META * (k + 1)], meta_tok[:, k * P:(k + 1) * P],
                                 ident[0:META, 0:META])
            t.then_inc(turned, 1)
            for g in range(2 * TILES):
                i, kh = g // 2, g % 2
                pe.wait_ge(x_in[1 + i], 16)
                if g >= 3:
                    pe.wait_ge(turned_out, 2 + g - 2)
                for k in range(4):
                    col = (4 * kh + k) * P
                    t = pe.transpose(ps[:, (g + 1) % 4, k * P:(k + 1) * P], x_tok[:, i, col:col + P], ident[:, :])
                t.then_inc(turned, 1)
            pe.wait_ge(turned_out, 2 + 1 + 2 * TILES)

            def three(outs, lhs, rhs_hi, rhs_lo, first, last):
                passes = ((lhs[0], rhs_hi), (lhs[0], rhs_lo), (lhs[1], rhs_hi))
                for n, (wt, rhs) in enumerate(passes):
                    for o_, r_ in zip(outs, rhs):
                        mm = pe.matmul(o_, wt, r_, start=first and n == 0, stop=last and n == 2)
                return mm

            def chunk(c, k):
                return w_hi[:, c, k * P:(k + 1) * P], w_lo[:, c, k * P:(k + 1) * P]

            def cols(t, k, wide):
                if wide:
                    return [t[:, k, 0:HALF], t[:, k, HALF:T]]
                return [t[:, k, META:T]]

            def outs(bank, wide):
                return [ps[:, bank, 0:HALF], ps[:, bank + 1, 0:HALF]] if wide else [ps[:, bank, :]]

            def product(qd, c, o_, bank, ins, nk, k0, wide, first, last, ready=None, base=0, colf=None):
                pe.wait_ge(lo_done, n_of(qd, c) + 1)
                if first and not (isinstance(o_, int) and o_ < 2):
                    pe.wait_ge(slot_free, o_ - 1)
                colf = colf or cols
                for k in range(nk):
                    if ready is not None:
                        pe.wait_ge(ready, base + k0 + k + 1)
                    mm = three(outs(bank, wide), chunk(c, k), colf(ins[0], k0 + k, wide), colf(ins[1], k0 + k, wide),
                               first and k == 0, last and k == nk - 1)
                mm.then_inc(used, 1)

            def stats_sum(r):
                pe.wait_ge(acc_added, 8 * (r + 1))
                if r > 0:
                    pe.wait_ge(rb_done, 2 * r)
                for t in range(5):
                    lo_ = 0 if t == 0 else META + (t - 1) * P
                    mm = pe.matmul(ps[:, 6, t:t + 1], acc[:, lo_:lo_ + P], ones[:, 0:1], start=True, stop=True)
                mm.then_inc(st_ready, 1)

            def stats_spread(r):
                pe.wait_ge(diag_done, r + 1)
                pe.matmul(ps[:, 6, P:P + META], ones[:, :], diag[:, 0, 0:META], start=True, stop=True)
                pe.matmul(ps[:, 7, :], ones[:, :], diag[:, 1:5, :].rearrange("p t n -> p (t n)"),
                          start=True, stop=True).then_inc(bc_ready, 1)

            act_in = (act_hi, act_lo)

            def taps(qd, e):
                ct = (qd - Q_IN) * 2 + e
                pe.wait_ge(calo_done, ct + 1)
                pe.wait_ge(dg_done, 2 * ct + 2)
                if not (isinstance(ct, int) and ct == 0):
                    pe.wait_ge(conv_mix, ct)
                e = e % 2
                for w in range(PE_TAPS):
                    at_ = DVE_TAPS + w
                    rng = lambda t: [t[:, e, at_ + HALF * z:at_ + HALF * (z + 1)] for z in range(2)]
                    mm = three(outs(4, True), (dg_hi[:, e, w, :], dg_lo[:, e, w, :]), rng(a_hi), rng(a_lo),
                               w == 0, w == PE_TAPS - 1)
                mm.then_inc(taps_pe, 1)

            def conv_in(qd, first):
                for e in range(2):
                    ct = (qd - Q_IN) * 2 + e
                    prime = first and e == 0
                    product(qd, 2 * e, O_IN + 2 * ct, 0, act_in, KT, 0, True, True, True,
                            alo_done if prime else None, 0)
                    if prime:
                        stats_sum(R_MIX0)
                    else:
                        taps(qd, e - 1)
                    product(qd, 2 * e + 1, O_IN + 2 * ct + 1, 2, act_in, KT, 0, True, True, True)
                    if prime:
                        stats_spread(R_MIX0)
            quad_loop(pe, Q_IN, 4, conv_in)
            taps(Q_IN + 3, 1)
            stats_sum(R_MEAN)
            stats_spread(R_MEAN)
            stats_sum(R_VAR)
            stats_spread(R_VAR)

            for m in range(KT):
                product(Q_CO + m // 4, m % 4, O_CO + m, slot_bank(O_CO + m), (ln_hi, ln_lo), KT, 0, True, True, True,
                        lnlo_done if m == 0 else None, 0)

            def ffn(L, s, round_):
                wide = L == 0

                def gu(qd, first):
                    for e in range(2):
                        fi = (qd - Q_GU[L][s]) * 2 + e
                        prime = first and e == 0 and s == 0
                        product(qd, 2 * e, O_GU[L][s] + 2 * fi, 0, act_in, KT, 0, wide, True, True,
                                alo_done if prime else None, 8 * PREP[round_] if prime else 0)
                        if prime:
                            stats_sum(round_)
                        product(qd, 2 * e + 1, O_GU[L][s] + 2 * fi + 1, 2, act_in, KT, 0, wide, True, True)
                        if prime:
                            stats_spread(round_)
                quad_loop(pe, Q_GU[L][s], FH[s] // 2, gu)
                hid_cols = lambda t, k, w_: [t[:, k, 0:HALF], t[:, k, HALF:T]] if w_ else [t[:, k, 0:SEQ]]

                def turn(qd, e):
                    m = (qd - Q_DN[L][s]) * 2 + e
                    pe.wait_ge(slot_free, O_DN[L][s] + m + 1)
                    e = e % 2
                    if not (isinstance(m, int) and m < 2):
                        pe.wait_ge(out_sb, m - 1)
                    for i in range(TILES):
                        t = pe.transpose(ps[:, 4 + e, i * P:(i + 1) * P], tmp[:, e, i * P:(i + 1) * P], ident[:, :])
                    t.then_inc(outT_ready, 1)

                def dn(qd, first):
                    for e in range(2):
                        m = (qd - Q_DN[L][s]) * 2 + e
                        for part in range(2):
                            product(qd, 2 * e + part, O_DN[L][s] + m, 2 * e, (hid_hi, hid_lo), PARTS[s],
                                    part * PARTS[s], wide, part == 0, part == 1,
                                    hidlo_done if first and e == 0 else None, G0[L][s], hid_cols)
                        if L == 1 and s == 1 and not (first and e == 0):
                            turn(qd, e - 1)
                quad_loop(pe, Q_DN[L][s], KT // 2, dn)
                if L == 1 and s == 1:
                    turn(Q_DN[L][s] + KT // 2 - 1, 1)

            ffn(0, 0, R_FFN0)
            ffn(0, 1, R_FFN0)

            stats_sum(R_MIX1)
            for t in range(1 + TILES):
                if t == 1:
                    stats_spread(R_MIX1)
                pe.wait_ge(kvalo_done, t + 1)
                if t >= 2:
                    pe.wait_ge(kx_done, t - 1)
                for c in range(SLOTS):
                    if t == 0:
                        pe.wait_ge(lo_done, n_of(Q_KV, c) + 1)
                    for kk in range(2):
                        k = 2 * c + kk
                        wh, wl = (w_[:, c, kk * 512:(kk + 1) * 512] for w_ in (w_hi, w_lo))
                        xh, xl = kva_hi[:, t % 2, k, :], kva_lo[:, t % 2, k, :]
                        for n, (l_, r_) in enumerate(((xh, wh), (xh, wl), (xl, wh))):
                            mm = pe.matmul(ps[:, 4 + t % 2, :], l_, r_, start=k == 0 and n == 0,
                                           stop=k == KT - 1 and n == 2)
                    if t == TILES:
                        mm.then_inc(used, 1)
                if t < TILES:
                    mm.then_inc(kv_ready, 1)

            def q_product(j):
                c = j % 4
                pe.wait_ge(lo_done, n_of(Q_Q, j) + 1)
                if j == 0:
                    pe.wait_ge(slot_free, O_O)
                    pe.wait_ge(alo_done, 8 * (PREP[R_MIX1] + 1))
                else:
                    pe.wait_ge(q_out, j)
                for k in range(KT):
                    mm = three([ps[:, 2, :]], chunk(c, k), cols(act_hi, k, False), cols(act_lo, k, False), k == 0,
                               k == KT - 1)
                mm.then_inc(used, 1)

            def q_sums(j):
                pe.wait_ge(qsq_done, j + 1)
                if j == PER:
                    pe.wait_ge(rq_step, 1)
                for i in range(TILES):
                    at_ = ((j % PER) * TILES + i) * 2
                    mm = pe.matmul(ps[:, 3, at_:at_ + 2], tmp[:, 2 + j % 2, i * P:(i + 1) * P], blk2[:, :],
                                   start=True, stop=True)
                mm.then_inc(qss_ready, 1)

            for j in range(PER):
                q_product(j)
                if j >= 1:
                    q_sums(j - 1)
            q_sums(PER - 1)

            pe.wait_ge(k_step, 9)
            for a in range(PAIRS):
                for i in range(TILES):
                    pe.transpose(ps[:, 4 + a, i * P:(i + 1) * P], kx[:, 1 + i, a * P:(a + 1) * P], ident[:, :])
            for a in range(PAIRS):
                t = pe.transpose(ps[:, 6, a * P:(a + 1) * P], kx[:, 0, a * P:(a + 1) * P], ident[:, :])
            t.then_inc(kt_ready, 1)
            pe.wait_ge(ktlo_done, 2 * PAIRS)

            def scores(u):
                a, b, i = units[u]
                half = slice(b * DH, (b + 1) * DH)
                if b == 0 and i == 0:
                    pe.wait_ge(qlo_done, PER * (a + 1))
                n = META + P * (1 if i == 0 else 2)
                parts = [(0, n, 0)] if i < 2 else [(0, META, 0), (META, n, (i - 1) * P)]
                for r in range(PER):
                    if 4 * u + r >= 2:
                        pe.wait_ge(s_read, 4 * u + r - 1)
                    j = a * PER + r
                    for f, t, shift in parts:
                        lhs = [q_[half, j, i * P:(i + 1) * P] for q_ in (q_hi, q_lo)]
                        rhs = [k_[half, a, f + shift:t + shift] for k_ in (kt_hi, kt_lo)]
                        mm = three([ps[:, r % 2, f:t]], lhs, [rhs[0]], [rhs[1]], True, True)
                    mm.then_inc(s_ready, 1)

            def turn_p(u):
                a, b, i = units[u]
                w = u % 2
                pe.wait_ge(p_norm, u + 1)
                if u >= 1:
                    pe.wait_ge(ptlo_done, before_pe[u])
                n = META + P * (1 if i == 0 else 2)
                for r in range(PER):
                    pe.transpose(ps[0:META, 6, r * P:(r + 1) * P], s_sb[:, w, r, 0:META], ident[:, :])
                    if i > 0:
                        pe.transpose(ps[:, 4, r * P:(r + 1) * P], s_sb[:, w, r, META:META + P], ident[:, :])
                    t = pe.transpose(ps[:, 5, r * P:(r + 1) * P], s_sb[:, w, r, n - P:n], ident[:, :])
                t.then_inc(pt_ready, 1)

            before_pe = [0]
            for a, b, i in units:
                before_pe.append(before_pe[-1] + (2 if i == 0 else 3))

            def values(u):
                a, b, i = units[u]
                pe.wait_ge(ptlo_done, before_pe[u + 1])
                if u >= 1:
                    pe.wait_ge(olo_done, u)
                parts = [(slice(0, META), 0, 0)] + ([(slice(0, P), 1, i)] if i > 0 else []) + [(slice(0, P), 2, i + 1)]
                for n, (rr, z, t) in enumerate(parts):
                    lhs = [v_[rr, t, a * P:(a + 1) * P] for v_ in (v_hi, v_lo)]
                    mm = three([ps[:, 7, :]], lhs, [pt_hi[rr, z, :]], [pt_lo[rr, z, :]], n == 0, n == len(parts) - 1)
                mm.then_inc(pv_ready, 1)

            scores(0)
            for u in range(NU):
                if u < NU // 2 and u % 2 == 0:
                    q_product(PER + u // 2)
                if u < NU // 2 and u % 2 == 1:
                    q_sums(PER + u // 2)
                if u + 1 < NU:
                    scores(u + 1)
                if u >= 1:
                    values(u - 1)
                turn_p(u)
            values(NU - 1)

            def o_cols(t, k, wide):
                src = {id(o_hi): (o_hi, q_hi), id(o_lo): (o_lo, q_lo)}[id(t)]
                return [src[k // PER][:, k % PER, :]]
            pe.wait_ge(olo_done, NU)
            for m in range(KT):
                product(Q_O + m // 4, m % 4, O_O + m, slot_bank(O_O + m), (o_hi, o_lo), KT, 0, False, True, True,
                        None, 0, o_cols)

            ffn(1, 0, R_FFN1)
            ffn(1, 1, R_FFN1)


_INS = ["x", "meta_tokens", "norm_mix", "norm_ffn", "conv_w_in", "conv_b_in", "conv_dw", "conv_ln_g", "conv_ln_b",
        "conv_w_out", "conv_b_out", "kv_norm", "w_kv", "k_norm", "w_q", "q_norm", "attn_sinks", "w_o",
        "ffn_w_gate", "ffn_w_up", "ffn_w_down"]


def kernel(**inputs):
    import numpy as np
    import concourse.bacc as bacc
    from concourse.bass_utils import run_bass_kernel_spmd

    nc = bacc.Bacc("TRN2", target_bir_lowering=False, num_devices=1)
    arrays, args = {}, []
    for name in _INS:
        a = np.ascontiguousarray(inputs[name])
        arrays[f"in_{name}"] = a
        args.append(nc.dram_tensor(f"in_{name}", a.shape, mybir.dt.from_np(a.dtype), kind="ExternalInput").ap())
    res = nc.dram_tensor("out_dram", arrays["in_x"].shape, F32, kind="ExternalOutput").ap()
    trunk_kernel(nc, *args, res)
    r = run_bass_kernel_spmd(nc, [arrays], core_ids=[0])
    return r.results[0]["out_dram"]
```

```python
from contextlib import ExitStack

import concourse.bass as bass
from concourse import mybir

F32 = mybir.dt.float32
F32R = mybir.dt.float32r
ACT = mybir.ActivationFunctionType
ALU = mybir.AluOpType
AX_X = mybir.AxisListType.X

P = 128
EPS = 1e-6
NEG = -1e30
SLOTS = 4
WIDE = 1024
PE_TAPS = 10
LAG_HI = 3
LAG_LO = 2


def trunk_kernel(nc, x, meta_tokens, norm_mix, norm_ffn, conv_w_in, conv_b_in, conv_dw, conv_ln_g, conv_ln_b,
                 conv_w_out, conv_b_out, kv_norm, w_kv, k_norm, w_q, q_norm, attn_sinks, w_o,
                 ffn_w_gate, ffn_w_up, ffn_w_down, out):
    _, SEQ, D = x.shape
    META = meta_tokens.shape[0]
    T = META + SEQ
    KT = D // P
    HALF = T // 2
    TILES = SEQ // P
    TAPS = conv_dw.shape[1]
    PAD = TAPS - 1
    DVE_TAPS = TAPS - PE_TAPS
    DH = k_norm.shape[0]
    HEADS = attn_sinks.shape[1]
    GROUPS = w_kv.shape[1] // (2 * DH)
    PER = HEADS // GROUPS
    PAIRS = GROUPS // 2
    KV = GROUPS * DH
    FT = ffn_w_gate.shape[2] // P
    FH = [12, FT - 12]
    PARTS = [6, 5]
    assert (D, T, DH, TILES, GROUPS, PER, FT) == (1024, 528, 64, 4, 4, 4, 22)

    q = 0
    Q_IN = q; q += 2 * KT // SLOTS
    Q_CO = q; q += KT // SLOTS
    Q_GU, Q_DN = [[0, 0], [0, 0]], [[0, 0], [0, 0]]
    for s in range(2):
        Q_GU[0][s] = q; q += 2 * FH[s] // SLOTS
        Q_DN[0][s] = q; q += 2 * KT // SLOTS
    Q_KV = q; q += 1
    Q_Q = q; q += KT // SLOTS
    Q_O = q; q += KT // SLOTS
    for s in range(2):
        Q_GU[1][s] = q; q += 2 * FH[s] // SLOTS
        Q_DN[1][s] = q; q += 2 * KT // SLOTS
    QUADS = q

    o = 0
    O_IN = o; o += 2 * KT
    O_CO = o; o += KT
    O_GU, O_DN = [[0, 0], [0, 0]], [[0, 0], [0, 0]]
    for L in range(2):
        if L == 1:
            O_O = o; o += KT
        for s in range(2):
            O_GU[L][s] = o; o += 2 * FH[s]
            O_DN[L][s] = o; o += KT

    G0 = [[0, FH[0]], [FT, FT + FH[0]]]

    R_MIX0, R_MEAN, R_VAR, R_FFN0, R_MIX1, R_FFN1 = range(6)
    STEPS = [6, 1, 6, 6, 6, 6]
    PREP = {R_MIX0: 0, R_FFN0: 1, R_MIX1: 2, R_FFN1: 3}
    SQ0 = {R_MIX0: 0, R_VAR: 1, R_FFN0: 2, R_MIX1: 3, R_FFN1: 4}

    rows = {}
    at = 0
    for name, n in (("mix0", KT), ("mix1", KT), ("ffn0", KT), ("ffn1", KT), ("b_in", 2 * KT), ("ln_g", KT),
                    ("ln_b", KT), ("b_out", KT), ("kv", KT)):
        rows[name] = at
        at += n
    NROWS = at
    units = [(a, b, i) for a in range(PAIRS) for b in range(2) for i in range(TILES)]
    NU = len(units)
    S_BANKS = [0, 1, 3]
    KEYS = 4 * P + 2 * META
    TILE_AT = [0, P + META, 2 * P + META, 3 * P + 2 * META]
    META_AT = [P, 3 * P + META]
    WINDOW_AT = [0, 0, P, 2 * P + META]
    ORDER = [(None, 0, P), (0, P + META, P), (META, META + P, 0), (0, P + META, P)]
    CONSTS = 13
    QJ = PAIRS * PER

    ctx = ExitStack()
    with ctx:
        def sb(name, shape, dt, where=ctx):
            return where.enter_context(nc.sbuf_tensor(name, shape, dt))

        def sem(name):
            return ctx.enter_context(nc.semaphore(name))

        h = sb("h", [P, KT, T], F32)
        act_hi = sb("act_hi", [P, KT, T], F32R)
        act_lo = sb("act_lo", [P, KT, T], F32R)
        raw = sb("raw", [P, SLOTS, WIDE], F32)
        w_hi = sb("w_hi", [P, SLOTS, WIDE], F32R)
        w_lo = sb("w_lo", [P, SLOTS, WIDE], F32R)
        tmp = sb("tmp", [P, 4, T], F32)
        sq = sb("sq", [P, 2, T], F32)
        acc = sb("acc", [P, T], F32)
        rb = sb("rb", [P, T], F32)
        ident = sb("ident", [P, P], F32)
        ones = sb("ones", [P, P], F32)
        blk2 = sb("blk2", [P, 2], F32)
        mask_a = sb("mask_a", [P, 2 * P + 2 * META], F32)
        mask_b = sb("mask_b", [P, META + 2 * P], F32)
        par = sb("par", [P, NROWS], F32)
        sinks = sb("sinks", [P, HEADS], F32)
        gk = sb("gk", [P, DH], F32)
        gq = sb("gq", [P, DH], F32)
        gqk = sb("gqk", [P, DH], F32)
        st = sb("st", [P, 5, 5], F32)
        diag = tmp[:, 2:4, :].rearrange("p a t -> p (a t)")[:, 0:5 * P].rearrange("p (t n) -> p t n", t=5)

        rk = sb("rk", [P, 5, (1 + TILES) * GROUPS], F32)
        rq = sb("rq", [P, 5, 2 * PER * TILES], F32)
        rqs = sb("rqs", [P, PAIRS, PER, TILES, 2], F32)
        smx = sb("smx", [P, 3, 8, PER], F32)
        sden = sb("sden", [P, 3, PER], F32)
        qss = sb("qss", [P, 2 * PER * TILES], F32)

        with ExitStack() as region:
            conv = sb("conv", [P, KT, T], F32, region)
            dw = sb("dw", [P, KT, 32], F32, region)
            dw_hi = sb("dw_hi", [P, KT, 32], F32R, region)
            dw_lo = sb("dw_lo", [P, KT, 32], F32R, region)
            apad = sb("apad", [P, PAD + T], F32, region)
            with ExitStack() as early:
                x_tok = sb("x_tok", [P, TILES, D], F32, early)
                meta_tok = sb("meta_tok", [META, D], F32, early)
                par_rows = sb("par_rows", [NROWS, P], F32, early)
                dw_rows = sb("dw_rows", [TAPS, D], F32, early)
            with ExitStack() as early:
                a_hi = sb("a_hi", [P, 2, PAD + T], F32R, early)
                a_lo = sb("a_lo", [P, 2, PAD + T], F32R, early)
                ca = sb("ca", [P, T], F32, early)
                cb = sb("cb", [P, T], F32, early)
                dg_hi = sb("dg_hi", [P, 2, PE_TAPS, P], F32R, early)
                dg_lo = sb("dg_lo", [P, 2, PE_TAPS, P], F32R, early)
            ln_hi = sb("ln_hi", [P, KT, T], F32R, region)
            ln_lo = sb("ln_lo", [P, KT, T], F32R, region)
        with ExitStack() as region:
            hid_hi = sb("hid_hi", [P, FH[0], T], F32R, region)
            hid_lo = sb("hid_lo", [P, FH[0], T], F32R, region)
        with ExitStack() as region:
            q1 = sb("q1", [P, PER, SEQ], F32, region)
            kt = sb("kt", [P, PAIRS, KEYS], F32, region)
            v_hi = sb("v_hi", [P, 1 + TILES, KV], F32R, region)
            v_lo = sb("v_lo", [P, 1 + TILES, KV], F32R, region)
            v_meta = sb("v_meta", [P, KV], F32, region)
            with ExitStack() as early:
                q0 = sb("q0", [P, PER, SEQ], F32, early)
            o1_lo = sb("o1_lo", [P, PER, SEQ], F32R, region)
            with ExitStack() as early:
                kx = sb("kx", [P, 1 + TILES, KV], F32, early)
                kva_hi = sb("kva_hi", [P, 2, KT, P], F32R, early)
                kva_lo = sb("kva_lo", [P, 2, KT, P], F32R, early)
                kva = sb("kva", [P, 2, KT, P], F32, early)
            s_sb = sb("s_sb", [P, 3, PER, META + 2 * P], F32, region)
            pt_hi = sb("pt_hi", [P, 2, 2, PER * P], F32R, region)
            pt_lo = sb("pt_lo", [P, 2, 2, PER * P], F32R, region)
            o0_hi = sb("o0_hi", [P, PER, SEQ], F32R, region)
            o0_lo = sb("o0_lo", [P, PER, SEQ], F32R, region)
            o1_hi = sb("o1_hi", [P, PER, SEQ], F32R, region)

        ps = ctx.enter_context(nc.psum_tensor("ps", [P, 8, 512], F32))

        par_in, sink_in, dwr_in = sem("par_in"), sem("sink_in"), sem("dwr_in")
        x_in = [sem(f"x_in{i}") for i in range(1 + TILES)]
        landed = [sem(f"landed{c}") for c in range(SLOTS)]
        landed2 = [sem(f"landed_second_half{c}") for c in range(SLOTS)]
        hi_done, lo_done, used = sem("w_hi_done"), sem("w_lo_done"), sem("w_used")
        consts, zeroed = sem("consts"), sem("acc_zeroed")
        turned, turned_out = sem("turned"), sem("turned_out")
        dw_split = sem("dw_split")
        sq_done, acc_added = sem("sq_done"), sem("acc_added")
        ahi_done, alo_done = sem("act_hi_done"), sem("act_lo_done")
        st_ready, st_step, st_sqrt = sem("st_ready"), sem("st_step"), sem("st_sqrt")
        diag_done, bc_ready, rb_done = sem("diag_done"), sem("bc_ready"), sem("rb_done")
        slot_free = sem("slot_free")
        sig_done, a_done, cahi_done, calo_done = sem("sig_done"), sem("a_done"), sem("conv_a_hi"), sem("conv_a_lo")
        tap_done, taps_pe, conv_mix, c_done = sem("tap_done"), sem("taps_pe"), sem("conv_mix"), sem("c_done")
        dg_done = sem("dg_done")
        cc_done, ln_mul, ln_silu, lnhi_done, lnlo_done = (sem("cc_done"), sem("ln_mul"), sem("ln_silu"),
                                                         sem("ln_hi_done"), sem("ln_lo_done"))
        silu_done, p_done, hidhi_done, hidlo_done = (sem("silu_done"), sem("hid_product"), sem("hid_hi_done"),
                                                     sem("hid_lo_done"))
        kva_done, kvahi_done, kvalo_done, kv_ready = sem("kva_done"), sem("kva_hi"), sem("kva_lo"), sem("kv_ready")
        vhi_done, kx_done, ksq_done, k_step, k_sqrt = (sem("v_hi_done"), sem("kx_done"), sem("ksq_done"),
                                                      sem("k_step"), sem("k_sqrt"))
        kt_ready, kt_done = sem("kt_ready"), sem("kt_done")
        q_out, qsq_done, qss_ready, qss_read = sem("q_out"), sem("qsq_done"), sem("q_sums"), sem("q_sums_read")
        rq_step, rq_sqrt = sem("rq_step"), sem("rq_sqrt")
        s_ready, s_read, m_step, p_exp, p_step, p_norm = (sem("s_ready"), sem("s_read"), sem("m_step"), sem("p_exp"),
                                                         sem("p_step"), sem("p_norm"))
        pt_ready, ptm_done, pthi_done, ptlo_done, pv_ready = (sem("pt_ready"), sem("pt_meta_done"), sem("pt_hi_done"),
                                                             sem("pt_lo_done"), sem("pv_ready"))
        ohi_done, olo_done = sem("o_hi_done"), sem("o_lo_done")
        outT_ready, out_sb, out_sent = sem("out_turned"), sem("out_copied"), [sem("out_sent0"), sem("out_sent1")]

        v_low, gqk_done = sem("v_low_done"), sem("gqk_done")
        tmp2k = tmp[:, :, :].rearrange("p a t -> p (a t)")[:, 0:(1 + TILES) * KV]

        block = ctx.enter_context(nc.Block())

        def n_of(qd, c):
            return qd * SLOTS + c

        def slot_bank(o):
            return 2 * (o % 2)

        def pair_view(bank, cols=None):
            return ps[:, bank:bank + 2, 0:HALF]

        def two(ap):
            return ap.rearrange("p (b n) -> p b n", b=2)

        def quad_loop(eng, start, count, body):
            body(start, True)
            if count > 1:
                with eng.Fori(start + 1, start + count) as qd:
                    body(qd, False)

        blocks_before = [0]
        for _, _, i_ in units:
            blocks_before.append(blocks_before[-1] + (1 if i_ == 0 else 2))

        def keys_of(i):
            return META + (P if i == 0 else 2 * P)

        def q_of(a):
            return (q0, q1)[a]

        def steps_before(r):
            return sum(STEPS[:r])

        def sqrts_before(r):
            return sum(1 for s in STEPS[:r] if s > 1)

        @block.sync
        def _(sp):
            sp.dma_start(meta_tok[:, :], meta_tokens).then_inc(x_in[0], 16)
            for i in range(TILES):
                sp.dma_start(x_tok[:, i, :], x[0, i * P:(i + 1) * P, :]).then_inc(x_in[1 + i], 16)

            def col_of(i):
                return i * P if isinstance(i, int) else sp.snap(i * P)

            def load(qd, c, src, k):
                if not (isinstance(qd, int) and qd == 0):
                    sp.wait_ge(lo_done, n_of(qd, c) - SLOTS + 1)
                sp.dma_start(raw[:, c, 0:k * P].rearrange("p (k n) -> p k n", k=k), src).then_inc(landed[c], 16)

            w_in = conv_w_in[0].rearrange("(k p) n -> p k n", p=P)

            def conv_in(qd, first):
                for c in range(SLOTS):
                    ct = (qd - Q_IN) * 2 + c // 2
                    col = col_of(ct + (KT if c % 2 == 0 else 0))
                    load(qd, c, w_in[:, :, bass.ds(col, P)], KT)
            quad_loop(sp, Q_IN, 4, conv_in)

            w_out = conv_w_out[0].rearrange("(k p) n -> p k n", p=P)
            for m in range(KT):
                load(Q_CO + m // 4, m % 4, w_out[:, :, m * P:(m + 1) * P], KT)

            def ffn(L, s):
                gate = ffn_w_gate[L].rearrange("(k p) n -> p k n", p=P)
                up = ffn_w_up[L].rearrange("(k p) n -> p k n", p=P)
                down = ffn_w_down[L].rearrange("(k p) n -> p k n", p=P)
                f0 = s * FH[0]

                def gu(qd, first):
                    for c in range(SLOTS):
                        col = col_of((qd - Q_GU[L][s]) * 2 + c // 2 + f0)
                        load(qd, c, (gate if c % 2 == 0 else up)[:, :, bass.ds(col, P)], KT)

                def dn(qd, first):
                    for c in range(SLOTS):
                        col = col_of((qd - Q_DN[L][s]) * 2 + c // 2)
                        k0 = f0 + (c % 2) * PARTS[s]
                        load(qd, c, down[:, k0:k0 + PARTS[s], bass.ds(col, P)], PARTS[s])
                quad_loop(sp, Q_GU[L][s], FH[s] // 2, gu)
                quad_loop(sp, Q_DN[L][s], KT // 2, dn)

            ffn(0, 0)
            ffn(0, 1)

            w_kv_v = w_kv.rearrange("(k p) n -> p k n", p=P)
            for c in range(SLOTS):
                sp.wait_ge(lo_done, n_of(Q_KV, c) - SLOTS + 1)
                sp.dma_start(raw[:, c, :].rearrange("p (k n) -> p k n", k=2), w_kv_v[:, 2 * c:2 * c + 2, :])\
                  .then_inc(landed[c], 16)

            w_q_v = w_q[0].rearrange("(k p) (g r d) -> g r p k d", p=P, g=GROUPS, r=PER)
            for j in range(QJ):
                c = j % 4
                sp.wait_ge(lo_done, n_of(Q_Q + j // 4, c) - SLOTS + 1)
                dst = raw[:, c, :].rearrange("p (k n) -> p k n", k=KT)
                for b in range(2):
                    sp.dma_start(dst[:, :, b * DH:(b + 1) * DH], w_q_v[2 * (j // PER) + b, j % PER])\
                      .then_inc((landed, landed2)[b][c], 16)

            w_o_v = w_o[0].rearrange("(a b r d) n -> b a d r n", a=PAIRS, b=2, r=PER)
            for m in range(KT):
                c = m % 4
                sp.wait_ge(lo_done, n_of(Q_O + m // 4, c) - SLOTS + 1)
                for b in range(2):
                    for a in range(PAIRS):
                        dst = raw[b * DH:(b + 1) * DH, c, a * PER * P:(a + 1) * PER * P]
                        sp.dma_start(dst.rearrange("p (r n) -> p r n", r=PER), w_o_v[b, a, :, :, m * P:(m + 1) * P])\
                          .then_inc((landed if a == b == 0 else landed2)[c], 16)

            ffn(1, 0)
            ffn(1, 1)

        @block.scalar
        def _(act):
            for name, src in (("mix0", norm_mix[0]), ("mix1", norm_mix[1]), ("ffn0", norm_ffn[0]),
                              ("ffn1", norm_ffn[1]), ("b_in", conv_b_in[0]), ("ln_g", conv_ln_g[0]),
                              ("ln_b", conv_ln_b[0]), ("b_out", conv_b_out[0]), ("kv", kv_norm)):
                v = src.rearrange("(k p) -> k p", p=P)
                act.dma_start(par_rows[rows[name]:rows[name] + v.shape[0], :], v).then_inc(par_in, 16)
            act.dma_start(dw_rows[:, :], conv_dw[0]).then_inc(dwr_in, 16)
            for dst, src in ((gk, k_norm), (gq, q_norm[0]), (sinks, attn_sinks[0])):
                n = src.shape[0]
                act.dma_start(dst[:, :], src.rearrange("(a n) -> a n", a=1).broadcast_to([P, n]))\
                   .then_inc(sink_in, 16)

            def hi(qd, c):
                qd, c = (qd + c // SLOTS, c % SLOTS)
                static = isinstance(qd, int)
                if static and qd >= QUADS:
                    return
                act.wait_ge(landed[c], 16 * (qd + 1))
                if static and Q_Q <= qd < Q_Q + 2:
                    act.wait_ge(landed2[c], 16 * (qd - Q_Q + 1))
                if static and Q_O <= qd < Q_O + 2:
                    act.wait_ge(landed2[c], 16 * (2 + 3 * (qd - Q_O + 1)))
                if not (static and qd == 0):
                    act.wait_ge(used, n_of(qd, c) - SLOTS + 1)
                act.activation(w_hi[:, c, :], raw[:, c, :], ACT.Copy).then_inc(hi_done, 1)

            def square(r, k, src, ready, count):
                act.wait_ge(ready, count)
                if not (isinstance(k, int) and k < 2):
                    act.wait_ge(acc_added, 8 * r + k - 1)
                return act.activation(sq[:, k_par[0], :], src, ACT.Square).then_inc(sq_done, 1)

            k_par = [0]

            def prep(r, k, gain, ready, count):
                k_par[0] = k % 2
                square(r, k, h[:, k, :], ready, count)
                act.activation(act_hi[:, k, :], h[:, k, :], ACT.Copy,
                               scale=par[:, rows[gain] + k:rows[gain] + k + 1]).then_inc(ahi_done, 1)

            def stat_sqrt(r):
                act.wait_ge(st_step, steps_before(r) + 1)
                act.activation(st[:, 1, :], st[:, 0, :], ACT.Sqrt).then_inc(st_sqrt, 1)

            for c in range(LAG_HI):
                hi(0, c)
            act.wait_ge(turned_out, 2)
            act.activation(dw_hi[:, :, 0:TAPS], dw[:, :, 0:TAPS], ACT.Copy).then_inc(dw_split, 1)
            act.wait_ge(turned_out, 2 + 1 + 2 * TILES)
            for k in range(KT):
                act.activation(act_hi[:, k, :], h[:, k, :], ACT.Copy,
                               scale=par[:, rows["mix0"] + k:rows["mix0"] + k + 1]).then_inc(ahi_done, 1)
            for k in range(KT):
                k_par[0] = k % 2
                square(R_MIX0, k, h[:, k, :], turned_out, 2 + 1 + 2 * TILES)
            stat_sqrt(R_MIX0)

            def conv_in(qd, first):
                for e in range(2):
                    ct = (qd - Q_IN) * 2 + e
                    hi(qd, 2 * e + LAG_HI)
                    act.wait_ge(slot_free, O_IN + 2 * ct + 1)
                    if not (first and e == 0):
                        act.wait_ge(a_done, ct)
                    act.activation(tmp[:, 1, :], tmp[:, 0, :], ACT.Sigmoid,
                                   bias=par[:, bass.ds(rows["b_in"] + KT + ct, 1)]).then_inc(sig_done, 1)
                    hi(qd, 2 * e + 1 + LAG_HI)
                    act.wait_ge(a_done, ct + 1)
                    if not first:
                        act.wait_ge(taps_pe, ct - 1)
                    act.activation(a_hi[:, e, :], apad[:, :], ACT.Copy).then_inc(cahi_done, 1)
            quad_loop(act, Q_IN, 4, conv_in)

            for k in range(KT):
                k_par[0] = k % 2
                square(R_VAR, k, conv[:, k, :], cc_done, k + 1)
            stat_sqrt(R_VAR)
            for k in range(KT):
                act.wait_ge(ln_mul, k + 1)
                if k >= 2:
                    act.wait_ge(lnlo_done, k - 1)
                act.activation(tmp[:, k % 2, :], conv[:, k, :], ACT.Silu,
                               scale=par[:, rows["ln_g"] + k:rows["ln_g"] + k + 1],
                               bias=par[:, rows["ln_b"] + k:rows["ln_b"] + k + 1]).then_inc(ln_silu, 1)
                act.wait_ge(ln_silu, k + 1)
                act.activation(ln_hi[:, k, :], tmp[:, k % 2, :], ACT.Copy).then_inc(lnhi_done, 1)

            for m in range(KT):
                hi(Q_CO, m + LAG_HI)
                prep(R_FFN0, m, "ffn0", slot_free, O_CO + m + 1)
            stat_sqrt(R_FFN0)

            def ffn(L, s, gain, round_):
                N = T if L == 0 else SEQ

                def hid_hi_of(qd, e):
                    fi = (qd - Q_GU[L][s]) * 2 + e
                    g = G0[L][s] + fi
                    act.wait_ge(p_done, g + 1)
                    act.activation(hid_hi[:, bass.ds(fi, 1), 0:N], tmp[:, 3:4, 0:N], ACT.Copy)\
                       .then_inc(hidhi_done, 1)

                def gu(qd, first):
                    for e in range(2):
                        fi = (qd - Q_GU[L][s]) * 2 + e
                        g = G0[L][s] + fi
                        hi(qd, 2 * e + LAG_HI)
                        act.wait_ge(slot_free, O_GU[L][s] + 2 * fi + 1)
                        if not (isinstance(g, int) and g == 0):
                            act.wait_ge(p_done, g)
                        act.activation(tmp[:, 1, 0:N], tmp[:, 0, 0:N], ACT.Silu).then_inc(silu_done, 1)
                        hi(qd, 2 * e + 1 + LAG_HI)
                        if not (first and e == 0):
                            hid_hi_of(qd, e - 1)
                quad_loop(act, Q_GU[L][s], FH[s] // 2, gu)
                hid_hi_of(Q_GU[L][s] + FH[s] // 2 - 1, 1)

                def dn(qd, first):
                    for e in range(2):
                        m = (qd - Q_DN[L][s]) * 2 + e
                        hi(qd, 2 * e + LAG_HI)
                        hi(qd, 2 * e + 1 + LAG_HI)
                        if s == 1 and L == 0:
                            act.wait_ge(slot_free, O_DN[L][s] + m + 1)
                            if not (first):
                                act.wait_ge(acc_added, 8 * round_ + m - 1)
                            act.activation(sq[:, e, :], h[:, bass.ds(m, 1), :].rearrange("p a t -> p (a t)"),
                                           ACT.Square).then_inc(sq_done, 1)
                            act.activation(act_hi[:, bass.ds(m, 1), :], h[:, bass.ds(m, 1), :], ACT.Copy,
                                           scale=par[:, bass.ds(rows[gain] + m, 1)]).then_inc(ahi_done, 1)
                        if s == 1 and L == 1 and not (first and e == 0):
                            send(qd, e - 1, first)

                def send(qd, e, first):
                    m = (qd - Q_DN[L][s]) * 2 + e
                    z = e % 2
                    act.wait_ge(outT_ready, m + 1)
                    if not (isinstance(m, int) and m < 2):
                        act.wait_ge(out_sent[z], 16 * (m // 2))
                    act.activation(tmp[:, 2 + z, 0:SEQ], ps[:, 4 + z, :], ACT.Copy).then_inc(out_sb, 1)
                    act.wait_ge(out_sb, m + 1)
                    act.dma_start(out[0].rearrange("(i p) d -> p i d", p=P)[:, :, bass.ds(m * P, P)],
                                  tmp[:, 2 + z, 0:SEQ].rearrange("p (i n) -> p i n", i=TILES))\
                       .then_inc(out_sent[z], 16)

                if L == 1 and s == 1:
                    for qd in range(Q_DN[L][s], Q_DN[L][s] + KT // 2):
                        dn(qd, qd == Q_DN[L][s])
                    send(Q_DN[L][s] + KT // 2 - 1, 1, False)
                else:
                    quad_loop(act, Q_DN[L][s], KT // 2, dn)

            ffn(0, 0, None, None)
            ffn(0, 1, "mix1", R_MIX1)

            hi(Q_KV, LAG_HI)
            for t in range(1 + TILES):
                act.wait_ge(kva_done, t + 1)
                if t >= 2:
                    act.wait_ge(kv_ready, t - 1)
                act.activation(kva_hi[:, t % 2], kva[:, t % 2], ACT.Copy).then_inc(kvahi_done, 1)
                if t == 0:
                    stat_sqrt(R_MIX1)
                else:
                    act.wait_ge(kv_ready, t)
                    if t == 1:
                        act.wait_ge(st_step, steps_before(R_MIX1) + STEPS[R_MIX1])
                    act.activation(v_hi[:, t - 1, :], ps[:, 4 + (t - 1) % 2, KV:2 * KV], ACT.Copy,
                                   scale=st[:, 4, t - 1:t]).then_inc(vhi_done, 1)
            act.wait_ge(used, n_of(Q_KV, SLOTS))
            act.activation(v_hi[:, TILES, :], ps[:, 4 + TILES % 2, KV:2 * KV], ACT.Copy,
                           scale=st[:, 4, TILES:TILES + 1]).then_inc(vhi_done, 1)
            for c in range(LAG_HI):
                hi(Q_Q, c)
            act.wait_ge(kx_done, 1 + TILES)
            act.activation(tmp2k, kx[:, :, :].rearrange("p t n -> p (t n)"), ACT.Square).then_inc(ksq_done, 1)
            act.wait_ge(k_step, 2)
            act.activation(rk[:, 1, :], rk[:, 0, :], ACT.Sqrt).then_inc(k_sqrt, 1)

            def q_tile(j):
                hi(Q_Q, j + LAG_HI)
                act.wait_ge(q_out, j + 1)
                if j == 0:
                    act.wait_ge(k_step, 1)
                if j >= 2:
                    act.wait_ge(qss_ready, j - 1)
                act.activation(tmp[:, 2 + j % 2, 0:SEQ], q_of(j // PER)[:, j % PER, :], ACT.Square)\
                   .then_inc(qsq_done, 1)

            def q_sqrt(a):
                act.wait_ge(rq_step, 7 * a + 1)
                act.activation(rq[:, 1, :], rq[:, 0, :], ACT.Sqrt).then_inc(rq_sqrt, 1)

            def exps(u):
                a, b, i = units[u]
                n, w = keys_of(i), u % 3
                act.wait_ge(m_step, 4 * (u + 1))
                for r in range(PER):
                    act.activation(s_sb[:, w, r, 0:n], s_sb[:, w, r, 0:n], ACT.Exp, bias=smx[:, w, 3, r:r + 1],
                                   scale=rqs[:, a, r, i, b:b + 1], accum_out=smx[:, w, 6, r:r + 1]).then_inc(p_exp, 1)
                act.activation(smx[:, w, 5, :], smx[:, w, 4, :], ACT.Exp).then_inc(p_exp, 1)

            def pt_high(u):
                a, b, i = units[u]
                act.wait_ge(pt_ready, u + 1)
                if u >= 2:
                    act.wait_ge(pv_ready, u - 1)
                act.activation(pt_hi[:, u % 2, 1, :], ps[:, 5, :], ACT.Copy).then_inc(pthi_done, 1)
                if i > 0:
                    act.activation(pt_hi[:, u % 2, 0, :], ps[:, 4, :], ACT.Copy).then_inc(pthi_done, 1)
                act.activation(sq[0:META, u % 2, 0:PER * P], ps[0:META, 6, :], ACT.Copy).then_inc(ptm_done, 1)

            def o_high(u):
                a, b, i = units[u]
                rowsel = slice(b * DH, (b + 1) * DH)
                act.wait_ge(pv_ready, u + 1)
                act.activation((o0_hi, o1_hi)[a][rowsel, :, i * P:(i + 1) * P],
                               ps[rowsel, 7, :].rearrange("p (r n) -> p r n", r=PER), ACT.Copy).then_inc(ohi_done, 1)

            for j in range(PER):
                q_tile(j)
            q_sqrt(0)
            exps(0)
            exps(1)
            for u in range(NU):
                pt_high(u)
                if u + 2 == NU // 2:
                    q_tile(QJ - 1)
                    q_sqrt(1)
                if u + 2 < NU:
                    exps(u + 2)
                if u >= 1:
                    o_high(u - 1)
                if u < NU // 2 - 2 and u % 2 == 0:
                    q_tile(PER + u // 2)
            o_high(NU - 1)

            for m in range(KT):
                hi(Q_O, m + LAG_HI)
                prep(R_FFN1, m, "ffn1", slot_free, O_O + m + 1)
            stat_sqrt(R_FFN1)
            ffn(1, 0, None, None)
            ffn(1, 1, None, None)
            for e in range(2):
                act.wait_ge(out_sent[e], 16 * (KT // 2))

        @block.gpsimd
        def _(pool):
            pool.memset(ident[:, :], 0.0).then_inc(consts, 1)
            pool.memset(ones[:, :], 1.0).then_inc(consts, 1)
            pool.memset(blk2[:, :], 1.0).then_inc(consts, 1)
            pool.memset(mask_a[:, :], 0.0).then_inc(consts, 1)
            pool.memset(mask_b[:, :], 0.0).then_inc(consts, 1)
            pool.memset(apad[:, 0:PAD], 0.0).then_inc(consts, 1)
            pool.wait_ge(consts, 6)
            pool.affine_select(out=ident[:, :], in_=ident[:, :], compare_op=ALU.not_equal, fill=1.0, base=0,
                               pattern=[[-1, P]], channel_multiplier=1).then_inc(consts, 1)
            pool.affine_select(out=blk2[:, :], in_=blk2[:, :], compare_op=ALU.is_ge, fill=0.0, base=0,
                               pattern=[[-DH, 2]], channel_multiplier=1).then_inc(consts, 1)
            pool.wait_ge(consts, 8)
            pool.affine_select(out=blk2[:, :], in_=blk2[:, :], compare_op=ALU.is_ge, fill=0.0, base=DH - 1,
                               pattern=[[DH, 2]], channel_multiplier=-1).then_inc(consts, 1)
            for m_, at_ in ((mask_a, 0), (mask_b, META)):
                pool.affine_select(out=m_[:, at_:at_ + P], in_=m_[:, at_:at_ + P], compare_op=ALU.is_ge, fill=NEG,
                                   base=-1, pattern=[[1, P]], channel_multiplier=-1).then_inc(consts, 1)
            for m_, at_ in ((mask_a, P + META), (mask_b, META + P)):
                pool.affine_select(out=m_[:, at_:at_ + P], in_=m_[:, at_:at_ + P], compare_op=ALU.is_ge, fill=NEG,
                                   base=0, pattern=[[-1, P]], channel_multiplier=1).then_inc(consts, 1)

            def lo(qd, c):
                qd, c = (qd + c // SLOTS, c % SLOTS)
                if isinstance(qd, int) and qd >= QUADS:
                    return
                pool.wait_ge(hi_done, n_of(qd, c) + 1)
                pool.tensor_tensor(w_lo[:, c, :], raw[:, c, :], w_hi[:, c, :].bitcast(F32), ALU.subtract)\
                    .then_inc(lo_done, 1)

            def zero(r):
                if r > 0:
                    pool.wait_ge(st_ready, r)
                pool.memset(acc[:, :], 0.0).then_inc(zeroed, 1)

            def add(r, k, src, ready, count):
                pool.wait_ge(ready, count)
                if isinstance(k, int) and k == 0:
                    pool.wait_ge(zeroed, r + 1)
                else:
                    pool.wait_ge(acc_added, 8 * r + k)
                pool.tensor_tensor(acc[:, :], acc[:, :], src, ALU.add).then_inc(acc_added, 1)

            def add_square(r, k):
                add(r, k, sq[:, k % 2, :], sq_done, 8 * SQ0[r] + k + 1)

            zero(R_MIX0)
            for c in range(LAG_LO):
                lo(0, c)
            for k in range(KT):
                add_square(R_MIX0, k)
            zero(R_MEAN)

            def conv_in(qd, first):
                for e in range(2):
                    ct = (qd - Q_IN) * 2 + e
                    if first and e == 0:
                        pool.wait_ge(dw_split, 2)
                    if not first:
                        pool.wait_ge(taps_pe, ct - 1)
                    for dst, src in ((dg_hi, dw_hi), (dg_lo, dw_lo)):
                        w = src[:, bass.ds(ct, 1), DVE_TAPS:TAPS].bitcast(F32).rearrange("p a w -> p (a w)")
                        pool.tensor_tensor(dst[:, e], ident[:, :].unsqueeze(1).broadcast_to([P, PE_TAPS, P]),
                                           w.unsqueeze(2).broadcast_to([P, PE_TAPS, P]), ALU.mult)\
                            .then_inc(dg_done, 1)
                        lo(qd, 2 * e + (dst is dg_lo) + LAG_LO)
                    if not (first and e == 0):
                        add(R_MEAN, ct - 1, conv[:, bass.ds(ct - 1, 1), :].rearrange("p a t -> p (a t)"), c_done, ct)
            quad_loop(pool, Q_IN, 4, conv_in)
            add(R_MEAN, KT - 1, conv[:, KT - 1, :], c_done, KT)
            zero(R_VAR)
            for k in range(KT):
                add_square(R_VAR, k)
            zero(R_FFN0)
            for m in range(KT):
                lo(Q_CO, m + LAG_LO)
                add_square(R_FFN0, m)
            zero(R_MIX1)

            def ffn(L, s, round_):
                N = T if L == 0 else SEQ

                def gu(qd, first):
                    for e in range(2):
                        fi = (qd - Q_GU[L][s]) * 2 + e
                        g = G0[L][s] + fi
                        lo(qd, 2 * e + LAG_LO)
                        lo(qd, 2 * e + 1 + LAG_LO)
                        pool.wait_ge(silu_done, g + 1)
                        pool.wait_ge(slot_free, O_GU[L][s] + 2 * fi + 2)
                        if not (isinstance(g, int) and g == 0):
                            pool.wait_ge(hidlo_done, g)
                        pool.tensor_tensor(tmp[:, 3, 0:N], tmp[:, 1, 0:N], tmp[:, 2, 0:N], ALU.mult)\
                            .then_inc(p_done, 1)
                quad_loop(pool, Q_GU[L][s], FH[s] // 2, gu)

                def dn(qd, first):
                    for e in range(2):
                        m = (qd - Q_DN[L][s]) * 2 + e
                        lo(qd, 2 * e + LAG_LO)
                        lo(qd, 2 * e + 1 + LAG_LO)
                        if L == 0 and s == 1:
                            add(round_, m, sq[:, e, :], sq_done, 8 * SQ0[round_] + m + 1)
                if L == 1 and s == 1:
                    dn(Q_DN[L][s], True)
                    with pool.Fori(Q_DN[L][s] + 1, Q_DN[L][s] + KT // 2 - 1) as qd:
                        dn(qd, False)
                    dn(Q_DN[L][s] + KT // 2 - 1, False)
                else:
                    quad_loop(pool, Q_DN[L][s], KT // 2, dn)

            ffn(0, 0, None)
            ffn(0, 1, R_MIX1)
            zero(R_FFN1)
            for c in range(LAG_LO, SLOTS):
                lo(Q_KV, c)
            for j in range(PER + LAG_LO):
                lo(Q_Q, j)
            for u in range(NU):
                a, b, i = units[u]
                n, w = keys_of(i), u % 3
                if u % 2 == 0 and u < NU // 2:
                    lo(Q_Q, PER + LAG_LO + u // 2)
                pool.wait_ge(p_step, 2 * (u + 1))
                pool.tensor_tensor(s_sb[:, w, :, 0:n], s_sb[:, w, :, 0:n],
                                   smx[:, w, 7, :].unsqueeze(2).broadcast_to([P, PER, n]), ALU.mult)\
                    .then_inc(p_norm, 1)
            for m in range(KT):
                lo(Q_O, m + LAG_LO)
                add_square(R_FFN1, m)
            ffn(1, 0, None)
            ffn(1, 1, None)

        @block.vector
        def _(dve):
            dve.wait_ge(turned, 1)
            dve.tensor_copy(par[:, :], ps[:, 4, 0:NROWS]).then_inc(turned_out, 1)
            dve.wait_ge(turned, 2)
            dve.tensor_copy(dw[:, :, 0:TAPS], ps[:, 5, 0:KT * 32].rearrange("p (k w) -> p k w", w=32)[:, :, 0:TAPS])\
               .then_inc(turned_out, 1)
            dve.wait_ge(turned, 3)
            dve.tensor_copy(h[:, :, 0:META], ps[:, 0, 0:KT * META].rearrange("p (k n) -> p k n", k=KT))\
               .then_inc(turned_out, 1)
            for g in range(2 * TILES):
                i, kh = g // 2, g % 2
                dve.wait_ge(turned, 4 + g)
                dve.tensor_copy(h[:, 4 * kh:4 * kh + 4, META + i * P:META + (i + 1) * P],
                                ps[:, (g + 1) % 4, :].rearrange("p (k n) -> p k n", k=4)).then_inc(turned_out, 1)
            dve.wait_ge(dw_split, 1)
            dve.tensor_tensor(dw_lo[:, :, 0:TAPS], dw[:, :, 0:TAPS], dw_hi[:, :, 0:TAPS].bitcast(F32), ALU.subtract)\
               .then_inc(dw_split, 1)

            def prep(r, k, gain):
                dve.wait_ge(ahi_done, 8 * PREP[r] + k + 1)
                dve.scalar_tensor_tensor(out=act_lo[:, k, :], in0=h[:, k, :],
                                         scalar=par[:, rows[gain] + k:rows[gain] + k + 1],
                                         in1=act_hi[:, k, :].bitcast(F32), op0=ALU.mult, op1=ALU.subtract)\
                   .then_inc(alo_done, 1)

            def newton(s, step, base, sqrt_sem, sqrt_count, ms, sd, r, t, res, last=None):
                dve.wait_ge(sqrt_sem, sqrt_count)
                dve.reciprocal(r, sd).then_inc(step, 1)
                dve.wait_ge(step, base + 1)
                dve.tensor_tensor(t, r, r, ALU.mult).then_inc(step, 1)
                dve.wait_ge(step, base + 2)
                dve.tensor_tensor(t, t, ms, ALU.mult).then_inc(step, 1)
                dve.wait_ge(step, base + 3)
                dve.tensor_scalar(t, t, -0.5, 1.5, ALU.mult, ALU.add).then_inc(step, 1)
                dve.wait_ge(step, base + 4)
                dve.tensor_tensor(res, r, t, ALU.mult).then_inc(step, 1)

            def stats(r):
                b0 = steps_before(r)
                dve.wait_ge(st_ready, r + 1)
                if r > 0:
                    dve.wait_ge(diag_done, r)
                if STEPS[r] == 1:
                    dve.tensor_scalar(st[:, 4, :], ps[:, 6, 0:5], -1.0 / D, None, ALU.mult).then_inc(st_step, 1)
                else:
                    dve.tensor_scalar(st[:, 0, :], ps[:, 6, 0:5], 1.0 / D, EPS, ALU.mult, ALU.add)\
                       .then_inc(st_step, 1)
                    newton(None, st_step, b0 + 1, st_sqrt, sqrts_before(r) + 1, st[:, 0, :], st[:, 1, :],
                           st[:, 2, :], st[:, 3, :], st[:, 4, :])
                dve.wait_ge(st_step, b0 + STEPS[r])
                if r > 0:
                    dve.wait_ge(bc_ready, r)
                dve.tensor_tensor(diag[:, :, :], ident[:, :].unsqueeze(1).broadcast_to([P, 5, P]),
                                  st[:, 4, :].unsqueeze(2).broadcast_to([P, 5, P]), ALU.mult).then_inc(diag_done, 1)
                dve.wait_ge(bc_ready, r + 1)
                dve.tensor_copy(rb[:, 0:META], ps[:, 6, P:P + META]).then_inc(rb_done, 1)
                dve.tensor_copy(rb[:, META:T], ps[:, 7, :]).then_inc(rb_done, 1)
                dve.wait_ge(rb_done, 2 * (r + 1))

            for k in range(KT):
                prep(R_MIX0, k, "mix0")
            dve.wait_ge(consts, CONSTS)
            stats(R_MIX0)

            rb2 = two(rb[:, :])

            def conv_in(qd, first):
                for e in range(2):
                    ct = (qd - Q_IN) * 2 + e
                    prime = first and e == 0
                    dve.wait_ge(used, 2 * ct + 1)
                    if not prime:
                        dve.wait_ge(sig_done, ct)
                    dve.tensor_tensor(two(tmp[:, 0, :]), pair_view(0), rb2, ALU.mult).then_inc(slot_free, 1)
                    dve.wait_ge(used, 2 * ct + 2)
                    if not prime:
                        dve.wait_ge(a_done, ct)
                    dve.tensor_tensor(two(tmp[:, 2, :]), pair_view(2), rb2, ALU.mult).then_inc(slot_free, 1)
                    dve.wait_ge(sig_done, ct + 1)
                    dve.wait_ge(slot_free, O_IN + 2 * ct + 2)
                    if not prime:
                        dve.wait_ge(c_done, ct)
                    dve.scalar_tensor_tensor(out=apad[:, PAD:PAD + T], in0=tmp[:, 2, :],
                                             scalar=par[:, bass.ds(rows["b_in"] + ct, 1)], in1=tmp[:, 1, :],
                                             op0=ALU.add, op1=ALU.mult).then_inc(a_done, 1)
                    dve.wait_ge(a_done, ct + 1)

                    def tap(w):
                        dst = (ca, cb)[w % 2]
                        tapw = dw[:, bass.ds(ct, 1), w:w + 1].rearrange("p a w -> p (a w)")
                        if w < 2:
                            dve.tensor_scalar(dst[:, :], apad[:, w:w + T], tapw, None, ALU.mult).then_inc(tap_done, 1)
                        else:
                            dve.wait_ge(tap_done, DVE_TAPS * ct + w - 1)
                            dve.scalar_tensor_tensor(out=dst[:, :], in0=apad[:, w:w + T], scalar=tapw,
                                                     in1=dst[:, :], op0=ALU.mult, op1=ALU.add).then_inc(tap_done, 1)
                    for w in range(4):
                        tap(w)
                    dve.wait_ge(cahi_done, ct + 1)
                    dve.tensor_tensor(a_lo[:, e, :], apad[:, :], a_hi[:, e, :].bitcast(F32), ALU.subtract)\
                       .then_inc(calo_done, 1)
                    for w in range(4, DVE_TAPS):
                        tap(w)
                    dve.wait_ge(taps_pe, ct + 1)
                    dve.wait_ge(tap_done, DVE_TAPS * (ct + 1))
                    dve.tensor_tensor(two(cb[:, :]), pair_view(4), two(cb[:, :]), ALU.add).then_inc(conv_mix, 1)
                    dve.wait_ge(conv_mix, ct + 1)
                    dve.tensor_tensor(conv[:, bass.ds(ct, 1), :].rearrange("p a t -> p (a t)"), ca[:, :], cb[:, :],
                                      ALU.add).then_inc(c_done, 1)
            quad_loop(dve, Q_IN, 4, conv_in)

            stats(R_MEAN)
            for k in range(KT):
                if k == 0:
                    dve.wait_ge(acc_added, 8 * (R_MEAN + 1))
                    dve.wait_ge(c_done, KT)
                dve.tensor_tensor(conv[:, k, :], conv[:, k, :], rb[:, :], ALU.add).then_inc(cc_done, 1)
            dve.wait_ge(cc_done, KT)
            stats(R_VAR)

            def ln_low(k):
                dve.wait_ge(lnhi_done, k + 1)
                dve.tensor_tensor(ln_lo[:, k, :], tmp[:, k % 2, :], ln_hi[:, k, :].bitcast(F32), ALU.subtract)\
                   .then_inc(lnlo_done, 1)
            for k in range(KT):
                dve.tensor_tensor(conv[:, k, :], conv[:, k, :], rb[:, :], ALU.mult).then_inc(ln_mul, 1)
                if k >= 2:
                    ln_low(k - 2)
            dve.wait_ge(ln_mul, KT)
            ln_low(KT - 2)
            ln_low(KT - 1)

            for m in range(KT):
                dve.wait_ge(used, n_of(Q_CO, m) + 1)
                dve.scalar_tensor_tensor(out=two(h[:, m, :]), in0=pair_view(slot_bank(O_CO + m)),
                                         scalar=par[:, rows["b_out"] + m:rows["b_out"] + m + 1], in1=two(h[:, m, :]),
                                         op0=ALU.add, op1=ALU.add).then_inc(slot_free, 1)
                if m >= 1:
                    prep(R_FFN0, m - 1, "ffn0")
            prep(R_FFN0, KT - 1, "ffn0")
            stats(R_FFN0)

            def ffn(L, s, gain, round_):
                N = T if L == 0 else SEQ
                if L == 0:
                    view = lambda ap: two(ap)
                    bank = lambda b: pair_view(b)
                    rbv = rb2
                else:
                    view = lambda ap: ap
                    bank = lambda b: ps[:, b, :]
                    rbv = rb[:, META:T]

                def low(qd, e):
                    fi = (qd - Q_GU[L][s]) * 2 + e
                    g = G0[L][s] + fi
                    dve.wait_ge(hidhi_done, g + 1)
                    dve.tensor_tensor(hid_lo[:, bass.ds(fi, 1), 0:N], tmp[:, 3:4, 0:N],
                                      hid_hi[:, bass.ds(fi, 1), 0:N].bitcast(F32), ALU.subtract)\
                       .then_inc(hidlo_done, 1)

                def gu(qd, first):
                    for e in range(2):
                        fi = (qd - Q_GU[L][s]) * 2 + e
                        g = G0[L][s] + fi
                        dve.wait_ge(used, n_of(qd, 2 * e) + 1)
                        if not (isinstance(g, int) and g == 0):
                            dve.wait_ge(silu_done, g)
                        dve.tensor_tensor(view(tmp[:, 0, 0:N]), bank(0), rbv, ALU.mult).then_inc(slot_free, 1)
                        if not (first and e == 0):
                            low(qd, e - 1)
                        dve.wait_ge(used, n_of(qd, 2 * e + 1) + 1)
                        if not (isinstance(g, int) and g == 0):
                            dve.wait_ge(p_done, g)
                        dve.tensor_tensor(view(tmp[:, 2, 0:N]), bank(2), rbv, ALU.mult).then_inc(slot_free, 1)
                quad_loop(dve, Q_GU[L][s], FH[s] // 2, gu)
                low(Q_GU[L][s] + FH[s] // 2 - 1, 1)

                def prep_m(qd, e):
                    m = (qd - Q_DN[L][s]) * 2 + e
                    dve.wait_ge(ahi_done, 8 * PREP[round_] + m + 1)
                    dve.scalar_tensor_tensor(out=act_lo[:, bass.ds(m, 1), :], in0=h[:, bass.ds(m, 1), :],
                                             scalar=par[:, bass.ds(rows[gain] + m, 1)],
                                             in1=act_hi[:, bass.ds(m, 1), :].bitcast(F32), op0=ALU.mult,
                                             op1=ALU.subtract).then_inc(alo_done, 1)

                def dn(qd, first):
                    for e in range(2):
                        m = (qd - Q_DN[L][s]) * 2 + e
                        dve.wait_ge(used, n_of(qd, 2 * e + 1) + 1)
                        src = h[:, bass.ds(m, 1), T - N:T].rearrange("p a t -> p (a t)")
                        if L == 1 and s == 1:
                            if not first:
                                dve.wait_ge(outT_ready, m - 1)
                            dst = tmp[:, e, 0:N]
                        else:
                            dst = src
                        dve.tensor_tensor(view(dst), bank(2 * e), view(src), ALU.add).then_inc(slot_free, 1)
                        if round_ is not None and not (first and e == 0):
                            prep_m(qd, e - 1)
                quad_loop(dve, Q_DN[L][s], KT // 2, dn)
                if round_ is not None:
                    prep_m(Q_DN[L][s] + KT // 2 - 1, 1)

            ffn(0, 0, None, None)
            ffn(0, 1, "mix1", R_MIX1)

            def tok(t):
                return slice(0, P) if t == 0 else slice(META + (t - 1) * P, META + t * P)

            def kv_in(t):
                if t >= 2:
                    dve.wait_ge(kvahi_done, t - 1)
                    dve.wait_ge(kvalo_done, t - 1)
                g = par[:, rows["kv"]:rows["kv"] + KT].unsqueeze(2).broadcast_to([P, KT, P])
                dve.tensor_tensor(kva[:, t % 2], h[:, :, tok(t)], g, ALU.mult).then_inc(kva_done, 1)

            def kv_low(t):
                dve.wait_ge(kvahi_done, t + 1)
                dve.tensor_tensor(kva_lo[:, t % 2], kva[:, t % 2], kva_hi[:, t % 2].bitcast(F32), ALU.subtract)\
                   .then_inc(kvalo_done, 1)

            def kv_out(t):
                src = ps[:, 4 + t % 2, :]
                dve.wait_ge(vhi_done, t + 1)
                dve.scalar_tensor_tensor(out=v_lo[:, t, :], in0=src[:, KV:2 * KV], scalar=st[:, 4, t:t + 1],
                                         in1=v_hi[:, t, :].bitcast(F32), op0=ALU.mult, op1=ALU.subtract)\
                   .then_inc(v_low, 1)
                if t == 0:
                    dve.tensor_scalar(v_meta[0:META, :], src[0:META, KV:2 * KV], st[0:META, 4, 0:1], None, ALU.mult)\
                       .then_inc(v_low, 1)
                dve.tensor_scalar(kx[:, t, :], src[:, 0:KV], st[:, 4, t:t + 1], None, ALU.mult).then_inc(kx_done, 1)

            kv_in(0)
            kv_in(1)
            kv_low(0)
            stats(R_MIX1)
            for t in range(1 + TILES):
                if t + 1 <= TILES:
                    kv_low(t + 1)
                if t + 2 <= TILES:
                    kv_in(t + 2)
                kv_out(t)
            dve.wait_ge(sink_in, 48)
            dve.tensor_tensor(gqk[:, :], gk[:, :], gq[:, :], ALU.mult).then_inc(gqk_done, 1)

            def q_scale(j):
                dve.wait_ge(used, n_of(Q_Q, j) + 1)
                dve.tensor_tensor(q_of(j // PER)[:, j % PER, :], ps[:, 2, :], rb[:, META:T], ALU.mult)\
                   .then_inc(q_out, 1)

            def q_sums(j):
                dve.wait_ge(qss_ready, j + 1)
                if j == PER:
                    dve.wait_ge(rq_step, 1)
                n = 2 * TILES
                dve.tensor_copy(qss[:, (j % PER) * n:(j % PER + 1) * n], ps[:, 2, 0:n]).then_inc(qss_read, 1)

            dve.wait_ge(ksq_done, 1)
            dve.tensor_reduce(rk[:, 3, :], tmp2k.rearrange("p (t d) -> p t d", d=DH), AX_X, ALU.add)\
               .then_inc(k_step, 1)
            dve.wait_ge(k_step, 1)
            dve.tensor_scalar(rk[:, 0, :], rk[:, 3, :], 1.0 / DH, EPS, ALU.mult, ALU.add).then_inc(k_step, 1)
            q_scale(0)
            newton(None, k_step, 2, k_sqrt, 1, rk[:, 0, :], rk[:, 1, :], rk[:, 2, :], rk[:, 3, :], rk[:, 4, :])
            dve.wait_ge(k_step, 7)
            k3 = kx[:, :, :].rearrange("p t (g d) -> p (t g) d", d=DH)
            NG = (1 + TILES) * GROUPS
            dve.tensor_tensor(k3, k3, rk[:, 4, :].unsqueeze(2).broadcast_to([P, NG, DH]), ALU.mult)\
               .then_inc(k_step, 1)
            dve.wait_ge(k_step, 8)
            dve.wait_ge(gqk_done, 1)
            dve.tensor_tensor(k3, k3, gqk[:, :].unsqueeze(1).broadcast_to([P, NG, DH]), ALU.mult)\
               .then_inc(k_step, 1)
            q_sums(0)
            for j in range(1, PER):
                q_scale(j)
                q_sums(j)
            dve.wait_ge(kt_ready, 1)
            for a in range(PAIRS):
                for i in range(TILES):
                    dve.tensor_copy(kt[:, a, TILE_AT[i]:TILE_AT[i] + P], ps[:, 4 + a, i * P:(i + 1) * P])\
                       .then_inc(kt_done, 1)
                for at_ in META_AT:
                    dve.tensor_copy(kt[:, a, at_:at_ + META], ps[:, 6, a * P:a * P + META]).then_inc(kt_done, 1)

            def q_norms(a):
                dve.wait_ge(qss_read, PER * (a + 1))
                dve.tensor_scalar(rq[:, 0, :], qss[:, :], 1.0 / DH, EPS, ALU.mult, ALU.add).then_inc(rq_step, 1)
                newton(None, rq_step, 7 * a + 1, rq_sqrt, a + 1, rq[:, 0, :], rq[:, 1, :], rq[:, 2, :], rq[:, 3, :],
                       rq[:, 4, :])
                dve.wait_ge(rq_step, 7 * a + 6)
                dve.tensor_scalar(rqs[:, a].rearrange("p r i b -> p (r i b)"), rq[:, 4, :], DH ** -0.5, None,
                                  ALU.mult).then_inc(rq_step, 1)
                dve.wait_ge(rq_step, 7 * (a + 1))

            def scores(u):
                a, b, i = units[u]
                w, n, z = u % 3, keys_of(i), ORDER[i][2]
                m_ = {0: mask_a[:, P + META:2 * P + 2 * META], 2: mask_b[:, :]}.get(i, mask_a[:, 0:2 * P + META])
                if u >= 3:
                    dve.wait_ge(pt_ready, u - 2)
                for r in range(PER):
                    dve.wait_ge(s_ready, PER * u + r + 1)
                    dve.tensor_tensor_reduce(out=s_sb[:, w, r, 0:n], in0=ps[:, S_BANKS[(PER * u + r) % 3], 0:n],
                                             in1=m_, scale=1.0, scalar=-3.0e38,
                                             op0=ALU.add, op1=ALU.max, accum_out=smx[:, w, 0, r:r + 1])\
                       .then_inc(s_read, 1)

            def maxima(u):
                a, b, i = units[u]
                w = u % 3
                sink = sinks[:, (2 * a + b) * PER:(2 * a + b + 1) * PER]
                dve.wait_ge(s_read, 4 * (u + 1))
                dve.tensor_tensor(smx[:, w, 1, :], smx[:, w, 0, :], rqs[:, a, :, i, b], ALU.mult).then_inc(m_step, 1)
                dve.wait_ge(m_step, 4 * u + 1)
                dve.tensor_tensor(smx[:, w, 2, :], smx[:, w, 1, :], sink, ALU.max).then_inc(m_step, 1)
                dve.wait_ge(m_step, 4 * u + 2)
                dve.tensor_scalar(smx[:, w, 3, :], smx[:, w, 2, :], -1.0, None, ALU.mult).then_inc(m_step, 1)
                dve.wait_ge(m_step, 4 * u + 3)
                dve.tensor_tensor(smx[:, w, 4, :], smx[:, w, 3, :], sink, ALU.add).then_inc(m_step, 1)

            def denominators(u):
                w = u % 3
                dve.wait_ge(p_exp, 5 * (u + 1))
                if u >= 3:
                    dve.wait_ge(p_norm, u - 2)
                dve.tensor_tensor(sden[:, w, :], smx[:, w, 6, :], smx[:, w, 5, :], ALU.add).then_inc(p_step, 1)
                dve.wait_ge(p_step, 2 * u + 1)
                dve.reciprocal(smx[:, w, 7, :], sden[:, w, :]).then_inc(p_step, 1)

            def pt_low(u):
                a, b, i = units[u]
                n = blocks_before[u]
                for z in (1, 0)[:1 if i == 0 else 2]:
                    n += 1
                    dve.wait_ge(pthi_done, n)
                    dve.tensor_tensor(pt_lo[:, u % 2, z, :], ps[:, 4 + z, :], pt_hi[:, u % 2, z, :].bitcast(F32),
                                      ALU.subtract).then_inc(ptlo_done, 1)

            def o_low(u):
                a, b, i = units[u]
                rowsel = slice(b * DH, (b + 1) * DH)
                hi_, lo_ = ((o0_hi, o0_lo), (o1_hi, o1_lo))[a]
                dve.wait_ge(ohi_done, u + 1)
                dve.tensor_tensor(lo_[rowsel, :, i * P:(i + 1) * P],
                                  ps[rowsel, 7, :].rearrange("p (r n) -> p r n", r=PER),
                                  hi_[rowsel, :, i * P:(i + 1) * P].bitcast(F32), ALU.subtract)\
                   .then_inc(olo_done, 1)

            q_norms(0)
            for u in range(2):
                scores(u)
                maxima(u)
            denominators(0)
            for u in range(NU):
                if u + 1 < NU:
                    denominators(u + 1)
                if u < NU // 2 and u % 2 == 0 and u >= 2:
                    q_sums(PER + u // 2 - 1)
                if u + 2 == NU // 2:
                    q_scale(QJ - 1)
                    q_sums(QJ - 1)
                    q_norms(1)
                if u + 2 < NU:
                    scores(u + 2)
                    maxima(u + 2)
                pt_low(u)
                if u < NU // 2 - 2 and u % 2 == 0:
                    q_scale(PER + u // 2)
                if u >= 1:
                    o_low(u - 1)
            o_low(NU - 1)

            for m in range(KT):
                dve.wait_ge(used, n_of(Q_O, m) + 1)
                dve.tensor_tensor(h[:, m, META:T], ps[:, slot_bank(O_O + m), :], h[:, m, META:T], ALU.add)\
                   .then_inc(slot_free, 1)
                if m >= 1:
                    prep(R_FFN1, m - 1, "ffn1")
            prep(R_FFN1, KT - 1, "ffn1")
            stats(R_FFN1)
            ffn(1, 0, None, None)
            ffn(1, 1, None, None)

        @block.tensor
        def _(pe):
            pe.wait_ge(consts, CONSTS)
            pe.wait_ge(par_in, 16 * 9)
            pe.transpose(ps[:, 4, 0:NROWS], par_rows[:, :], ident[0:NROWS, 0:NROWS]).then_inc(turned, 1)
            pe.wait_ge(dwr_in, 16)
            for k in range(KT):
                t = pe.transpose(ps[:, 5, 32 * k:32 * k + TAPS], dw_rows[:, k * P:(k + 1) * P],
                                 ident[0:TAPS, 0:TAPS])
            t.then_inc(turned, 1)
            pe.wait_ge(x_in[0], 16)
            for k in range(KT):
                t = pe.transpose(ps[:, 0, META * k:META * (k + 1)], meta_tok[:, k * P:(k + 1) * P],
                                 ident[0:META, 0:META])
            t.then_inc(turned, 1)
            for g in range(2 * TILES):
                i, kh = g // 2, g % 2
                pe.wait_ge(x_in[1 + i], 16)
                if g >= 3:
                    pe.wait_ge(turned_out, 2 + g - 2)
                for k in range(4):
                    col = (4 * kh + k) * P
                    t = pe.transpose(ps[:, (g + 1) % 4, k * P:(k + 1) * P], x_tok[:, i, col:col + P], ident[:, :])
                t.then_inc(turned, 1)
            pe.wait_ge(turned_out, 2 + 1 + 2 * TILES)

            def three(outs, lhs, rhs_hi, rhs_lo, first, last):
                passes = ((lhs[0], rhs_hi), (lhs[0], rhs_lo), (lhs[1], rhs_hi))
                for n, (wt, rhs) in enumerate(passes):
                    for o_, r_ in zip(outs, rhs):
                        mm = pe.matmul(o_, wt, r_, start=first and n == 0, stop=last and n == 2)
                return mm

            def chunk(c, k):
                return w_hi[:, c, k * P:(k + 1) * P], w_lo[:, c, k * P:(k + 1) * P]

            def cols(t, k, wide):
                if wide:
                    return [t[:, k, 0:HALF], t[:, k, HALF:T]]
                return [t[:, k, META:T]]

            def outs(bank, wide):
                return [ps[:, bank, 0:HALF], ps[:, bank + 1, 0:HALF]] if wide else [ps[:, bank, :]]

            def product(qd, c, o_, bank, ins, nk, k0, wide, first, last, ready=None, base=0, colf=None):
                pe.wait_ge(lo_done, n_of(qd, c) + 1)
                if first and not (isinstance(o_, int) and o_ < 2):
                    pe.wait_ge(slot_free, o_ - 1)
                colf = colf or cols
                for k in range(nk):
                    if ready is not None:
                        pe.wait_ge(ready, base + k0 + k + 1)
                    mm = three(outs(bank, wide), chunk(c, k), colf(ins[0], k0 + k, wide), colf(ins[1], k0 + k, wide),
                               first and k == 0, last and k == nk - 1)
                mm.then_inc(used, 1)

            def stats_sum(r):
                pe.wait_ge(acc_added, 8 * (r + 1))
                if r > 0:
                    pe.wait_ge(rb_done, 2 * r)
                for t in range(5):
                    lo_ = 0 if t == 0 else META + (t - 1) * P
                    mm = pe.matmul(ps[:, 6, t:t + 1], acc[:, lo_:lo_ + P], ones[:, 0:1], start=True, stop=True)
                mm.then_inc(st_ready, 1)

            def stats_spread(r):
                pe.wait_ge(diag_done, r + 1)
                pe.matmul(ps[:, 6, P:P + META], ones[:, :], diag[:, 0, 0:META], start=True, stop=True)
                pe.matmul(ps[:, 7, :], ones[:, :], diag[:, 1:5, :].rearrange("p t n -> p (t n)"),
                          start=True, stop=True).then_inc(bc_ready, 1)

            act_in = (act_hi, act_lo)

            def taps(qd, e):
                ct = (qd - Q_IN) * 2 + e
                pe.wait_ge(calo_done, ct + 1)
                pe.wait_ge(dg_done, 2 * ct + 2)
                if not (isinstance(ct, int) and ct == 0):
                    pe.wait_ge(conv_mix, ct)
                e = e % 2
                for w in range(PE_TAPS):
                    at_ = DVE_TAPS + w
                    rng = lambda t: [t[:, e, at_ + HALF * z:at_ + HALF * (z + 1)] for z in range(2)]
                    mm = three(outs(4, True), (dg_hi[:, e, w, :], dg_lo[:, e, w, :]), rng(a_hi), rng(a_lo),
                               w == 0, w == PE_TAPS - 1)
                mm.then_inc(taps_pe, 1)

            def conv_in(qd, first):
                for e in range(2):
                    ct = (qd - Q_IN) * 2 + e
                    prime = first and e == 0
                    product(qd, 2 * e, O_IN + 2 * ct, 0, act_in, KT, 0, True, True, True,
                            alo_done if prime else None, 0)
                    if prime:
                        stats_sum(R_MIX0)
                    else:
                        taps(qd, e - 1)
                    product(qd, 2 * e + 1, O_IN + 2 * ct + 1, 2, act_in, KT, 0, True, True, True)
                    if prime:
                        stats_spread(R_MIX0)
            quad_loop(pe, Q_IN, 4, conv_in)
            taps(Q_IN + 3, 1)
            stats_sum(R_MEAN)
            stats_spread(R_MEAN)
            stats_sum(R_VAR)
            stats_spread(R_VAR)

            for m in range(KT):
                product(Q_CO + m // 4, m % 4, O_CO + m, slot_bank(O_CO + m), (ln_hi, ln_lo), KT, 0, True, True, True,
                        lnlo_done if m == 0 else None, 0)

            def ffn(L, s, round_):
                wide = L == 0

                def gu(qd, first):
                    for e in range(2):
                        fi = (qd - Q_GU[L][s]) * 2 + e
                        prime = first and e == 0 and s == 0
                        product(qd, 2 * e, O_GU[L][s] + 2 * fi, 0, act_in, KT, 0, wide, True, True,
                                alo_done if prime else None, 8 * PREP[round_] if prime else 0)
                        if prime:
                            stats_sum(round_)
                        product(qd, 2 * e + 1, O_GU[L][s] + 2 * fi + 1, 2, act_in, KT, 0, wide, True, True)
                        if prime:
                            stats_spread(round_)
                quad_loop(pe, Q_GU[L][s], FH[s] // 2, gu)
                hid_cols = lambda t, k, w_: [t[:, k, 0:HALF], t[:, k, HALF:T]] if w_ else [t[:, k, 0:SEQ]]

                def turn(qd, e):
                    m = (qd - Q_DN[L][s]) * 2 + e
                    pe.wait_ge(slot_free, O_DN[L][s] + m + 1)
                    e = e % 2
                    if not (isinstance(m, int) and m < 2):
                        pe.wait_ge(out_sb, m - 1)
                    for i in range(TILES):
                        t = pe.transpose(ps[:, 4 + e, i * P:(i + 1) * P], tmp[:, e, i * P:(i + 1) * P], ident[:, :])
                    t.then_inc(outT_ready, 1)

                def dn(qd, first):
                    for e in range(2):
                        m = (qd - Q_DN[L][s]) * 2 + e
                        for part in range(2):
                            product(qd, 2 * e + part, O_DN[L][s] + m, 2 * e, (hid_hi, hid_lo), PARTS[s],
                                    part * PARTS[s], wide, part == 0, part == 1,
                                    hidlo_done if first and e == 0 else None, G0[L][s], hid_cols)
                        if L == 1 and s == 1 and not (first and e == 0):
                            turn(qd, e - 1)
                quad_loop(pe, Q_DN[L][s], KT // 2, dn)
                if L == 1 and s == 1:
                    turn(Q_DN[L][s] + KT // 2 - 1, 1)

            ffn(0, 0, R_FFN0)
            ffn(0, 1, R_FFN0)

            stats_sum(R_MIX1)
            for t in range(1 + TILES):
                if t == 1:
                    stats_spread(R_MIX1)
                pe.wait_ge(kvalo_done, t + 1)
                if t >= 2:
                    pe.wait_ge(kx_done, t - 1)
                for c in range(SLOTS):
                    if t == 0:
                        pe.wait_ge(lo_done, n_of(Q_KV, c) + 1)
                    for kk in range(2):
                        k = 2 * c + kk
                        wh, wl = (w_[:, c, kk * 512:(kk + 1) * 512] for w_ in (w_hi, w_lo))
                        xh, xl = kva_hi[:, t % 2, k, :], kva_lo[:, t % 2, k, :]
                        for n, (l_, r_) in enumerate(((xh, wh), (xh, wl), (xl, wh))):
                            mm = pe.matmul(ps[:, 4 + t % 2, :], l_, r_, start=k == 0 and n == 0,
                                           stop=k == KT - 1 and n == 2)
                    if t == TILES:
                        mm.then_inc(used, 1)
                if t < TILES:
                    mm.then_inc(kv_ready, 1)

            def q_product(j):
                c = j % 4
                pe.wait_ge(lo_done, n_of(Q_Q, j) + 1)
                if j == 0:
                    pe.wait_ge(slot_free, O_O)
                    pe.wait_ge(alo_done, 8 * (PREP[R_MIX1] + 1))
                else:
                    pe.wait_ge(qss_read, j)
                for k in range(KT):
                    mm = three([ps[:, 2, :]], chunk(c, k), cols(act_hi, k, False), cols(act_lo, k, False), k == 0,
                               k == KT - 1)
                mm.then_inc(used, 1)

            def q_sums(j):
                pe.wait_ge(qsq_done, j + 1)
                for i in range(TILES):
                    at_ = i * 2
                    mm = pe.matmul(ps[:, 2, at_:at_ + 2], tmp[:, 2 + j % 2, i * P:(i + 1) * P], blk2[:, :],
                                   start=True, stop=True)
                mm.then_inc(qss_ready, 1)

            def turn_keys():
                pe.wait_ge(k_step, 9)
                for a in range(PAIRS):
                    for i in range(TILES):
                        pe.transpose(ps[:, 4 + a, i * P:(i + 1) * P], kx[:, 1 + i, a * P:(a + 1) * P], ident[:, :])
                for a in range(PAIRS):
                    t = pe.transpose(ps[:, 6, a * P:(a + 1) * P], kx[:, 0, a * P:(a + 1) * P], ident[:, :])
                t.then_inc(kt_ready, 1)

            for j in range(PER):
                q_product(j)
                if j == PER - 1:
                    turn_keys()
                q_sums(j)
            pe.wait_ge(kt_done, PAIRS * (TILES + 2))

            def scores(u):
                a, b, i = units[u]
                half = slice(b * DH, (b + 1) * DH)
                if b == 0 and i == 0:
                    pe.wait_ge(q_out, PER * (a + 1))
                n, at_ = keys_of(i), WINDOW_AT[i]
                for r in range(PER):
                    s_ = PER * u + r
                    if s_ >= 3:
                        pe.wait_ge(s_read, s_ - 2)
                    pe.matmul(ps[:, S_BANKS[s_ % 3], 0:n], q_of(a)[half, r, i * P:(i + 1) * P],
                              kt[half, a, at_:at_ + n], start=True, stop=True).then_inc(s_ready, 1)

            def turn_p(u):
                a, b, i = units[u]
                before_, this_, meta_ = ORDER[i]
                pe.wait_ge(p_norm, u + 1)
                if u >= 1:
                    pe.wait_ge(ptlo_done, blocks_before[u])
                    pe.wait_ge(ptm_done, u)
                for bank, at_, n in ((5, this_, P), (4, before_, P), (6, meta_, META)):
                    if at_ is None:
                        continue
                    for r in range(PER):
                        t = pe.transpose(ps[0:n, bank, r * P:(r + 1) * P], s_sb[:, u % 3, r, at_:at_ + n],
                                         ident[:, :])
                t.then_inc(pt_ready, 1)

            def values(u):
                a, b, i = units[u]
                pair = slice(a * P, (a + 1) * P)
                pe.wait_ge(ptm_done, u + 1)
                pe.wait_ge(ptlo_done, blocks_before[u + 1])
                if u >= 1:
                    pe.wait_ge(olo_done, u)
                for n, (z, t) in enumerate([(1, i + 1), (0, i)][:1 if i == 0 else 2]):
                    three([ps[:, 7, :]], [v_[:, t, pair] for v_ in (v_hi, v_lo)], [pt_hi[:, u % 2, z, :]],
                          [pt_lo[:, u % 2, z, :]], n == 0, False)
                pe.matmul(ps[:, 7, :], v_meta[0:META, pair], sq[0:META, u % 2, 0:PER * P], start=False, stop=True)\
                  .then_inc(pv_ready, 1)

            scores(0)
            scores(1)
            for u in range(NU):
                turn_p(u)
                if u < NU // 2 - 2 and u % 2 == 0:
                    q_product(PER + u // 2)
                if u + 2 < NU:
                    if u + 2 == NU // 2:
                        q_product(QJ - 1)
                        q_sums(QJ - 1)
                    scores(u + 2)
                if u >= 1:
                    values(u - 1)
                if u < NU // 2 - 2 and u % 2 == 1:
                    q_sums(PER + u // 2)
            values(NU - 1)

            def o_cols(t, k, wide):
                src = (o0_hi, o1_hi) if t is o0_hi else (o0_lo, o1_lo)
                return [src[k // PER][:, k % PER, :]]
            pe.wait_ge(olo_done, NU)
            for m in range(KT):
                product(Q_O + m // 4, m % 4, O_O + m, slot_bank(O_O + m), (o0_hi, o0_lo), KT, 0, False, True, True,
                        None, 0, o_cols)

            ffn(1, 0, R_FFN1)
            ffn(1, 1, R_FFN1)


_INS = ["x", "meta_tokens", "norm_mix", "norm_ffn", "conv_w_in", "conv_b_in", "conv_dw", "conv_ln_g", "conv_ln_b",
        "conv_w_out", "conv_b_out", "kv_norm", "w_kv", "k_norm", "w_q", "q_norm", "attn_sinks", "w_o",
        "ffn_w_gate", "ffn_w_up", "ffn_w_down"]


def kernel(**inputs):
    import numpy as np
    import concourse.bacc as bacc
    from concourse.bass_utils import run_bass_kernel_spmd

    nc = bacc.Bacc("TRN2", target_bir_lowering=False, num_devices=1)
    arrays, args = {}, []
    for name in _INS:
        a = np.ascontiguousarray(inputs[name])
        arrays[f"in_{name}"] = a
        args.append(nc.dram_tensor(f"in_{name}", a.shape, mybir.dt.from_np(a.dtype), kind="ExternalInput").ap())
    res = nc.dram_tensor("out_dram", arrays["in_x"].shape, F32, kind="ExternalOutput").ap()
    trunk_kernel(nc, *args, res)
    r = run_bass_kernel_spmd(nc, [arrays], core_ids=[0])
    return r.results[0]["out_dram"]
```

```python
from contextlib import ExitStack

import concourse.bass as bass
from concourse import mybir

F32 = mybir.dt.float32
F32R = mybir.dt.float32r
ACT = mybir.ActivationFunctionType
ALU = mybir.AluOpType
AX_X = mybir.AxisListType.X

P = 128
EPS = 1e-6
NEG = -1e30
SLOTS = 4
WIDE = 1024
PE_TAPS = 7
LAST_TAPS = 4
AP_TAPS = 6
STATS_AT = 6
GATE_AFTER = 7
LAG_HI = 3
LAG_LO = 2


def trunk_kernel(nc, x, meta_tokens, norm_mix, norm_ffn, conv_w_in, conv_b_in, conv_dw, conv_ln_g, conv_ln_b,
                 conv_w_out, conv_b_out, kv_norm, w_kv, k_norm, w_q, q_norm, attn_sinks, w_o,
                 ffn_w_gate, ffn_w_up, ffn_w_down, out):
    _, SEQ, D = x.shape
    META = meta_tokens.shape[0]
    T = META + SEQ
    KT = D // P
    HALF = T // 2
    TILES = SEQ // P
    TAPS = conv_dw.shape[1]
    PAD = TAPS - 1
    DVE_TAPS = TAPS - PE_TAPS - AP_TAPS
    AP0, PE0 = DVE_TAPS, DVE_TAPS + AP_TAPS
    LAST0 = DVE_TAPS - LAST_TAPS
    DH = k_norm.shape[0]
    HEADS = attn_sinks.shape[1]
    GROUPS = w_kv.shape[1] // (2 * DH)
    PER = HEADS // GROUPS
    PAIRS = GROUPS // 2
    KV = GROUPS * DH
    FT = ffn_w_gate.shape[2] // P
    FH = [12, FT - 12]
    PARTS = [6, 5]
    assert (D, T, DH, TILES, GROUPS, PER, FT) == (1024, 528, 64, 4, 4, 4, 22)

    q = 0
    Q_IN = q; q += 2 * KT // SLOTS
    Q_CO = q; q += KT // SLOTS
    Q_GU, Q_DN = [[0, 0], [0, 0]], [[0, 0], [0, 0]]
    for s in range(2):
        Q_GU[0][s] = q; q += 2 * FH[s] // SLOTS
        Q_DN[0][s] = q; q += 2 * KT // SLOTS
    Q_Q0 = q; q += 1
    Q_KV = q; q += 1
    Q_Q1 = q; q += 1
    Q_O = q; q += KT // SLOTS
    for s in range(2):
        Q_GU[1][s] = q; q += 2 * FH[s] // SLOTS
        Q_DN[1][s] = q; q += 2 * KT // SLOTS
    QUADS = q

    o = 0
    O_IN = o; o += 2 * KT
    O_CO = o; o += KT
    O_GU, O_DN = [[0, 0], [0, 0]], [[0, 0], [0, 0]]
    for L in range(2):
        if L == 1:
            O_O = o; o += KT
        for s in range(2):
            O_GU[L][s] = o; o += 2 * FH[s]
            O_DN[L][s] = o; o += KT

    G0 = [[0, FH[0]], [FT, FT + FH[0]]]

    R_MIX0, R_MEAN, R_VAR, R_FFN0, R_MIX1, R_FFN1 = range(6)
    STEPS = [4, 0, 4, 4, 4, 4]
    PREP = {R_MIX0: 0, R_FFN0: 1, R_MIX1: 2, R_FFN1: 3}
    SQ0 = {R_MIX0: 0, R_VAR: 1, R_FFN0: 2, R_MIX1: 3, R_FFN1: 4}
    ADDED = {R_MIX0: 0, R_MEAN: 7, R_FFN0: 14, R_MIX1: 22, R_FFN1: 30}
    SUM_BANK = [6, 6, 4, 6, 6, 6]
    ACCS = [R_MIX0, R_MEAN, R_FFN0, R_MIX1, R_FFN1]

    rows = {}
    at = 0
    for name, n in (("mix0", KT), ("mix1", KT), ("ffn0", KT), ("ffn1", KT), ("b_in", 2 * KT), ("ln_g", KT),
                    ("ln_b", KT), ("b_out", KT), ("kv", KT)):
        rows[name] = at
        at += n
    NROWS = at
    units = [(a, b, i) for a in range(PAIRS) for b in range(2) for i in range(TILES)]
    NU = len(units)
    S_BANKS = [0, 1, 3, 2]
    Q_BANKS = [0, 1, 2, 3, 0, 1, 2, 4]
    BUFS = 4
    AHEAD = 3
    KEYS = 4 * P + 2 * META
    TILE_AT = [0, P + META, 2 * P + META, 3 * P + 2 * META]
    META_AT = [P, 3 * P + META]
    WINDOW_AT = [0, 0, P, 2 * P + META]
    ORDER = [(None, 0, P), (0, P + META, P), (META, META + P, 0), (0, P + META, P)]
    CONSTS = 13
    QJ = PAIRS * PER

    ctx = ExitStack()
    with ctx:
        def sb(name, shape, dt, where=ctx):
            return where.enter_context(nc.sbuf_tensor(name, shape, dt))

        def sem(name):
            return ctx.enter_context(nc.semaphore(name))

        h = sb("h", [P, KT, T], F32)
        act_hi = sb("act_hi", [P, KT, T], F32R)
        act_lo = sb("act_lo", [P, KT, T], F32R)
        raw = sb("raw", [P, SLOTS, WIDE], F32)
        w_hi = sb("w_hi", [P, SLOTS, WIDE], F32R)
        w_lo = sb("w_lo", [P, SLOTS, WIDE], F32R)
        tmp = sb("tmp", [P, 4, T], F32)
        sq = sb("sq", [P, 2, T], F32)
        acc = sb("acc", [P, T], F32)
        rb = sb("rb", [P, T], F32)
        ident = sb("ident", [P, P], F32)
        ones = sb("ones", [P, P], F32)
        blk2 = sb("blk2", [P, 2], F32)
        mask_a = sb("mask_a", [P, 2 * P + 2 * META], F32)
        mask_b = sb("mask_b", [P, META + 2 * P], F32)
        par = sb("par", [P, NROWS], F32)
        sinks = sb("sinks", [P, HEADS], F32)
        gk = sb("gk", [P, DH], F32)
        gq = sb("gq", [P, DH], F32)
        gqk = sb("gqk", [P, DH], F32)
        rms_tok = sb("rms_tok", [P, 1 + TILES], F32)
        rk = sb("rk", [P, 5, (1 + TILES) * GROUPS], F32)
        rq = sb("rq", [P, 5, 2 * PER * TILES], F32)
        rqs = sb("rqs", [P, PAIRS, PER, TILES, 2], F32)
        smx = sb("smx", [P, BUFS, 8, PER], F32)
        sden = sb("sden", [P, BUFS, PER], F32)

        with ExitStack() as region:
            conv = sb("conv", [P, KT, T], F32, region)
            dw = sb("dw", [P, KT, 32], F32, region)
            dw_hi = sb("dw_hi", [P, KT, 32], F32R, region)
            dw_lo = sb("dw_lo", [P, KT, 32], F32R, region)
            apad = sb("apad", [P, PAD + T], F32, region)
            with ExitStack() as early:
                x_tok = sb("x_tok", [P, TILES, D], F32, early)
                meta_tok = sb("meta_tok", [META, D], F32, early)
                par_rows = sb("par_rows", [NROWS, P], F32, early)
                dw_rows = sb("dw_rows", [TAPS, D], F32, early)
            with ExitStack() as early:
                a_hi = sb("a_hi", [P, 2, PAD + T], F32R, early)
                a_lo = sb("a_lo", [P, 2, PAD + T], F32R, early)
                ca = sb("ca", [P, T], F32, early)
                cb = sb("cb", [P, T], F32, early)
                cp = sb("cp", [P, 2, T], F32, early)
                prod = sb("prod", [P, 2, T], F32, early)
                dg_hi = sb("dg_hi", [P, 2, PE_TAPS, P], F32R, early)
                dg_lo = sb("dg_lo", [P, 2, PE_TAPS, P], F32R, early)
            ln_hi = sb("ln_hi", [P, KT, T], F32R, region)
            ln_lo = sb("ln_lo", [P, KT, T], F32R, region)
        with ExitStack() as region:
            hid_hi = sb("hid_hi", [P, FH[0], T], F32R, region)
            hid_lo = sb("hid_lo", [P, FH[0], T], F32R, region)
        with ExitStack() as region:
            q1 = sb("q1", [P, PER, SEQ], F32, region)
            kt = sb("kt", [P, PAIRS, KEYS], F32, region)
            v_hi = sb("v_hi", [P, 1 + TILES, KV], F32R, region)
            v_lo = sb("v_lo", [P, 1 + TILES, KV], F32R, region)
            with ExitStack() as early:
                q0 = sb("q0", [P, PER, SEQ], F32, early)
            o1_lo = sb("o1_lo", [P, PER, SEQ], F32R, region)
            with ExitStack() as early:
                kx = sb("kx", [P, 1 + TILES, KV], F32, early)
                kva_hi = sb("kva_hi", [P, 3, KT, P], F32R, early)
                kva_lo = sb("kva_lo", [P, 3, KT, P], F32R, early)
                kva = sb("kva", [P, 3, KT, P], F32, early)
            s_sb = sb("s_sb", [P, BUFS, PER, META + 2 * P], F32, region)
            pt_hi = sb("pt_hi", [P, 2, 2, PER * P], F32R, region)
            pt_lo = sb("pt_lo", [P, 2, 2, PER * P], F32R, region)
            o0_hi = sb("o0_hi", [P, PER, SEQ], F32R, region)
            o0_lo = sb("o0_lo", [P, PER, SEQ], F32R, region)
            o1_hi = sb("o1_hi", [P, PER, SEQ], F32R, region)

        ps = ctx.enter_context(nc.psum_tensor("ps", [P, 8, 512], F32))

        par_in, sink_in, dwr_in = sem("par_in"), sem("sink_in"), sem("dwr_in")
        x_in = [sem(f"x_in{i}") for i in range(1 + TILES)]
        landed = [sem(f"landed{c}") for c in range(SLOTS)]
        landed2 = [sem(f"landed_second_half{c}") for c in range(SLOTS)]
        hi_done, lo_done, used = sem("w_hi_done"), sem("w_lo_done"), sem("w_used")
        consts, zeroed = sem("consts"), sem("acc_zeroed")
        turned, turned_out = sem("turned"), sem("turned_out")
        dw_split = sem("dw_split")
        sq_done, acc_added = sem("sq_done"), sem("acc_added")
        ahi_done, alo_done = sem("act_hi_done"), sem("act_lo_done")
        st_ready, st_step, st_root = sem("st_ready"), sem("st_step"), sem("st_root")
        var_paired, tok_ready, tok_done = sem("var_paired"), sem("rms_tok_ready"), sem("rms_tok_done")
        slot_free = sem("slot_free")
        sig_done, a_done, cahi_done, calo_done = sem("sig_done"), sem("a_done"), sem("conv_a_hi"), sem("conv_a_lo")
        tap_done, taps_pe, conv_mix, c_done = sem("tap_done"), sem("taps_pe"), sem("conv_mix"), sem("c_done")
        c_sum = sem("conv_summed")
        dg_done, prod_done, prod_added, t_done = (sem("dg_done"), sem("tap_products"), sem("tap_products_added"),
                                                  sem("vector_and_tensor_taps"))
        cc_done, ln_mul, ln_silu, lnhi_done, lnlo_done = (sem("cc_done"), sem("ln_mul"), sem("ln_silu"),
                                                         sem("ln_hi_done"), sem("ln_lo_done"))
        silu_done, p_done, hidhi_done, hidlo_done = (sem("silu_done"), sem("hid_product"), sem("hid_hi_done"),
                                                     sem("hid_lo_done"))
        kva_done, kvahi_done, kvalo_done, kv_ready = sem("kva_done"), sem("kva_hi"), sem("kva_lo"), sem("kv_ready")
        vhi_done, kx_done, ksq_done, k_step, k_sqrt = (sem("v_hi_done"), sem("kx_done"), sem("ksq_done"),
                                                      sem("k_step"), sem("k_sqrt"))
        kt_ready, kt_done = sem("kt_ready"), sem("kt_done")
        q_out, qsq_done, qss_ready = sem("q_out"), sem("qsq_done"), sem("q_sums")
        rq_step, rq_sqrt = sem("rq_step"), sem("rq_sqrt")
        s_ready, s_read, m_step, p_exp, p_step, p_norm = (sem("s_ready"), sem("s_read"), sem("m_step"), sem("p_exp"),
                                                         sem("p_step"), sem("p_norm"))
        pt_ready, ptm_done, pthi_done, ptlo_done, pv_ready = (sem("pt_ready"), sem("pt_meta_done"), sem("pt_hi_done"),
                                                             sem("pt_lo_done"), sem("pv_ready"))
        ohi_done, olo_done = sem("o_hi_done"), sem("o_lo_done")
        outT_ready, out_sb, out_sent = sem("out_turned"), sem("out_copied"), [sem("out_sent0"), sem("out_sent1")]

        v_low, gqk_done = sem("v_low_done"), sem("gqk_done")
        n_k = (1 + TILES) * KV
        tmp2k = tmp[:, :, :].rearrange("p a t -> p (a t)")[:, 0:n_k]
        v_meta = tmp[:, :, :].rearrange("p a t -> p (a t)")[:, n_k:n_k + KV]

        sq_many = [sq[:, 0, :], sq[:, 1, :]] + [tmp[:, b, :] for b in range(4)] + [ca[:, :], cb[:, :]]

        block = ctx.enter_context(nc.Block())

        def n_of(qd, c):
            return qd * SLOTS + c

        def slot_bank(o):
            return 2 * (o % 2)

        def pair_view(bank, cols=None):
            return ps[:, bank:bank + 2, 0:HALF]

        def two(ap):
            return ap.rearrange("p (b n) -> p b n", b=2)

        def quad_loop(eng, start, count, body):
            body(start, True)
            if count > 1:
                with eng.Fori(start + 1, start + count) as qd:
                    body(qd, False)

        blocks_before = [0]
        for _, _, i_ in units:
            blocks_before.append(blocks_before[-1] + (1 if i_ == 0 else 2))

        def keys_of(i):
            return META + (P if i == 0 else 2 * P)

        def q_of(a):
            return (q0, q1)[a]

        def steps_before(r):
            return sum(STEPS[:r])

        def roots_before(r):
            return sum(1 for s in STEPS[:r] if s > 1)

        @block.sync
        def _(sp):
            sp.dma_start(meta_tok[:, :], meta_tokens).then_inc(x_in[0], 16)
            for i in range(TILES):
                sp.dma_start(x_tok[:, i, :], x[0, i * P:(i + 1) * P, :]).then_inc(x_in[1 + i], 16)

            def col_of(i):
                return i * P if isinstance(i, int) else sp.snap(i * P)

            def load(qd, c, src, k):
                if not (isinstance(qd, int) and qd == 0):
                    sp.wait_ge(lo_done, n_of(qd, c) - SLOTS + 1)
                sp.dma_start(raw[:, c, 0:k * P].rearrange("p (k n) -> p k n", k=k), src).then_inc(landed[c], 16)

            w_in = conv_w_in[0].rearrange("(k p) n -> p k n", p=P)

            def conv_in(qd, first):
                for c in range(SLOTS):
                    ct = (qd - Q_IN) * 2 + c // 2
                    col = col_of(ct + (KT if c % 2 == 0 else 0))
                    load(qd, c, w_in[:, :, bass.ds(col, P)], KT)
            quad_loop(sp, Q_IN, 4, conv_in)

            for dst, src in ((gk, k_norm), (gq, q_norm[0]), (sinks, attn_sinks[0])):
                n = src.shape[0]
                sp.dma_start(dst[:, :], src.rearrange("(a n) -> a n", a=1).broadcast_to([P, n]))\
                   .then_inc(sink_in, 16)

            w_out = conv_w_out[0].rearrange("(k p) n -> p k n", p=P)
            for m in range(KT):
                load(Q_CO + m // 4, m % 4, w_out[:, :, m * P:(m + 1) * P], KT)

            def ffn(L, s):
                gate = ffn_w_gate[L].rearrange("(k p) n -> p k n", p=P)
                up = ffn_w_up[L].rearrange("(k p) n -> p k n", p=P)
                down = ffn_w_down[L].rearrange("(k p) n -> p k n", p=P)
                f0 = s * FH[0]

                def gu(qd, first):
                    for c in range(SLOTS):
                        col = col_of((qd - Q_GU[L][s]) * 2 + c // 2 + f0)
                        load(qd, c, (gate if c % 2 == 0 else up)[:, :, bass.ds(col, P)], KT)

                def dn(qd, first):
                    for c in range(SLOTS):
                        col = col_of((qd - Q_DN[L][s]) * 2 + c // 2)
                        k0 = f0 + (c % 2) * PARTS[s]
                        load(qd, c, down[:, k0:k0 + PARTS[s], bass.ds(col, P)], PARTS[s])
                quad_loop(sp, Q_GU[L][s], FH[s] // 2, gu)
                quad_loop(sp, Q_DN[L][s], KT // 2, dn)

            ffn(0, 0)
            ffn(0, 1)

            w_q_v = w_q[0].rearrange("(k p) (g r d) -> g r p k d", p=P, g=GROUPS, r=PER)

            def load_q(a):
                for r in range(PER):
                    sp.wait_ge(lo_done, n_of((Q_Q0, Q_Q1)[a], r) - SLOTS + 1)
                    dst = raw[:, r, :].rearrange("p (k n) -> p k n", k=KT)
                    for b in range(2):
                        sp.dma_start(dst[:, :, b * DH:(b + 1) * DH], w_q_v[2 * a + b, r])\
                          .then_inc((landed, landed2)[b][r], 16)

            load_q(0)
            w_kv_v = w_kv.rearrange("(k p) n -> p k n", p=P)
            for c in range(SLOTS):
                sp.wait_ge(lo_done, n_of(Q_KV, c) - SLOTS + 1)
                sp.dma_start(raw[:, c, :].rearrange("p (k n) -> p k n", k=2), w_kv_v[:, 2 * c:2 * c + 2, :])\
                  .then_inc(landed[c], 16)
            load_q(1)

            w_o_v = w_o[0].rearrange("(a b r d) n -> b a d r n", a=PAIRS, b=2, r=PER)
            for m in range(KT):
                c = m % 4
                sp.wait_ge(lo_done, n_of(Q_O + m // 4, c) - SLOTS + 1)
                for b in range(2):
                    for a in range(PAIRS):
                        dst = raw[b * DH:(b + 1) * DH, c, a * PER * P:(a + 1) * PER * P]
                        sp.dma_start(dst.rearrange("p (r n) -> p r n", r=PER), w_o_v[b, a, :, :, m * P:(m + 1) * P])\
                          .then_inc((landed if a == b == 0 else landed2)[c], 16)

            ffn(1, 0)
            ffn(1, 1)

        @block.scalar
        def _(act):
            for name, src in (("mix0", norm_mix), ("b_in", conv_b_in), ("ffn0", norm_ffn), ("ln_g", conv_ln_g),
                              ("ln_b", conv_ln_b), ("b_out", conv_b_out),
                              ("kv", kv_norm.rearrange("(a n) -> a n", a=1))):
                v = src.rearrange("a (k p) -> (a k) p", p=P)
                act.dma_start(par_rows[rows[name]:rows[name] + v.shape[0], :], v).then_inc(par_in, 16)
            act.dma_start(dw_rows[:, :], conv_dw[0]).then_inc(dwr_in, 16)

            def hi(qd, c):
                qd, c = (qd + c // SLOTS, c % SLOTS)
                static = isinstance(qd, int)
                if static and qd >= QUADS:
                    return
                act.wait_ge(landed[c], 16 * (qd + 1))
                if static and qd in (Q_Q0, Q_Q1):
                    act.wait_ge(landed2[c], 16 * (1 + (qd == Q_Q1)))
                if static and Q_O <= qd < Q_O + 2:
                    act.wait_ge(landed2[c], 16 * (2 + 3 * (qd - Q_O + 1)))
                if not (static and qd == 0):
                    act.wait_ge(used, n_of(qd, c) - SLOTS + 1)
                act.activation(w_hi[:, c, :], raw[:, c, :], ACT.Copy).then_inc(hi_done, 1)

            def square(r, k, src, ready, count):
                act.wait_ge(ready, count)
                if k >= 2:
                    act.wait_ge(acc_added, ADDED[r] + k - 1)
                return act.activation(sq[:, k % 2, :], src, ACT.Square).then_inc(sq_done, 1)

            def prep(r, k, gain, ready, count):
                square(r, k, h[:, k, :], ready, count)
                act.activation(act_hi[:, k, :], h[:, k, :], ACT.Copy,
                               scale=par[:, rows[gain] + k:rows[gain] + k + 1]).then_inc(ahi_done, 1)

            def stat_root(r):
                act.wait_ge(st_step, steps_before(r) + 1)
                act.activation(tmp[:, 3, :], tmp[:, 2, :], ACT.Ln).then_inc(st_root, 1)
                act.wait_ge(st_root, 2 * roots_before(r) + 1)
                act.activation(rb[:, :], tmp[:, 3, :], ACT.Exp, scale=-0.5).then_inc(st_root, 1)

            def diagonals(ct, e):
                if isinstance(ct, int) and ct == 0:
                    act.wait_ge(dw_split, 2)
                if not (isinstance(ct, int) and ct < 2):
                    act.wait_ge(taps_pe, ct - 1)
                for dst, src in ((dg_hi, dw_hi), (dg_lo, dw_lo)):
                    for w in range(PE_TAPS):
                        tapw = src[:, bass.ds(ct, 1), PE0 + w:PE0 + w + 1].bitcast(F32)
                        act.activation(dst[:, e % 2, w, :], ident[:, :], ACT.Copy,
                                       scale=tapw.rearrange("p a w -> p (a w)")).then_inc(dg_done, 1)

            for c in range(LAG_HI):
                hi(0, c)
            act.wait_ge(turned_out, 2 + 2 * TILES)
            for k in range(KT):
                act.activation(act_hi[:, k, :], h[:, k, :], ACT.Copy,
                               scale=par[:, rows["mix0"] + k:rows["mix0"] + k + 1]).then_inc(ahi_done, 1)
            act.wait_ge(turned_out, 3 + 2 * TILES)
            act.activation(dw_hi[:, :, 0:TAPS], dw[:, :, 0:TAPS], ACT.Copy).then_inc(dw_split, 1)
            for k in range(KT):
                act.activation(sq_many[k], h[:, k, :], ACT.Square).then_inc(sq_done, 1)
            diagonals(0, 0)
            stat_root(R_MIX0)

            def gate(ct, e):
                act.wait_ge(slot_free, O_IN + 2 * ct + 1)
                if not (isinstance(ct, int) and ct == 0):
                    act.wait_ge(a_done, ct)
                act.activation(tmp[:, 1, :], tmp[:, 0, :], ACT.Sigmoid,
                               bias=par[:, bass.ds(rows["b_in"] + KT + ct, 1)]).then_inc(sig_done, 1)
                if not (isinstance(ct, int) and ct == 0):
                    diagonals(ct, e)

            def last_diagonals():
                act.wait_ge(taps_pe, KT - 1)
                for dst, src in ((dg_hi, dw_hi), (dg_lo, dw_lo)):
                    for w in range(LAST_TAPS):
                        act.activation(dst[:, 0, w, :], ident[:, :], ACT.Copy,
                                       scale=src[:, KT - 1, LAST0 + w:LAST0 + w + 1].bitcast(F32))\
                           .then_inc(dg_done, 1)

            def keep(qd, e):
                ct = (qd - Q_IN) * 2 + e
                act.wait_ge(c_sum, ct + 1)
                act.activation(conv[:, bass.ds(ct, 1), :].rearrange("p a t -> p (a t)"), cp[:, e % 2, :], ACT.Copy)\
                   .then_inc(c_done, 1)

            def conv_in(qd, first):
                for e in range(2):
                    ct = (qd - Q_IN) * 2 + e
                    act.wait_ge(a_done, ct + 1)
                    act.activation(a_hi[:, e, :], apad[:, :], ACT.Copy).then_inc(cahi_done, 1)
                    hi(qd, 2 * e + LAG_HI)
                    for w in range(AP_TAPS):
                        if not (first and e == 0 and w < 2):
                            n = (AP_TAPS - 1) * ct
                            act.wait_ge(prod_added, n if w < 2 else n + w - 2 + (w == 2))
                        tapw = dw[:, bass.ds(ct, 1), AP0 + w:AP0 + w + 1].rearrange("p a w -> p (a w)")
                        act.activation(prod[:, w % 2, :], apad[:, AP0 + w:AP0 + w + T], ACT.Copy, scale=tapw)\
                           .then_inc(prod_done, 1)
                        if w == 1 and isinstance(ct, int) and ct == KT - 1:
                            last_diagonals()
                    if not (first and e == 0):
                        keep(qd, e - 1)
                    hi(qd, 2 * e + 1 + LAG_HI)
                    if not (isinstance(ct, int) and ct == KT - 1):
                        gate(ct + 1, e + 1)
            gate(0, 0)
            conv_in(Q_IN, True)
            with act.Fori(Q_IN + 1, Q_IN + 3) as qd:
                conv_in(qd, False)
            conv_in(Q_IN + 3, False)
            keep(Q_IN + 3, 1)

            for k in range(KT):
                act.wait_ge(cc_done, k + 1)
                act.activation(sq_many[k], conv[:, k, :], ACT.Square).then_inc(sq_done, 1)
            stat_root(R_VAR)
            for k in range(KT):
                act.wait_ge(ln_mul, k + 1)
                if k >= 2:
                    act.wait_ge(lnlo_done, k - 1)
                act.activation(tmp[:, k % 2, :], conv[:, k, :], ACT.Silu,
                               scale=par[:, rows["ln_g"] + k:rows["ln_g"] + k + 1],
                               bias=par[:, rows["ln_b"] + k:rows["ln_b"] + k + 1]).then_inc(ln_silu, 1)
                act.wait_ge(ln_silu, k + 1)
                act.activation(ln_hi[:, k, :], tmp[:, k % 2, :], ACT.Copy).then_inc(lnhi_done, 1)

            for m in range(KT):
                hi(Q_CO, m + LAG_HI)
                prep(R_FFN0, m, "ffn0", slot_free, O_CO + m + 1)
            stat_root(R_FFN0)

            def ffn(L, s, gain, round_):
                N = T if L == 0 else SEQ

                def hid_hi_of(qd, e):
                    fi = (qd - Q_GU[L][s]) * 2 + e
                    g = G0[L][s] + fi
                    act.wait_ge(p_done, g + 1)
                    act.activation(hid_hi[:, bass.ds(fi, 1), 0:N], tmp[:, 3:4, 0:N], ACT.Copy)\
                       .then_inc(hidhi_done, 1)

                def gu(qd, first):
                    for e in range(2):
                        fi = (qd - Q_GU[L][s]) * 2 + e
                        g = G0[L][s] + fi
                        hi(qd, 2 * e + LAG_HI)
                        act.wait_ge(slot_free, O_GU[L][s] + 2 * fi + 1)
                        if not (isinstance(g, int) and g == 0):
                            act.wait_ge(p_done, g)
                        act.activation(tmp[:, 1, 0:N], tmp[:, 0, 0:N], ACT.Silu).then_inc(silu_done, 1)
                        hi(qd, 2 * e + 1 + LAG_HI)
                        if not (first and e == 0):
                            hid_hi_of(qd, e - 1)
                quad_loop(act, Q_GU[L][s], FH[s] // 2, gu)
                hid_hi_of(Q_GU[L][s] + FH[s] // 2 - 1, 1)

                def dn(qd, first):
                    for e in range(2):
                        m = (qd - Q_DN[L][s]) * 2 + e
                        hi(qd, 2 * e + LAG_HI)
                        hi(qd, 2 * e + 1 + LAG_HI)
                        if s == 1 and L == 0:
                            act.wait_ge(slot_free, O_DN[L][s] + m + 1)
                            if not (first):
                                act.wait_ge(acc_added, ADDED[round_] + m - 1)
                            act.activation(sq[:, e, :], h[:, bass.ds(m, 1), :].rearrange("p a t -> p (a t)"),
                                           ACT.Square).then_inc(sq_done, 1)
                            act.activation(act_hi[:, bass.ds(m, 1), :], h[:, bass.ds(m, 1), :], ACT.Copy,
                                           scale=par[:, bass.ds(rows[gain] + m, 1)]).then_inc(ahi_done, 1)
                        if s == 1 and L == 1 and not (first and e == 0):
                            send(qd, e - 1, first)

                def send(qd, e, first):
                    m = (qd - Q_DN[L][s]) * 2 + e
                    z = e % 2
                    act.wait_ge(outT_ready, m + 1)
                    if not (isinstance(m, int) and m < 2):
                        act.wait_ge(out_sent[z], 16 * (m // 2))
                    act.activation(tmp[:, 2 + z, 0:SEQ], ps[:, 4 + z, :], ACT.Copy).then_inc(out_sb, 1)
                    act.wait_ge(out_sb, m + 1)
                    act.dma_start(out[0].rearrange("(i p) d -> p i d", p=P)[:, :, bass.ds(m * P, P)],
                                  tmp[:, 2 + z, 0:SEQ].rearrange("p (i n) -> p i n", i=TILES))\
                       .then_inc(out_sent[z], 16)

                if L == 1 and s == 1:
                    for qd in range(Q_DN[L][s], Q_DN[L][s] + KT // 2):
                        dn(qd, qd == Q_DN[L][s])
                    send(Q_DN[L][s] + KT // 2 - 1, 1, False)
                elif s == 1:
                    quad_loop(act, Q_DN[L][s], KT // 2 - 1, dn)
                    dn(Q_DN[L][s] + KT // 2 - 1, False)
                else:
                    quad_loop(act, Q_DN[L][s], KT // 2, dn)

            ffn(0, 0, None, None)
            ffn(0, 1, "mix1", R_MIX1)

            def q_tile(j):
                act.wait_ge(q_out, j + 1)
                if j >= 2:
                    act.wait_ge(qss_ready, j - 1)
                act.activation(sq[:, j % 2, 0:SEQ], q_of(j // PER)[:, j % PER, :], ACT.Square).then_inc(qsq_done, 1)

            def kv_high(t):
                act.wait_ge(kva_done, t + 1)
                if t >= 3:
                    act.wait_ge(kv_ready, t - 2)
                act.activation(kva_hi[:, t % 3], kva[:, t % 3], ACT.Copy).then_inc(kvahi_done, 1)

            def v_high(t):
                if t < TILES:
                    act.wait_ge(kv_ready, t + 1)
                else:
                    act.wait_ge(used, n_of(Q_KV, SLOTS))
                if t == 0:
                    act.wait_ge(tok_done, 1)
                act.activation(v_hi[:, t, :], ps[:, 4 + t % 3, KV:2 * KV], ACT.Copy,
                               scale=rms_tok[:, t:t + 1]).then_inc(vhi_done, 1)

            hi(Q_Q0, LAG_HI)
            for t in range(3):
                kv_high(t)
            stat_root(R_MIX1)
            for c in range(LAG_HI):
                hi(Q_KV, c)
            hi(Q_KV, LAG_HI)
            q_tile(0)
            q_tile(1)
            q_tile(2)
            q_tile(3)
            v_high(0)
            kv_high(3)
            v_high(1)
            kv_high(4)
            v_high(2)
            for c in range(LAG_HI):
                hi(Q_Q1, c)
            v_high(3)
            v_high(4)
            hi(Q_Q1, LAG_HI)
            act.wait_ge(kx_done, 1 + TILES)
            act.activation(tmp2k, kx[:, :, :].rearrange("p t n -> p (t n)"), ACT.Square).then_inc(ksq_done, 1)
            act.wait_ge(k_step, 2)
            act.activation(rk[:, 1, :], rk[:, 0, :], ACT.Sqrt).then_inc(k_sqrt, 1)

            def q_sqrt(a):
                act.wait_ge(rq_step, 7 * a + 1)
                act.activation(rq[:, 1, :], rq[:, 0, :], ACT.Sqrt).then_inc(rq_sqrt, 1)

            def exps(u):
                a, b, i = units[u]
                n, w = keys_of(i), u % BUFS
                act.wait_ge(m_step, 4 * (u + 1))
                for r in range(PER):
                    act.activation(s_sb[:, w, r, 0:n], s_sb[:, w, r, 0:n], ACT.Exp, bias=smx[:, w, 3, r:r + 1],
                                   scale=rqs[:, a, r, i, b:b + 1], accum_out=smx[:, w, 6, r:r + 1]).then_inc(p_exp, 1)
                act.activation(smx[:, w, 5, :], smx[:, w, 4, :], ACT.Exp).then_inc(p_exp, 1)

            def pt_high(u):
                a, b, i = units[u]
                act.wait_ge(pt_ready, u + 1)
                if u >= 2:
                    act.wait_ge(pv_ready, u - 1)
                act.activation(pt_hi[:, u % 2, 1, :], ps[:, 5, :], ACT.Copy).then_inc(pthi_done, 1)
                if i > 0:
                    act.activation(pt_hi[:, u % 2, 0, :], ps[:, 4, :], ACT.Copy).then_inc(pthi_done, 1)
                act.activation(sq[0:META, u % 2, 0:PER * P], ps[0:META, 6, :], ACT.Copy).then_inc(ptm_done, 1)

            def o_high(u):
                a, b, i = units[u]
                rowsel = slice(b * DH, (b + 1) * DH)
                act.wait_ge(pv_ready, u + 1)
                act.activation((o0_hi, o1_hi)[a][rowsel, :, i * P:(i + 1) * P],
                               ps[rowsel, 7, :].rearrange("p (r n) -> p r n", r=PER), ACT.Copy).then_inc(ohi_done, 1)

            q_sqrt(0)
            for j in range(PER, QJ - 1):
                q_tile(j)
                hi(Q_O, j - PER)
            exps(0)
            q_tile(QJ - 1)
            q_sqrt(1)
            exps(1)
            for u in range(NU):
                pt_high(u)
                if u >= 1:
                    o_high(u - 1)
                if u + 2 < NU:
                    exps(u + 2)
            o_high(NU - 1)

            for m in range(KT):
                hi(Q_O, m + LAG_HI)
                prep(R_FFN1, m, "ffn1", slot_free, O_O + m + 1)
            stat_root(R_FFN1)
            ffn(1, 0, None, None)
            ffn(1, 1, None, None)
            for e in range(2):
                act.wait_ge(out_sent[e], 16 * (KT // 2))

        @block.gpsimd
        def _(pool):
            pool.memset(ident[:, :], 0.0).then_inc(consts, 1)
            pool.memset(ones[:, :], 1.0).then_inc(consts, 1)
            pool.memset(blk2[:, :], 1.0).then_inc(consts, 1)
            pool.memset(mask_a[:, :], 0.0).then_inc(consts, 1)
            pool.memset(mask_b[:, :], 0.0).then_inc(consts, 1)
            pool.memset(apad[:, 0:PAD], 0.0).then_inc(consts, 1)
            pool.wait_ge(consts, 6)
            pool.affine_select(out=ident[:, :], in_=ident[:, :], compare_op=ALU.not_equal, fill=1.0, base=0,
                               pattern=[[-1, P]], channel_multiplier=1).then_inc(consts, 1)
            pool.affine_select(out=blk2[:, :], in_=blk2[:, :], compare_op=ALU.is_ge, fill=0.0, base=0,
                               pattern=[[-DH, 2]], channel_multiplier=1).then_inc(consts, 1)
            pool.wait_ge(consts, 8)
            pool.affine_select(out=blk2[:, :], in_=blk2[:, :], compare_op=ALU.is_ge, fill=0.0, base=DH - 1,
                               pattern=[[DH, 2]], channel_multiplier=-1).then_inc(consts, 1)
            for m_, at_ in ((mask_a, 0), (mask_b, META)):
                pool.affine_select(out=m_[:, at_:at_ + P], in_=m_[:, at_:at_ + P], compare_op=ALU.is_ge, fill=NEG,
                                   base=-1, pattern=[[1, P]], channel_multiplier=-1).then_inc(consts, 1)
            for m_, at_ in ((mask_a, P + META), (mask_b, META + P)):
                pool.affine_select(out=m_[:, at_:at_ + P], in_=m_[:, at_:at_ + P], compare_op=ALU.is_ge, fill=NEG,
                                   base=0, pattern=[[-1, P]], channel_multiplier=1).then_inc(consts, 1)

            def lo(qd, c):
                qd, c = (qd + c // SLOTS, c % SLOTS)
                if isinstance(qd, int) and qd >= QUADS:
                    return
                pool.wait_ge(hi_done, n_of(qd, c) + 1)
                pool.tensor_tensor(w_lo[:, c, :], raw[:, c, :], w_hi[:, c, :].bitcast(F32), ALU.subtract)\
                    .then_inc(lo_done, 1)

            def zero(r):
                pool.wait_ge(st_ready, ACCS[ACCS.index(r) - 1] + 1)
                pool.memset(acc[:, :], 0.0).then_inc(zeroed, 1)

            def add(r, k, src, ready, count):
                pool.wait_ge(ready, count)
                if isinstance(k, int) and k == 0:
                    pool.wait_ge(zeroed, ACCS.index(r))
                else:
                    pool.wait_ge(acc_added, ADDED[r] + k)
                pool.tensor_tensor(acc[:, :], acc[:, :], src, ALU.add).then_inc(acc_added, 1)

            def add_square(r, k):
                add(r, k, sq[:, k % 2, :], sq_done, 8 * SQ0[r] + k + 1)

            for c in range(LAG_LO + 1):
                lo(0, c)

            def conv_in(qd, first):
                for e in range(2):
                    ct = (qd - Q_IN) * 2 + e
                    last = isinstance(ct, int) and ct == KT - 1
                    for w in range(1, AP_TAPS):
                        if w == 3 and not last:
                            lo(qd, 2 * e + 1 + LAG_LO)
                        pool.wait_ge(prod_done, AP_TAPS * ct + w + 1)
                        if w == 1:
                            if not first:
                                pool.wait_ge(c_done, ct - 1)
                                pool.wait_ge(acc_added, ADDED[R_MEAN] + ct - 1)
                            pool.tensor_tensor(cp[:, e, :], prod[:, 0, :], prod[:, 1, :], ALU.add)\
                                .then_inc(prod_added, 1)
                        else:
                            pool.wait_ge(prod_added, (AP_TAPS - 1) * ct + w - 1)
                            pool.tensor_tensor(cp[:, e, :], cp[:, e, :], prod[:, w % 2, :], ALU.add)\
                                .then_inc(prod_added, 1)
                    if not last:
                        lo(qd, 2 * e + 2 + LAG_LO)
                    pool.wait_ge(prod_added, (AP_TAPS - 1) * (ct + 1))
                    pool.wait_ge(t_done, ct + 1)
                    pool.tensor_tensor(cp[:, e, :], ca[:, :], cp[:, e, :], ALU.add).then_inc(c_sum, 1)
                    if first and e == 0:
                        zero(R_MEAN)
                    if not (isinstance(ct, int) and ct == KT - 1):
                        add(R_MEAN, ct, cp[:, e, :], c_sum, ct + 1)
            conv_in(Q_IN, True)
            with pool.Fori(Q_IN + 1, Q_IN + 3) as qd:
                conv_in(qd, False)
            conv_in(Q_IN + 3, False)
            for m in range(-1, 1):
                lo(Q_CO, m + LAG_LO)
            zero(R_FFN0)
            for m in range(KT):
                if m > 0:
                    lo(Q_CO, m + LAG_LO)
                add_square(R_FFN0, m)

            def ffn(L, s, round_):
                N = T if L == 0 else SEQ

                def gu(qd, first):
                    for e in range(2):
                        fi = (qd - Q_GU[L][s]) * 2 + e
                        g = G0[L][s] + fi
                        lo(qd, 2 * e + LAG_LO)
                        lo(qd, 2 * e + 1 + LAG_LO)
                        pool.wait_ge(silu_done, g + 1)
                        pool.wait_ge(slot_free, O_GU[L][s] + 2 * fi + 2)
                        if not (isinstance(g, int) and g == 0):
                            pool.wait_ge(hidlo_done, g)
                        pool.tensor_tensor(tmp[:, 3, 0:N], tmp[:, 1, 0:N], tmp[:, 2, 0:N], ALU.mult)\
                            .then_inc(p_done, 1)
                quad_loop(pool, Q_GU[L][s], FH[s] // 2, gu)

                def dn(qd, first):
                    for e in range(2):
                        m = (qd - Q_DN[L][s]) * 2 + e
                        lo(qd, 2 * e + LAG_LO)
                        lo(qd, 2 * e + 1 + LAG_LO)
                        if L == 0 and s == 1:
                            add(round_, m, sq[:, e, :], sq_done, 8 * SQ0[round_] + m + 1)
                if L == 1 and s == 1:
                    dn(Q_DN[L][s], True)
                    with pool.Fori(Q_DN[L][s] + 1, Q_DN[L][s] + KT // 2 - 1) as qd:
                        dn(qd, False)
                    dn(Q_DN[L][s] + KT // 2 - 1, False)
                else:
                    quad_loop(pool, Q_DN[L][s], KT // 2, dn)

            ffn(0, 0, None)
            zero(R_MIX1)
            ffn(0, 1, R_MIX1)
            for qd in (Q_Q0, Q_KV, Q_Q1):
                for c in range(SLOTS):
                    lo(qd, c + LAG_LO)
            for u in range(NU):
                a, b, i = units[u]
                n, w = keys_of(i), u % BUFS
                pool.wait_ge(p_step, 2 * (u + 1))
                pool.tensor_tensor(s_sb[:, w, :, 0:n], s_sb[:, w, :, 0:n],
                                   smx[:, w, 7, :].unsqueeze(2).broadcast_to([P, PER, n]), ALU.mult)\
                    .then_inc(p_norm, 1)
            for m in range(KT):
                if m == 0:
                    zero(R_FFN1)
                lo(Q_O, m + LAG_LO)
                add_square(R_FFN1, m)
            ffn(1, 0, None)
            ffn(1, 1, None)

        @block.vector
        def _(dve):
            dve.wait_ge(turned, 1)
            dve.tensor_copy(h[:, :, 0:META], ps[:, 0, 0:KT * META].rearrange("p (k n) -> p k n", k=KT))\
               .then_inc(turned_out, 1)
            for g in range(2 * TILES):
                i, kh = g // 2, g % 2
                dve.wait_ge(turned, 2 + g)
                dve.tensor_copy(h[:, 4 * kh:4 * kh + 4, META + i * P:META + (i + 1) * P],
                                ps[:, (g + 1) % 4, :].rearrange("p (k n) -> p k n", k=4)).then_inc(turned_out, 1)
            dve.wait_ge(turned, 2 + 2 * TILES)
            dve.tensor_copy(par[:, :], ps[:, 4, 0:NROWS]).then_inc(turned_out, 1)
            dve.wait_ge(turned, 3 + 2 * TILES)
            dve.tensor_copy(dw[:, :, 0:TAPS], ps[:, 5, 0:KT * 32].rearrange("p (k w) -> p k w", w=32)[:, :, 0:TAPS])\
               .then_inc(turned_out, 1)

            def prep(r, k, gain):
                dve.wait_ge(ahi_done, 8 * PREP[r] + k + 1)
                dve.scalar_tensor_tensor(out=act_lo[:, k, :], in0=h[:, k, :],
                                         scalar=par[:, rows[gain] + k:rows[gain] + k + 1],
                                         in1=act_hi[:, k, :].bitcast(F32), op0=ALU.mult, op1=ALU.subtract)\
                   .then_inc(alo_done, 1)

            def newton(s, step, base, sqrt_sem, sqrt_count, ms, sd, r, t, res, last=None):
                dve.wait_ge(sqrt_sem, sqrt_count)
                dve.reciprocal(r, sd).then_inc(step, 1)
                dve.wait_ge(step, base + 1)
                dve.tensor_tensor(t, r, r, ALU.mult).then_inc(step, 1)
                dve.wait_ge(step, base + 2)
                dve.tensor_tensor(t, t, ms, ALU.mult).then_inc(step, 1)
                dve.wait_ge(step, base + 3)
                dve.tensor_scalar(t, t, -0.5, 1.5, ALU.mult, ALU.add).then_inc(step, 1)
                dve.wait_ge(step, base + 4)
                dve.tensor_tensor(res, r, t, ALU.mult).then_inc(step, 1)

            def stats(r):
                b0 = steps_before(r)
                ms, sd = tmp[:, 2, :], tmp[:, 3, :]
                dve.wait_ge(st_ready, r + 1)
                dve.tensor_scalar(two(ms), pair_view(SUM_BANK[r]), 1.0 / D, EPS, ALU.mult, ALU.add)\
                   .then_inc(st_step, 1)
                dve.wait_ge(st_root, 2 * roots_before(r) + 2)
                dve.tensor_tensor(sd, ms, rb[:, :], ALU.mult).then_inc(st_step, 1)
                dve.wait_ge(st_step, b0 + 2)
                dve.scalar_tensor_tensor(out=sd, in0=sd, scalar=-0.5, in1=rb[:, :], op0=ALU.mult, op1=ALU.mult)\
                   .then_inc(st_step, 1)
                dve.wait_ge(st_step, b0 + 3)
                dve.scalar_tensor_tensor(out=rb[:, :], in0=sd, scalar=1.5, in1=rb[:, :], op0=ALU.add, op1=ALU.mult)\
                   .then_inc(st_step, 1)
                dve.wait_ge(st_step, b0 + 4)

            for k in range(KT):
                prep(R_MIX0, k, "mix0")
            dve.wait_ge(dw_split, 1)
            dve.tensor_tensor(dw_lo[:, :, 0:TAPS], dw[:, :, 0:TAPS], dw_hi[:, :, 0:TAPS].bitcast(F32), ALU.subtract)\
               .then_inc(dw_split, 1)
            for k in range(1, KT):
                dve.wait_ge(sq_done, k + 1)
                if k >= 2:
                    dve.wait_ge(acc_added, k - 1)
                dve.tensor_tensor(acc[:, :], sq_many[0] if k == 1 else acc[:, :], sq_many[k], ALU.add)\
                   .then_inc(acc_added, 1)
            dve.wait_ge(consts, CONSTS)
            dve.wait_ge(acc_added, KT - 1)
            stats(R_MIX0)

            rb2 = two(rb[:, :])

            def gate(ct, bank):
                dve.wait_ge(used, 2 * ct + 1)
                if not (isinstance(ct, int) and ct == 0):
                    dve.wait_ge(sig_done, ct)
                dve.tensor_tensor(two(tmp[:, 0, :]), pair_view(bank), rb2, ALU.mult).then_inc(slot_free, 1)

            def conv_in(qd, first):
                for e in range(2):
                    ct = (qd - Q_IN) * 2 + e
                    prime = first and e == 0
                    dve.wait_ge(used, 2 * ct + 2)
                    if not prime:
                        dve.wait_ge(a_done, ct)
                    dve.tensor_tensor(two(tmp[:, 2, :]), pair_view(2), rb2, ALU.mult).then_inc(slot_free, 1)
                    dve.wait_ge(sig_done, ct + 1)
                    dve.wait_ge(slot_free, O_IN + 2 * ct + 2)
                    if not prime:
                        dve.wait_ge(t_done, ct)
                        dve.wait_ge(prod_done, AP_TAPS * ct)
                    dve.scalar_tensor_tensor(out=apad[:, PAD:PAD + T], in0=tmp[:, 2, :],
                                             scalar=par[:, bass.ds(rows["b_in"] + ct, 1)], in1=tmp[:, 1, :],
                                             op0=ALU.add, op1=ALU.mult).then_inc(a_done, 1)
                    dve.wait_ge(a_done, ct + 1)

                    def tap(w):
                        dst = (ca, cb)[w % 2]
                        tapw = dw[:, bass.ds(ct, 1), w:w + 1].rearrange("p a w -> p (a w)")
                        if w < 2:
                            if w == 0 and not prime:
                                dve.wait_ge(c_sum, ct)
                            dve.tensor_scalar(dst[:, :], apad[:, w:w + T], tapw, None, ALU.mult).then_inc(tap_done, 1)
                        else:
                            dve.wait_ge(tap_done, DVE_TAPS * ct + (2 if w == 2 else w - 1))
                            dve.scalar_tensor_tensor(out=dst[:, :], in0=apad[:, w:w + T], scalar=tapw,
                                                     in1=dst[:, :], op0=ALU.mult, op1=ALU.add).then_inc(tap_done, 1)
                    for w in (1, 0, 2):
                        tap(w)
                    dve.wait_ge(cahi_done, ct + 1)
                    dve.tensor_tensor(a_lo[:, e, :], apad[:, :], a_hi[:, e, :].bitcast(F32), ALU.subtract)\
                       .then_inc(calo_done, 1)
                    last = isinstance(ct, int) and ct == KT - 1
                    for w in range(3, LAST0 if last else DVE_TAPS):
                        tap(w)
                        if w == GATE_AFTER and not last:
                            gate(ct + 1, 6 if prime else 0)
                    dve.wait_ge(taps_pe, ct + 1)
                    dve.wait_ge(tap_done, DVE_TAPS * (ct + 1) - (LAST_TAPS if last else 0))
                    dve.tensor_tensor(two(cb[:, :]), pair_view(4), two(cb[:, :]), ALU.add).then_inc(conv_mix, 1)
                    dve.wait_ge(conv_mix, ct + 1)
                    dve.tensor_tensor(ca[:, :], ca[:, :], cb[:, :], ALU.add).then_inc(t_done, 1)
            gate(0, 0)
            conv_in(Q_IN, True)
            with dve.Fori(Q_IN + 1, Q_IN + 3) as qd:
                conv_in(qd, False)
            conv_in(Q_IN + 3, False)

            dve.wait_ge(st_ready, R_MEAN + 1)
            dve.wait_ge(c_done, KT)
            for k in range(KT):
                dve.scalar_tensor_tensor(out=two(conv[:, k, :]), in0=pair_view(6), scalar=-1.0 / D,
                                         in1=two(conv[:, k, :]), op0=ALU.mult, op1=ALU.add).then_inc(cc_done, 1)
            for k in (2, 4, 6):
                dve.wait_ge(sq_done, 8 * SQ0[R_VAR] + k + 2)
                dve.tensor_tensor(sq_many[k], sq_many[k], sq_many[k + 1], ALU.add).then_inc(var_paired, 1)
            dve.wait_ge(cc_done, KT)
            stats(R_VAR)

            def ln_low(k):
                dve.wait_ge(lnhi_done, k + 1)
                dve.tensor_tensor(ln_lo[:, k, :], tmp[:, k % 2, :], ln_hi[:, k, :].bitcast(F32), ALU.subtract)\
                   .then_inc(lnlo_done, 1)
            for k in range(KT):
                dve.tensor_tensor(conv[:, k, :], conv[:, k, :], rb[:, :], ALU.mult).then_inc(ln_mul, 1)
                if k >= 2:
                    ln_low(k - 2)
            dve.wait_ge(ln_mul, KT)
            ln_low(KT - 2)
            ln_low(KT - 1)

            for m in range(KT):
                dve.wait_ge(used, n_of(Q_CO, m) + 1)
                dve.scalar_tensor_tensor(out=two(h[:, m, :]), in0=pair_view(slot_bank(O_CO + m)),
                                         scalar=par[:, rows["b_out"] + m:rows["b_out"] + m + 1], in1=two(h[:, m, :]),
                                         op0=ALU.add, op1=ALU.add).then_inc(slot_free, 1)
                if m >= 1:
                    prep(R_FFN0, m - 1, "ffn0")
            prep(R_FFN0, KT - 1, "ffn0")
            stats(R_FFN0)

            def ffn(L, s, gain, round_):
                N = T if L == 0 else SEQ
                if L == 0:
                    view = lambda ap: two(ap)
                    bank = lambda b: pair_view(b)
                    rbv = rb2
                else:
                    view = lambda ap: ap
                    bank = lambda b: ps[:, b, :]
                    rbv = rb[:, META:T]

                def low(qd, e):
                    fi = (qd - Q_GU[L][s]) * 2 + e
                    g = G0[L][s] + fi
                    dve.wait_ge(hidhi_done, g + 1)
                    dve.tensor_tensor(hid_lo[:, bass.ds(fi, 1), 0:N], tmp[:, 3:4, 0:N],
                                      hid_hi[:, bass.ds(fi, 1), 0:N].bitcast(F32), ALU.subtract)\
                       .then_inc(hidlo_done, 1)

                def gu(qd, first):
                    for e in range(2):
                        fi = (qd - Q_GU[L][s]) * 2 + e
                        g = G0[L][s] + fi
                        dve.wait_ge(used, n_of(qd, 2 * e) + 1)
                        if not (isinstance(g, int) and g == 0):
                            dve.wait_ge(silu_done, g)
                        dve.tensor_tensor(view(tmp[:, 0, 0:N]), bank(4 if first and s == 0 and e == 1 else 0), rbv,
                                          ALU.mult).then_inc(slot_free, 1)
                        if not (first and e == 0):
                            low(qd, e - 1)
                        dve.wait_ge(used, n_of(qd, 2 * e + 1) + 1)
                        if not (isinstance(g, int) and g == 0):
                            dve.wait_ge(p_done, g)
                        dve.tensor_tensor(view(tmp[:, 2, 0:N]), bank(2), rbv, ALU.mult).then_inc(slot_free, 1)
                quad_loop(dve, Q_GU[L][s], FH[s] // 2, gu)
                low(Q_GU[L][s] + FH[s] // 2 - 1, 1)

                def prep_m(qd, e):
                    m = (qd - Q_DN[L][s]) * 2 + e
                    dve.wait_ge(ahi_done, 8 * PREP[round_] + m + 1)
                    dve.scalar_tensor_tensor(out=act_lo[:, bass.ds(m, 1), :], in0=h[:, bass.ds(m, 1), :],
                                             scalar=par[:, bass.ds(rows[gain] + m, 1)],
                                             in1=act_hi[:, bass.ds(m, 1), :].bitcast(F32), op0=ALU.mult,
                                             op1=ALU.subtract).then_inc(alo_done, 1)

                def dn(qd, first):
                    for e in range(2):
                        m = (qd - Q_DN[L][s]) * 2 + e
                        dve.wait_ge(used, n_of(qd, 2 * e + 1) + 1)
                        src = h[:, bass.ds(m, 1), T - N:T].rearrange("p a t -> p (a t)")
                        if L == 1 and s == 1:
                            if not first:
                                dve.wait_ge(outT_ready, m - 1)
                            dst = tmp[:, e, 0:N]
                        else:
                            dst = src
                        dve.tensor_tensor(view(dst), bank(2 * e), view(src), ALU.add).then_inc(slot_free, 1)
                        if round_ is not None and not (first and e == 0):
                            prep_m(qd, e - 1)
                quad_loop(dve, Q_DN[L][s], KT // 2, dn)
                if round_ is not None:
                    prep_m(Q_DN[L][s] + KT // 2 - 1, 1)

            ffn(0, 0, None, None)
            ffn(0, 1, "mix1", R_MIX1)

            def tok(t):
                return slice(0, P) if t == 0 else slice(META + (t - 1) * P, META + t * P)

            def kv_in(t):
                if t >= 3:
                    dve.wait_ge(kvahi_done, t - 2)
                    dve.wait_ge(kvalo_done, t - 2)
                g = par[:, rows["kv"]:rows["kv"] + KT].unsqueeze(2).broadcast_to([P, KT, P])
                dve.tensor_tensor(kva[:, t % 3], h[:, :, tok(t)], g, ALU.mult).then_inc(kva_done, 1)

            def kv_low(t):
                dve.wait_ge(kvahi_done, t + 1)
                dve.tensor_tensor(kva_lo[:, t % 3], kva[:, t % 3], kva_hi[:, t % 3].bitcast(F32), ALU.subtract)\
                   .then_inc(kvalo_done, 1)

            def kv_out(t):
                src = ps[:, 4 + t % 3, :]
                dve.wait_ge(vhi_done, t + 1)
                dve.scalar_tensor_tensor(out=v_lo[:, t, :], in0=src[:, KV:2 * KV], scalar=rms_tok[:, t:t + 1],
                                         in1=v_hi[:, t, :].bitcast(F32), op0=ALU.mult, op1=ALU.subtract)\
                   .then_inc(v_low, 1)
                if t == 0:
                    dve.tensor_scalar(v_meta[0:META, :], src[0:META, KV:2 * KV], rms_tok[0:META, 0:1], None,
                                      ALU.mult).then_inc(v_low, 1)
                dve.tensor_scalar(kx[:, t, :], src[:, 0:KV], rms_tok[:, t:t + 1], None, ALU.mult)\
                   .then_inc(kx_done, 1)

            def q_scale(j):
                dve.wait_ge(used, n_of((Q_Q0, Q_Q1)[j // PER], j % PER) + 1)
                dve.tensor_tensor(q_of(j // PER)[:, j % PER, :], ps[:, Q_BANKS[j], :], rb[:, META:T], ALU.mult)\
                   .then_inc(q_out, 1)

            def q_norms(a):
                n = 2 * TILES * PER
                dve.wait_ge(qss_ready, PER * (a + 1))
                dve.tensor_scalar(rq[:, 0, :], ps[:, 7, 0:n], 1.0 / DH, EPS, ALU.mult, ALU.add).then_inc(rq_step, 1)
                newton(None, rq_step, 7 * a + 1, rq_sqrt, a + 1, rq[:, 0, :], rq[:, 1, :], rq[:, 2, :], rq[:, 3, :],
                       rq[:, 4, :])
                dve.wait_ge(rq_step, 7 * a + 6)
                dve.tensor_scalar(rqs[:, a].rearrange("p r i b -> p (r i b)"), rq[:, 4, :], DH ** -0.5, None,
                                  ALU.mult).then_inc(rq_step, 1)
                dve.wait_ge(rq_step, 7 * (a + 1))

            for t in range(3):
                kv_in(t)
                if t >= 1:
                    kv_low(t - 1)
            kv_low(2)
            stats(R_MIX1)
            dve.wait_ge(tok_ready, 1)
            dve.tensor_copy(rms_tok[:, :], ps[:, 7, P:P + 1 + TILES]).then_inc(tok_done, 1)
            dve.wait_ge(tok_done, 1)
            for j in range(PER):
                q_scale(j)
            dve.wait_ge(sink_in, 48)
            dve.tensor_tensor(gqk[:, :], gk[:, :], gq[:, :], ALU.mult).then_inc(gqk_done, 1)
            for t in range(1 + TILES):
                kv_out(t)
                if t + 3 <= TILES:
                    kv_in(t + 3)
                    kv_low(t + 3)

            dve.wait_ge(ksq_done, 1)
            dve.tensor_reduce(rk[:, 3, :], tmp2k.rearrange("p (t d) -> p t d", d=DH), AX_X, ALU.add)\
               .then_inc(k_step, 1)
            dve.wait_ge(k_step, 1)
            dve.tensor_scalar(rk[:, 0, :], rk[:, 3, :], 1.0 / DH, EPS, ALU.mult, ALU.add).then_inc(k_step, 1)
            q_scale(PER)
            newton(None, k_step, 2, k_sqrt, 1, rk[:, 0, :], rk[:, 1, :], rk[:, 2, :], rk[:, 3, :], rk[:, 4, :])
            dve.wait_ge(k_step, 7)
            k3 = kx[:, :, :].rearrange("p t (g d) -> p (t g) d", d=DH)
            NG = (1 + TILES) * GROUPS
            dve.tensor_tensor(k3, k3, rk[:, 4, :].unsqueeze(2).broadcast_to([P, NG, DH]), ALU.mult)\
               .then_inc(k_step, 1)
            dve.wait_ge(k_step, 8)
            dve.wait_ge(gqk_done, 1)
            dve.tensor_tensor(k3, k3, gqk[:, :].unsqueeze(1).broadcast_to([P, NG, DH]), ALU.mult)\
               .then_inc(k_step, 1)
            q_norms(0)
            q_scale(PER + 1)
            q_scale(PER + 2)
            dve.wait_ge(kt_ready, 1)
            for a in range(PAIRS):
                for i in range(TILES):
                    dve.tensor_copy(kt[:, a, TILE_AT[i]:TILE_AT[i] + P], ps[:, 4 + a, i * P:(i + 1) * P])\
                       .then_inc(kt_done, 1)
                for at_ in META_AT:
                    dve.tensor_copy(kt[:, a, at_:at_ + META], ps[:, 6, a * P:a * P + META]).then_inc(kt_done, 1)


            def scores(u):
                a, b, i = units[u]
                w, n = u % BUFS, keys_of(i)
                m_ = {0: mask_a[:, P + META:2 * P + 2 * META], 2: mask_b[:, :]}.get(i, mask_a[:, 0:2 * P + META])
                if u >= BUFS:
                    dve.wait_ge(pt_ready, u - BUFS + 1)
                for r in range(PER):
                    dve.wait_ge(s_ready, PER * u + r + 1)
                    dve.tensor_tensor_reduce(out=s_sb[:, w, r, 0:n], in0=ps[:, S_BANKS[r], 0:n],
                                             in1=m_, scale=1.0, scalar=-3.0e38,
                                             op0=ALU.add, op1=ALU.max, accum_out=smx[:, w, 0, r:r + 1])\
                       .then_inc(s_read, 1)

            def maxima(u):
                a, b, i = units[u]
                w = u % BUFS
                sink = sinks[:, (2 * a + b) * PER:(2 * a + b + 1) * PER]
                dve.wait_ge(s_read, 4 * (u + 1))
                dve.tensor_tensor(smx[:, w, 1, :], smx[:, w, 0, :], rqs[:, a, :, i, b], ALU.mult).then_inc(m_step, 1)
                dve.wait_ge(m_step, 4 * u + 1)
                dve.tensor_tensor(smx[:, w, 2, :], smx[:, w, 1, :], sink, ALU.max).then_inc(m_step, 1)
                dve.wait_ge(m_step, 4 * u + 2)
                dve.tensor_scalar(smx[:, w, 3, :], smx[:, w, 2, :], -1.0, None, ALU.mult).then_inc(m_step, 1)
                dve.wait_ge(m_step, 4 * u + 3)
                dve.tensor_tensor(smx[:, w, 4, :], smx[:, w, 3, :], sink, ALU.add).then_inc(m_step, 1)

            def denominators(u):
                w = u % BUFS
                dve.wait_ge(p_exp, 5 * (u + 1))
                if u >= BUFS:
                    dve.wait_ge(p_norm, u - BUFS + 1)
                dve.tensor_tensor(sden[:, w, :], smx[:, w, 6, :], smx[:, w, 5, :], ALU.add).then_inc(p_step, 1)
                dve.wait_ge(p_step, 2 * u + 1)
                dve.reciprocal(smx[:, w, 7, :], sden[:, w, :]).then_inc(p_step, 1)

            def pt_low(u):
                a, b, i = units[u]
                n = blocks_before[u]
                for z in (1, 0)[:1 if i == 0 else 2]:
                    n += 1
                    dve.wait_ge(pthi_done, n)
                    dve.tensor_tensor(pt_lo[:, u % 2, z, :], ps[:, 4 + z, :], pt_hi[:, u % 2, z, :].bitcast(F32),
                                      ALU.subtract).then_inc(ptlo_done, 1)

            def o_low(u):
                a, b, i = units[u]
                rowsel = slice(b * DH, (b + 1) * DH)
                hi_, lo_ = ((o0_hi, o0_lo), (o1_hi, o1_lo))[a]
                dve.wait_ge(ohi_done, u + 1)
                dve.tensor_tensor(lo_[rowsel, :, i * P:(i + 1) * P],
                                  ps[rowsel, 7, :].rearrange("p (r n) -> p r n", r=PER),
                                  hi_[rowsel, :, i * P:(i + 1) * P].bitcast(F32), ALU.subtract)\
                   .then_inc(olo_done, 1)

            scores(0)
            maxima(0)
            q_scale(QJ - 1)
            denominators(0)
            q_norms(1)
            for u in range(1, AHEAD):
                scores(u)
                maxima(u)
            for u in range(NU):
                if u + 1 < NU:
                    denominators(u + 1)
                pt_low(u)
                if u >= 1:
                    o_low(u - 1)
                if u + AHEAD < NU:
                    scores(u + AHEAD)
                    maxima(u + AHEAD)
            o_low(NU - 1)

            for m in range(KT):
                dve.wait_ge(used, n_of(Q_O, m) + 1)
                dve.tensor_tensor(h[:, m, META:T], ps[:, slot_bank(O_O + m), :], h[:, m, META:T], ALU.add)\
                   .then_inc(slot_free, 1)
                if m >= 1:
                    prep(R_FFN1, m - 1, "ffn1")
            prep(R_FFN1, KT - 1, "ffn1")
            stats(R_FFN1)
            ffn(1, 0, None, None)
            ffn(1, 1, None, None)

        @block.tensor
        def _(pe):
            pe.wait_ge(consts, CONSTS)
            pe.wait_ge(x_in[0], 16)
            for k in range(KT):
                t = pe.transpose(ps[:, 0, META * k:META * (k + 1)], meta_tok[:, k * P:(k + 1) * P],
                                 ident[0:META, 0:META])
            t.then_inc(turned, 1)
            for g in range(2 * TILES):
                i, kh = g // 2, g % 2
                pe.wait_ge(x_in[1 + i], 16)
                if g >= 3:
                    pe.wait_ge(turned_out, g - 2)
                for k in range(4):
                    col = (4 * kh + k) * P
                    t = pe.transpose(ps[:, (g + 1) % 4, k * P:(k + 1) * P], x_tok[:, i, col:col + P], ident[:, :])
                t.then_inc(turned, 1)
            pe.wait_ge(par_in, 16 * 7)
            pe.transpose(ps[:, 4, 0:NROWS], par_rows[:, :], ident[0:NROWS, 0:NROWS]).then_inc(turned, 1)
            pe.wait_ge(dwr_in, 16)
            for k in range(KT):
                t = pe.transpose(ps[:, 5, 32 * k:32 * k + TAPS], dw_rows[:, k * P:(k + 1) * P],
                                 ident[0:TAPS, 0:TAPS])
            t.then_inc(turned, 1)
            pe.wait_ge(turned_out, 1 + 2 * TILES)

            def three(outs, lhs, rhs_hi, rhs_lo, first, last):
                passes = ((lhs[0], rhs_hi), (lhs[0], rhs_lo), (lhs[1], rhs_hi))
                for n, (wt, rhs) in enumerate(passes):
                    for o_, r_ in zip(outs, rhs):
                        mm = pe.matmul(o_, wt, r_, start=first and n == 0, stop=last and n == 2)
                return mm

            def chunk(c, k):
                return w_hi[:, c, k * P:(k + 1) * P], w_lo[:, c, k * P:(k + 1) * P]

            def cols(t, k, wide):
                if wide:
                    return [t[:, k, 0:HALF], t[:, k, HALF:T]]
                return [t[:, k, META:T]]

            def outs(bank, wide):
                return [ps[:, bank, 0:HALF], ps[:, bank + 1, 0:HALF]] if wide else [ps[:, bank, :]]

            def product(qd, c, o_, bank, ins, nk, k0, wide, first, last, ready=None, base=0, colf=None):
                pe.wait_ge(lo_done, n_of(qd, c) + 1)
                if first and not (isinstance(o_, int) and o_ < 2):
                    pe.wait_ge(slot_free, o_ - 1)
                colf = colf or cols
                for k in range(nk):
                    if ready is not None:
                        pe.wait_ge(ready, base + k0 + k + 1)
                    mm = three(outs(bank, wide), chunk(c, k), colf(ins[0], k0 + k, wide), colf(ins[1], k0 + k, wide),
                               first and k == 0, last and k == nk - 1)
                mm.then_inc(used, 1)

            def two_primed(qd, c, o_, ins, wide, ready, base, round_=None):
                for k in range(KT):
                    if k == STATS_AT and round_ is not None:
                        stats(round_)
                    pe.wait_ge(ready, base + k + 1)
                    for e in range(2):
                        if k == 0:
                            pe.wait_ge(lo_done, n_of(qd, c + e) + 1)
                            if o_ > 0:
                                pe.wait_ge(slot_free, o_ + e - 1)
                        mm = three(outs(2 * e, wide), chunk(c + e, k), cols(ins[0], k, wide), cols(ins[1], k, wide),
                                   k == 0, k == KT - 1)
                        if k == KT - 1:
                            mm.then_inc(used, 1)

            def spread_sum(r, src, start, stop):
                for z in range(2):
                    mm = pe.matmul(ps[:, SUM_BANK[r] + z, 0:HALF], ones[:, :], src[:, z * HALF:(z + 1) * HALF],
                                   start=start, stop=stop)
                return mm

            def stats(r):
                pe.wait_ge(acc_added, ADDED[r] + (KT - 1 if r == R_MIX0 else KT))
                if r > 0:
                    pe.wait_ge(st_step, steps_before(r))
                spread_sum(r, acc, True, True).then_inc(st_ready, 1)

            act_in = (act_hi, act_lo)

            def taps(qd, e):
                ct = (qd - Q_IN) * 2 + e
                pe.wait_ge(calo_done, ct + 1)
                pe.wait_ge(dg_done, 2 * PE_TAPS * (ct + 1))
                if not (isinstance(ct, int) and ct == 0):
                    pe.wait_ge(conv_mix, ct)
                e = e % 2
                last = isinstance(ct, int) and ct == KT - 1
                where = [(e, w, PE0 + w) for w in range(PE_TAPS)]
                if last:
                    where += [(0, w, LAST0 + w) for w in range(LAST_TAPS)]
                for n, (z_, w, at_) in enumerate(where):
                    if n == PE_TAPS:
                        pe.wait_ge(dg_done, 2 * PE_TAPS * KT + 2 * LAST_TAPS)
                    rng = lambda t: [t[:, e, at_ + HALF * z:at_ + HALF * (z + 1)] for z in range(2)]
                    mm = three(outs(4, True), (dg_hi[:, z_, w, :], dg_lo[:, z_, w, :]), rng(a_hi), rng(a_lo),
                               n == 0, n == len(where) - 1)
                mm.then_inc(taps_pe, 1)

            def conv_in(qd, first):
                if first:
                    two_primed(qd, 0, O_IN, act_in, True, alo_done, 0, R_MIX0)
                    pe.wait_ge(st_step, 1)
                    product(qd, 2, O_IN, 6, act_in, KT, 0, True, True, True)
                    taps(qd, 0)
                    product(qd, 3, O_IN + 3, 2, act_in, KT, 0, True, True, True)
                else:
                    for e in range(2):
                        ct = (qd - Q_IN) * 2 + e
                        product(qd, 2 * e, O_IN + 2 * ct, 0, act_in, KT, 0, True, True, True)
                        taps(qd, e - 1)
                        product(qd, 2 * e + 1, O_IN + 2 * ct + 1, 2, act_in, KT, 0, True, True, True)
            quad_loop(pe, Q_IN, 4, conv_in)
            taps(Q_IN + 3, 1)

            pe.wait_ge(acc_added, ADDED[R_MEAN] + 7)
            pe.wait_ge(st_step, steps_before(R_MEAN))
            spread_sum(R_MEAN, acc, True, False)
            pe.wait_ge(c_sum, KT)
            spread_sum(R_MEAN, cp[:, (KT - 1) % 2, :], False, True).then_inc(st_ready, 1)
            for k in range(KT):
                if k in (3, 5, 7):
                    continue
                if k < 2:
                    pe.wait_ge(sq_done, 8 * SQ0[R_VAR] + k + 1)
                else:
                    pe.wait_ge(var_paired, k // 2)
                mm = spread_sum(R_VAR, sq_many[k], k == 0, k == 6)
            mm.then_inc(st_ready, 1)

            two_primed(Q_CO, 0, O_CO, (ln_hi, ln_lo), True, lnlo_done, 0)
            for m in range(2, KT):
                product(Q_CO + m // 4, m % 4, O_CO + m, slot_bank(O_CO + m), (ln_hi, ln_lo), KT, 0, True, True, True)

            def ffn(L, s, round_):
                wide = L == 0

                def gu(qd, first):
                    if first and s == 0:
                        o_ = O_GU[L][s]
                        two_primed(qd, 0, o_, act_in, wide, alo_done, 8 * PREP[round_], round_)
                        product(qd, 2, 0, 4, act_in, KT, 0, wide, True, True)
                        product(qd, 3, o_ + 3, 2, act_in, KT, 0, wide, True, True)
                        return
                    for c in range(SLOTS):
                        product(qd, c, O_GU[L][s] + (qd - Q_GU[L][s]) * SLOTS + c, 2 * (c % 2), act_in, KT, 0, wide,
                                True, True)
                quad_loop(pe, Q_GU[L][s], FH[s] // 2, gu)
                hid_cols = lambda t, k, w_: [t[:, k, 0:HALF], t[:, k, HALF:T]] if w_ else [t[:, k, 0:SEQ]]

                def turn(qd, e):
                    m = (qd - Q_DN[L][s]) * 2 + e
                    pe.wait_ge(slot_free, O_DN[L][s] + m + 1)
                    e = e % 2
                    if not (isinstance(m, int) and m < 2):
                        pe.wait_ge(out_sb, m - 1)
                    for i in range(TILES):
                        t = pe.transpose(ps[:, 4 + e, i * P:(i + 1) * P], tmp[:, e, i * P:(i + 1) * P], ident[:, :])
                    t.then_inc(outT_ready, 1)

                def dn(qd, first):
                    for e in range(2):
                        m = (qd - Q_DN[L][s]) * 2 + e
                        for part in range(2):
                            product(qd, 2 * e + part, O_DN[L][s] + m, 2 * e, (hid_hi, hid_lo), PARTS[s],
                                    part * PARTS[s], wide, part == 0, part == 1,
                                    hidlo_done if first and e == 0 else None, G0[L][s], hid_cols)
                        if L == 1 and s == 1 and not (first and e == 0):
                            turn(qd, e - 1)
                quad_loop(pe, Q_DN[L][s], KT // 2, dn)
                if L == 1 and s == 1:
                    turn(Q_DN[L][s] + KT // 2 - 1, 1)

            ffn(0, 0, R_FFN0)
            ffn(0, 1, R_FFN0)

            def q_product(j):
                qd, c = (Q_Q0, Q_Q1)[j // PER], j % PER
                pe.wait_ge(lo_done, n_of(qd, c) + 1)
                if j >= PER:
                    pe.wait_ge(q_out, j - PER + 1)
                elif j >= 2:
                    pe.wait_ge(slot_free, O_O)
                if j == QJ - 1:
                    pe.wait_ge(kt_done, PAIRS * (TILES + 2))
                for k in range(KT):
                    mm = three([ps[:, Q_BANKS[j], :]], chunk(c, k), cols(act_hi, k, False), cols(act_lo, k, False),
                               k == 0, k == KT - 1)
                mm.then_inc(used, 1)

            def q_sums(j):
                if j == 0:
                    pe.wait_ge(st_step, steps_before(R_MIX1) + 1)
                if j == PER:
                    pe.wait_ge(rq_step, 1)
                pe.wait_ge(qsq_done, j + 1)
                for i in range(TILES):
                    at_ = ((j % PER) * TILES + i) * 2
                    mm = pe.matmul(ps[:, 7, at_:at_ + 2], sq[:, j % 2, i * P:(i + 1) * P], blk2[:, :],
                                   start=True, stop=True)
                mm.then_inc(qss_ready, 1)

            def kv_chunk(t, c):
                if c == 0:
                    pe.wait_ge(kvalo_done, t + 1)
                    if t >= 3:
                        pe.wait_ge(kx_done, t - 2)
                if t == 0:
                    pe.wait_ge(lo_done, n_of(Q_KV, c) + 1)
                for kk in range(2):
                    k = 2 * c + kk
                    wh, wl = (w_[:, c, kk * 512:(kk + 1) * 512] for w_ in (w_hi, w_lo))
                    xh, xl = kva_hi[:, t % 3, k, :], kva_lo[:, t % 3, k, :]
                    for n, (l_, r_) in enumerate(((xh, wh), (xh, wl), (xl, wh))):
                        mm = pe.matmul(ps[:, 4 + t % 3, :], l_, r_, start=k == 0 and n == 0,
                                       stop=k == KT - 1 and n == 2)
                if t == TILES:
                    mm.then_inc(used, 1)
                elif c == SLOTS - 1:
                    mm.then_inc(kv_ready, 1)

            def turn_keys():
                pe.wait_ge(k_step, 9)
                for a in range(PAIRS):
                    for i in range(TILES):
                        pe.transpose(ps[:, 4 + a, i * P:(i + 1) * P], kx[:, 1 + i, a * P:(a + 1) * P], ident[:, :])
                for a in range(PAIRS):
                    t = pe.transpose(ps[:, 6, a * P:(a + 1) * P], kx[:, 0, a * P:(a + 1) * P], ident[:, :])
                t.then_inc(kt_ready, 1)

            for k in range(KT):
                if k == STATS_AT:
                    stats(R_MIX1)
                pe.wait_ge(alo_done, 8 * PREP[R_MIX1] + k + 1)
                for j in range(2):
                    if k == 0:
                        pe.wait_ge(lo_done, n_of(Q_Q0, j) + 1)
                        pe.wait_ge(slot_free, O_O - 1)
                    mm = three([ps[:, j, :]], chunk(j, k), cols(act_hi, k, False), cols(act_lo, k, False), k == 0,
                               k == KT - 1)
                    if k == KT - 1:
                        mm.then_inc(used, 1)
            q_product(2)
            q_product(3)
            pe.wait_ge(st_step, steps_before(R_MIX1) + STEPS[R_MIX1])
            for t in range(1 + TILES):
                at_ = 0 if t == 0 else META + (t - 1) * P
                mm = pe.matmul(ps[:, 7, P + t:P + t + 1], rb[:, at_:at_ + P], ident[:, 0:1], start=True, stop=True)
            mm.then_inc(tok_ready, 1)
            for c in range(SLOTS):
                kv_chunk(0, c)
            q_sums(0)
            q_sums(1)
            for c in range(SLOTS):
                kv_chunk(1, c)
            q_sums(2)
            q_sums(3)
            for c in range(SLOTS):
                kv_chunk(2, c)
            for c in range(SLOTS):
                kv_chunk(3, c)
                kv_chunk(4, c)
            q_product(PER)
            q_product(PER + 1)
            turn_keys()
            q_product(PER + 2)
            q_sums(PER)
            q_sums(PER + 1)

            def scores(u):
                a, b, i = units[u]
                half = slice(b * DH, (b + 1) * DH)
                if u == 0:
                    pe.wait_ge(kt_done, PAIRS * (TILES + 2))
                    pe.wait_ge(q_out, QJ - 1)
                n, at_ = keys_of(i), WINDOW_AT[i]
                for r in range(PER):
                    s_ = PER * u + r
                    if u >= 1:
                        pe.wait_ge(s_read, s_ - PER + 1)
                    pe.matmul(ps[:, S_BANKS[r], 0:n], q_of(a)[half, r, i * P:(i + 1) * P],
                              kt[half, a, at_:at_ + n], start=True, stop=True).then_inc(s_ready, 1)

            def turn_p(u):
                a, b, i = units[u]
                before_, this_, meta_ = ORDER[i]
                pe.wait_ge(p_norm, u + 1)
                if u == 0:
                    pe.wait_ge(q_out, QJ)
                if u >= 1:
                    pe.wait_ge(ptlo_done, blocks_before[u])
                    pe.wait_ge(ptm_done, u)
                for bank, at_, n in ((5, this_, P), (4, before_, P), (6, meta_, META)):
                    if at_ is None:
                        continue
                    for r in range(PER):
                        t = pe.transpose(ps[0:n, bank, r * P:(r + 1) * P], s_sb[:, u % BUFS, r, at_:at_ + n],
                                         ident[:, :])
                t.then_inc(pt_ready, 1)

            def values(u):
                a, b, i = units[u]
                pair = slice(a * P, (a + 1) * P)
                pe.wait_ge(ptm_done, u + 1)
                pe.wait_ge(ptlo_done, blocks_before[u + 1])
                if u >= 1:
                    pe.wait_ge(olo_done, u)
                else:
                    pe.wait_ge(rq_step, 8)
                for n, (z, t) in enumerate([(1, i + 1), (0, i)][:1 if i == 0 else 2]):
                    three([ps[:, 7, :]], [v_[:, t, pair] for v_ in (v_hi, v_lo)], [pt_hi[:, u % 2, z, :]],
                          [pt_lo[:, u % 2, z, :]], n == 0, False)
                pe.matmul(ps[:, 7, :], v_meta[0:META, pair], sq[0:META, u % 2, 0:PER * P], start=False, stop=True)\
                  .then_inc(pv_ready, 1)

            def o_cols(t, k, wide):
                src = (o0_hi, o1_hi) if t is o0_hi else (o0_lo, o1_lo)
                return [src[k // PER][:, k % PER, :]]

            def o_part(m, k):
                return three(outs(slot_bank(O_O + m), False), chunk(m, k), o_cols(o0_hi, k, False),
                             o_cols(o0_lo, k, False), k == 0, k == KT - 1)

            def o_first(m):
                if m == 0:
                    pe.wait_ge(s_read, PER * NU)
                    pe.wait_ge(olo_done, NU // 2)
                pe.wait_ge(lo_done, n_of(Q_O, m) + 1)
                for k in range(PER):
                    o_part(m, k)

            def o_second(m):
                if m == 0:
                    pe.wait_ge(olo_done, NU)
                for k in range(PER, KT):
                    mm = o_part(m, k)
                mm.then_inc(used, 1)

            scores(0)
            q_product(QJ - 1)
            q_sums(QJ - 2)
            q_sums(QJ - 1)
            for u in range(1, AHEAD):
                scores(u)
            for u in range(NU):
                turn_p(u)
                if u >= 1:
                    values(u - 1)
                if u >= NU - 2:
                    o_first(u - (NU - 2))
                if u + AHEAD < NU:
                    scores(u + AHEAD)
            values(NU - 1)

            for m in range(2):
                o_second(m)
            for m in range(2, KT):
                product(Q_O + m // 4, m % 4, O_O + m, slot_bank(O_O + m), (o0_hi, o0_lo), KT, 0, False, True, True,
                        None, 0, o_cols)

            ffn(1, 0, R_FFN1)
            ffn(1, 1, R_FFN1)


_INS = ["x", "meta_tokens", "norm_mix", "norm_ffn", "conv_w_in", "conv_b_in", "conv_dw", "conv_ln_g", "conv_ln_b",
        "conv_w_out", "conv_b_out", "kv_norm", "w_kv", "k_norm", "w_q", "q_norm", "attn_sinks", "w_o",
        "ffn_w_gate", "ffn_w_up", "ffn_w_down"]


def kernel(**inputs):
    import numpy as np
    import concourse.bacc as bacc
    from concourse.bass_utils import run_bass_kernel_spmd

    nc = bacc.Bacc("TRN2", target_bir_lowering=False, num_devices=1)
    arrays, args = {}, []
    for name in _INS:
        a = np.ascontiguousarray(inputs[name])
        arrays[f"in_{name}"] = a
        args.append(nc.dram_tensor(f"in_{name}", a.shape, mybir.dt.from_np(a.dtype), kind="ExternalInput").ap())
    res = nc.dram_tensor("out_dram", arrays["in_x"].shape, F32, kind="ExternalOutput").ap()
    trunk_kernel(nc, *args, res)
    r = run_bass_kernel_spmd(nc, [arrays], core_ids=[0])
    return r.results[0]["out_dram"]
```
